# Optimizing a Trainium2 kernel written in Bass

```python
import jax, jax.numpy as jnp
from jax import lax
import numpy as np

D_MODEL = 1024
BATCH = 1
SEQ = 128
DEPTH = 2
DEC_BATCH = 1
DEC_SEQ = 256
PAST_LEN = 128

GRID_W = 64
N_HEADS = 8
N_KV_HEADS = 2
HEAD_DIM = 64
ATTN_W = N_HEADS * HEAD_DIM
KV_W = N_KV_HEADS * HEAD_DIM
POOL_WINDOWS = (2, 4, 8, 16)
POOL_GROUPS = len(POOL_WINDOWS)
POOL_GROUP_W = 128
POOL_W = POOL_GROUPS * POOL_GROUP_W
A_IN_W = ATTN_W + 2 * KV_W + POOL_W
MIX_W = ATTN_W + POOL_W
CONV_W = D_MODEL
CONV_K = 3
PEER_HEADS = 8
PEER_NKEYS = 128
PEER_EXPERTS = PEER_NKEYS * PEER_NKEYS
PEER_TOPK = 16
PEER_DK = 128
PEER_BLOCK = 128
Q_BLOCK = 128
ROPE_THETA = 10000.0
N_ATTN_LAYERS = (DEPTH + 1) // 2
N_CONV_LAYERS = DEPTH // 2
EPS = 1e-6

kernel_name = "hybrid_diffusion_attn_pool_conv_peer_step"

def rms_norm(x, g):
    xf = x.astype(jnp.float32)
    y = xf * lax.rsqrt(jnp.mean(xf * xf, axis=-1, keepdims=True) + EPS)
    return (y * g.astype(jnp.float32)).astype(x.dtype)

def modulate(x, shift, scale):
    return x * (1 + scale) + shift

def axial_rope(x):
    T = x.shape[1]
    rows_n = T // GRID_W
    row = jnp.repeat(jnp.arange(rows_n), GRID_W)
    col = jnp.tile(jnp.arange(GRID_W), rows_n)
    half = HEAD_DIM // 2
    nf = half // 2
    inv = ROPE_THETA ** (-jnp.arange(nf, dtype=jnp.float32) / nf)

    def rot(seg, pos):
        ang = pos.astype(jnp.float32)[:, None] * inv[None, :]
        cos = jnp.cos(ang)[None, :, None, :].astype(seg.dtype)
        sin = jnp.sin(ang)[None, :, None, :].astype(seg.dtype)
        s1, s2 = seg[..., :nf], seg[..., nf:]
        return jnp.concatenate([s1 * cos - s2 * sin, s2 * cos + s1 * sin], axis=-1)

    return jnp.concatenate([rot(x[..., :half], row), rot(x[..., half:], col)], axis=-1)

def block_attention(q, k, v):
    B, T, H, Dh = q.shape
    G = H // N_KV_HEADS
    nb = T // Q_BLOCK
    qb = q.reshape(B, nb, Q_BLOCK, N_KV_HEADS, G, Dh).transpose(1, 0, 2, 3, 4, 5)
    scale = HEAD_DIM ** -0.5

    def one(qblk):
        s = jnp.einsum("bqkgd,bskd->bkgqs", qblk, k).astype(jnp.float32) * scale
        p = jax.nn.softmax(s, axis=-1).astype(v.dtype)
        return jnp.einsum("bkgqs,bskd->bqkgd", p, v)

    o = lax.map(one, qb)
    return o.transpose(1, 0, 2, 3, 4, 5).reshape(B, T, H * Dh)

def pool_mixer(p, w, scale):
    B, T, _ = p.shape
    pg = p.reshape(B, T, POOL_GROUPS, POOL_GROUP_W)
    cs = jnp.pad(jnp.cumsum(pg.astype(jnp.float32), axis=1), ((0, 0), (1, 0), (0, 0), (0, 0)))
    t = jnp.arange(T)
    means = []
    for g, win in enumerate(POOL_WINDOWS):
        lo = jnp.clip(t - win // 2, 0, T)
        hi = jnp.clip(t + win - win // 2, 0, T)
        tot = cs[:, hi, g] - cs[:, lo, g]
        cnt = (hi - lo).astype(jnp.float32)[None, :, None]
        means.append(tot / cnt)
    mean = jnp.stack(means, axis=2).astype(p.dtype)
    y = jnp.einsum("btgc,gcd->btgd", mean - pg, w)
    return y.reshape(B, T, POOL_W) * scale

def attn_pool_mixer(h, w_in, w_out, q_g, k_g, pool_w, pool_s, ctx_k=None, ctx_v=None):
    B, T, _ = h.shape
    z = h @ w_in
    q = z[..., :ATTN_W].reshape(B, T, N_HEADS, HEAD_DIM)
    k = z[..., ATTN_W:ATTN_W + KV_W].reshape(B, T, N_KV_HEADS, HEAD_DIM)
    v = z[..., ATTN_W + KV_W:ATTN_W + 2 * KV_W].reshape(B, T, N_KV_HEADS, HEAD_DIM)
    p = z[..., ATTN_W + 2 * KV_W:]
    q = rms_norm(q, q_g)
    k = rms_norm(k, k_g)
    if ctx_k is None:
        a = block_attention(q, k, v)
    else:
        keys = jnp.concatenate([axial_rope(k), ctx_k.astype(k.dtype)], axis=1)
        vals = jnp.concatenate([v, ctx_v.astype(v.dtype)], axis=1)
        a = block_attention(axial_rope(q), keys, vals)
    out = jnp.concatenate([a, pool_mixer(p, pool_w, pool_s)], axis=-1) @ w_out
    return out, k, v

def conv_mixer(h, w_in, conv_w, w_out):
    gb, gc, hh = jnp.split(h @ w_in, 3, axis=-1)
    u = gc * hh
    T = u.shape[1]
    pad = CONV_K // 2
    up = jnp.pad(u, ((0, 0), (pad, CONV_K - 1 - pad), (0, 0)))
    y = up[:, 0:T] * conv_w[0]
    for j in range(1, CONV_K):
        y = y + up[:, j:j + T] * conv_w[j]
    return (gb * y) @ w_out

def peer(h, wq, subkeys, U, V):
    B, T, D = h.shape
    hb = h.reshape(-1, PEER_BLOCK, D)

    def one(xb):
        q = (xb @ wq).reshape(PEER_BLOCK, PEER_HEADS, 2, PEER_DK)
        s = jnp.einsum("nhpk,pek->nhpe", q, subkeys)
        sv, si = lax.top_k(s, PEER_TOPK)
        cand = (sv[:, :, 0, :, None] + sv[:, :, 1, None, :]).reshape(PEER_BLOCK, PEER_HEADS, PEER_TOPK * PEER_TOPK)
        fv, fi = lax.top_k(cand, PEER_TOPK)
        i1 = jnp.take_along_axis(si[:, :, 0], fi // PEER_TOPK, axis=-1)
        i2 = jnp.take_along_axis(si[:, :, 1], fi % PEER_TOPK, axis=-1)
        idx = i1 * PEER_NKEYS + i2
        g = jax.nn.softmax(fv.astype(jnp.float32), axis=-1).astype(xb.dtype)
        act = jax.nn.gelu(jnp.einsum("nhed,nd->nhe", U[idx], xb), approximate=False)
        return jnp.einsum("nhe,nhed->nd", g * act, V[idx])

    return lax.map(one, hb).reshape(B, T, D)

def setup_inputs(seed: int = 0) -> dict:
    key = jax.random.key(seed)
    ks = jax.random.split(key, 24)

    def nrm(k, shape, s):
        return jax.random.normal(k, shape, jnp.float32) * s

    D = D_MODEL
    return {
        "x_prompt": nrm(ks[0], (BATCH, SEQ, D), 1.0),
        "x_sample": nrm(ks[1], (DEC_BATCH, DEC_SEQ, D), 1.0),
        "cache_k": nrm(ks[2], (DEC_BATCH, N_ATTN_LAYERS, PAST_LEN, N_KV_HEADS, HEAD_DIM), 1.0),
        "cache_v": nrm(ks[3], (DEC_BATCH, N_ATTN_LAYERS, PAST_LEN, N_KV_HEADS, HEAD_DIM), 1.0),
        "c": nrm(ks[4], (DEC_BATCH, D), 1.0),
        "c_ctx": nrm(ks[5], (D,), 1.0),
        "mod_w": nrm(ks[6], (DEPTH, D, 6 * D), 0.5 * D ** -0.5),
        "mod_b": nrm(ks[7], (DEPTH, 6 * D), 0.02),
        "norm1_g": 1.0 + nrm(ks[8], (DEPTH, D), 0.02),
        "norm2_g": 1.0 + nrm(ks[9], (DEPTH, D), 0.02),
        "a_in_w": nrm(ks[10], (N_ATTN_LAYERS, D, A_IN_W), D ** -0.5),
        "a_out_w": nrm(ks[11], (N_ATTN_LAYERS, MIX_W, D), MIX_W ** -0.5),
        "q_norm_g": 1.0 + nrm(ks[12], (N_ATTN_LAYERS, HEAD_DIM), 0.02),
        "k_norm_g": 1.0 + nrm(ks[13], (N_ATTN_LAYERS, HEAD_DIM), 0.02),
        "pool_w": nrm(ks[14], (N_ATTN_LAYERS, POOL_GROUPS, POOL_GROUP_W, POOL_GROUP_W), POOL_GROUP_W ** -0.5),
        "pool_scale": 0.5 + nrm(ks[15], (N_ATTN_LAYERS, POOL_W), 0.1),
        "c_in_w": nrm(ks[16], (N_CONV_LAYERS, D, 3 * CONV_W), D ** -0.5),
        "c_conv_w": nrm(ks[17], (N_CONV_LAYERS, CONV_K, CONV_W), CONV_K ** -0.5),
        "c_out_w": nrm(ks[18], (N_CONV_LAYERS, CONV_W, D), CONV_W ** -0.5),
        "peer_wq": nrm(ks[19], (DEPTH, D, PEER_HEADS * 2 * PEER_DK), D ** -0.5),
        "peer_subkeys": nrm(ks[20], (DEPTH, 2, PEER_NKEYS, PEER_DK), PEER_DK ** -0.5),
        "peer_u": nrm(ks[21], (DEPTH, PEER_EXPERTS, D), D ** -0.5),
        "peer_v": nrm(ks[22], (DEPTH, PEER_EXPERTS, D), 0.5),
        "final_g": 1.0 + nrm(ks[23], (D,), 0.02),
    }

def reference(x_prompt, x_sample, cache_k, cache_v, c, c_ctx, mod_w, mod_b, norm1_g, norm2_g,
              a_in_w, a_out_w, q_norm_g, k_norm_g, pool_w, pool_scale, c_in_w, c_conv_w, c_out_w,
              peer_wq, peer_subkeys, peer_u, peer_v, final_g):
    xp, xs = x_prompt, x_sample
    new_k, new_v = [], []
    for l in range(DEPTH):
        mp = jnp.split(jax.nn.silu(c_ctx) @ mod_w[l] + mod_b[l], 6, axis=-1)
        ms = [m[:, None, :] for m in jnp.split(jax.nn.silu(c) @ mod_w[l] + mod_b[l], 6, axis=-1)]
        hp = modulate(rms_norm(xp, norm1_g[l]), mp[0], mp[1])
        hs = modulate(rms_norm(xs, norm1_g[l]), ms[0], ms[1])
        if l % 2 == 0:
            i = l // 2
            yp, kp, vp = attn_pool_mixer(hp, a_in_w[i], a_out_w[i], q_norm_g[i], k_norm_g[i], pool_w[i], pool_scale[i])
            ys, _, _ = attn_pool_mixer(hs, a_in_w[i], a_out_w[i], q_norm_g[i], k_norm_g[i], pool_w[i], pool_scale[i],
                                       ctx_k=cache_k[:, i], ctx_v=cache_v[:, i])
            new_k.append(kp)
            new_v.append(vp)
        else:
            j = l // 2
            yp = conv_mixer(hp, c_in_w[j], c_conv_w[j], c_out_w[j])
            ys = conv_mixer(hs, c_in_w[j], c_conv_w[j], c_out_w[j])
        xp = xp + mp[2] * yp
        xs = xs + ms[2] * ys
        hp = modulate(rms_norm(xp, norm2_g[l]), mp[3], mp[4])
        hs = modulate(rms_norm(xs, norm2_g[l]), ms[3], ms[4])
        xp = xp + mp[5] * peer(hp, peer_wq[l], peer_subkeys[l], peer_u[l], peer_v[l])
        xs = xs + ms[5] * peer(hs, peer_wq[l], peer_subkeys[l], peer_u[l], peer_v[l])
    y_prompt = rms_norm(xp, final_g)
    y_sample = rms_norm(xs, final_g)
    new_cache_k = jnp.stack(new_k, axis=1)
    new_cache_v = jnp.stack(new_v, axis=1)
    return (y_prompt, y_sample, new_cache_k, new_cache_v)


_drawn_inputs = setup_inputs


def setup_inputs(seed=0):
    import zlib

    import numpy as np

    out = dict(_drawn_inputs(seed))
    spreads = {}
    factors = {'cache_k': 3.857,
     'cache_v': 3.38,
     'norm1_g': 2.959,
     'norm2_g': 3.024,
     'q_norm_g': 8.0,
     'k_norm_g': 2.819,
     'final_g': 2.918}
    for name, (base, spread) in spreads.items():
        noise = np.random.default_rng([zlib.crc32(name.encode()), seed]).standard_normal(out[name].shape)
        drawn = base * np.exp(spread * noise) if base else spread * noise
        out[name] = __import__('jax').numpy.asarray(drawn.astype(out[name].dtype))
    for name, factor in factors.items():
        out[name] = (out[name] * factor).astype(out[name].dtype)
    return out
```

```python
import concourse.bass as bass
from concourse import mybir
from contextlib import ExitStack, contextmanager

F32 = mybir.dt.float32
F32R = mybir.dt.float32r
BF16 = mybir.dt.bfloat16
U32 = mybir.dt.uint32
ALU = mybir.AluOpType
ACT = mybir.ActivationFunctionType
AX = mybir.AxisListType

P = 128
D = 1024
KC = D // P
NPROMPT, NSAMPLE = 128, 256
T = NPROMPT + NSAMPLE
TT = T // P
SEGS = ((0, NPROMPT, 0), (NPROMPT, NSAMPLE, 1))
LAYERS = 2
EPS = 1e-6
HEADS, TOPK, NK = 8, 16, 128
PICKS = HEADS * TOPK
NEG = -3.0e38
WINDOWS = (2, 4, 8, 16)

R_N1, R_N2, R_FIN, R_QG, R_KG, R_PS, R_CW, R_CTX, R_C = 0, 16, 32, 40, 41, 42, 46, 70, 78
VROWS = 86

STAGES = (("q", 4, 2), ("kvp", 6, 1), ("a_out", 8, 3), ("wq0", 16, 1), ("v0", 128, 1),
          ("c_in", 24, 1), ("c_out", 8, 1), ("wq1", 16, 1), ("v1", 128, 1))
UNIT0, FILLED0, PROJ0, DMAS = {}, {}, {}, {}
_u = _f = _p = 0
for _name, _n, _d in STAGES:
    UNIT0[_name], FILLED0[_name], PROJ0[_name], DMAS[_name] = _u, _f, _p, 16 * _d
    _u += _n
    _f += 16 * _d * _n // 2
    _p += 0 if _name in ("v0", "v1") else _n
NEXT = {a[0]: b[0] for a, b in zip(STAGES, STAGES[1:])}
COUNT = {s[0]: s[1] for s in STAGES}

MODB = 256
MODPAIRS = 6 * D // MODB // 2


class Steps:

    def __init__(self, eng, sem):
        self.eng, self.sem, self.n, self.extra = eng, sem, 0, 0

    def mark(self, ins):
        ins.then_inc(self.sem, 1)
        self.n += 1

    def wait(self):
        self.eng.wait_ge(self.sem, self.extra + self.n)

    def do(self, ins):
        self.mark(ins)
        self.wait()

    @contextmanager
    def loop(self, turns, per):
        n0 = self.n
        with self.eng.Fori(0, turns) as i:
            self.extra = i * per
            yield i
            self.extra = 0
        assert self.n - n0 == per, (self.n - n0, per)
        self.n = n0 + turns * per


class Marks:

    def __init__(self, sem, names):
        self.sem, self.names, self.at = sem, names, 0

    def mark(self, name, ins):
        assert self.names[self.at] == name, (self.names[self.at], name)
        self.at += 1
        ins.then_inc(self.sem, 1)

    def wait(self, eng, name):
        eng.wait_ge(self.sem, self.names.index(name) + 1)


def build_step(nc, x_prompt, x_sample, cache_k, cache_v, c, c_ctx, mod_w, mod_b, norm1_g, norm2_g,
               a_in_w, a_out_w, q_norm_g, k_norm_g, pool_w, pool_scale, c_in_w, c_conv_w, c_out_w,
               peer_wq, peer_subkeys, peer_u, peer_v, final_g,
               k_ident, k_headmean, k_rot, k_cos, k_sin, k_rcnt, k_iota,
               y_prompt, y_sample, new_k, new_v):
    ctx = ExitStack()
    with ctx:
        def sb(name, shape, dt=F32):
            return ctx.enter_context(nc.sbuf_tensor(name, shape, dt))

        def sem(name):
            return ctx.enter_context(nc.semaphore(name))

        xT = sb("xT", [P, KC, T])
        HH = sb("HH", [P, KC, T], F32R)
        HL = sb("HL", [P, KC, T], F32R)
        RAW = sb("RAW", [P, 2, D])
        WHI = [sb(f"WHI{i}", [P, D], F32R) for i in range(2)]
        WLO = [sb(f"WLO{i}", [P, D], F32R) for i in range(2)]
        URAW = sb("URAW", [P, 2, D])
        UHI = [sb(f"UHI{i}", [P, D], F32R) for i in range(2)]
        ULO = [sb(f"ULO{i}", [P, D], F32R) for i in range(2)]
        GIN = sb("GIN", [P, 2, T])
        GEL = sb("GEL", [P, 2, T])
        EHI = [sb(f"EHI{i}", [P, T], F32R) for i in range(2)]
        ELO = [sb(f"ELO{i}", [P, T], F32R) for i in range(2)]
        VR = sb("VR", [P, P])
        MBR = sb("MBR", [P, P])
        VT = sb("VT", [P, VROWS])
        MBT = sb("MBT", [P, LAYERS * 48])
        COND = sb("COND", [P, KC, 2])
        MODR = sb("MODR", [P, 2, KC, MODB])
        MROW = sb("MROW", [2, 2, MODB])
        MODT = sb("MODT", [P, LAYERS, 48, 2])
        GS = sb("GS", [P, LAYERS, 2, KC, 2])
        IDENT = sb("IDENT", [P, P])
        MEAN1 = sb("MEAN1", [P, P])
        HMEAN = sb("HMEAN", [P, P])
        ROT = sb("ROT", [P, P])
        IOTA = sb("IOTA", [P, P])
        IOTAB = sb("IOTAB", [P, P], BF16)
        SKR = sb("SKR", [P, 4, P])
        SKT = sb("SKT", [P, 4, P])
        I16U = sb("I16U", [P, 16, TOPK], U32)
        FIU = sb("FIU", [P, HEADS, TOPK], U32)
        FAU = sb("FAU", [P, PICKS], U32)
        FBU = sb("FBU", [P, PICKS], U32)
        IT1 = sb("IT1", [P, T])
        IT2 = sb("IT2", [P, T])
        GP = sb("GP", [P, 3, T])
        GB = sb("GB", [P, P], BF16)
        OH2 = sb("OH2", [P, 8, P], BF16)
        OH1 = sb("OH1", [P, 8, 3, P], BF16)
        AR = sb("AR", [P, P * P])

        def ar(at, *dims):
            n = 1
            for d in dims:
                n *= d
            v = AR[:, at:at + n]
            if len(dims) == 2:
                v = v.rearrange("p (a b) -> p a b", a=dims[0])
            if len(dims) == 3:
                v = v.rearrange("p (a b c) -> p a b c", a=dims[0], b=dims[1])
            return v

        XS = ar(0, TT, D)
        Z = ar(0, 10, T)
        QN = ar(3840, 5, T)
        ZS = ar(5760, 5, T)
        VAR = ar(7680, 5, T)
        RQ = ar(9600, 4, NSAMPLE)
        COS, SIN = ar(10880, NSAMPLE), ar(11136, NSAMPLE)
        RCNT = ar(11392, 4, T)
        KALL = ar(12928, T)
        VTOK = ar(13312, 3, P)
        VPAST = ar(13696, P)
        KTOK = ar(13824, P)
        KPAST = ar(13952, P)
        PADW = 432
        XPAD, SUM0, SUM1 = ar(14080, PADW), ar(14512, PADW), ar(14944, PADW)
        MX, NB, SM, RV = ar(15376, 4), ar(15380, 4), ar(15384, 4), ar(15388, 4)
        PW = ar(15392, 4, P)
        PROB = [ar(5760, 4, T), ar(7680, 4, T)]
        PROBT = ar(0, 4, T)
        NB0 = 13312
        SQ = ar(NB0, 2, T)
        MV, RC, RT, NT = (ar(NB0 + (2 + i) * T, T) for i in range(4))
        T1 = ar(NB0 + 6 * T, 2, T)
        QT = ar(0, 16, T)
        SC = ar(6144, 16, NK)
        SC2 = ar(8192, 16, NK)
        V16 = ar(10240, 16, TOPK)
        I16F = ar(10496, 16, TOPK)
        CA = ar(10752, HEADS, 256)
        CA2 = ar(12800, HEADS, 256)
        V2 = ar(14848, HEADS, TOPK)
        FA, FB = ar(14976, PICKS), ar(15104, PICKS)
        ID1, ID2 = ar(15232, PICKS), ar(15360, PICKS)
        EX = ar(15488, HEADS, TOPK)
        GT = ar(15616, HEADS, TOPK)
        ZSUM, ZINV = ar(15744, HEADS), ar(15752, HEADS)
        GRES = ar(15760, P)
        EQ = ar(8192, PICKS, TOPK)
        EQ2 = ar(12800, PICKS, TOPK)
        STAGE = ar(0, P, P)
        CM = ar(0, KC, T)
        GC = ar(3072, T)
        UP = ar(3456, 388)
        YA = ar(3844, 386)
        YT = ar(3072, KC, T)
        YTOK = ar(6144, TT, D)

        PS = ctx.enter_context(nc.psum_tensor("PS", [P, 8, 512], F32))
        GD = nc.dram_tensor("gates_dram", [LAYERS, P, P, T], F32, kind="Internal").ap()

        s_vec, s_cst, s_x = sem("s_vec"), sem("s_cst"), sem("s_x")
        s_att = sem("s_att")
        s_init = sem("s_init")
        s_vt = sem("s_vt")
        s_act0 = sem("s_act0")
        s_xt, s_xe = sem("s_xt"), sem("s_xe")
        mod_in = [sem(f"mod_in{i}") for i in range(2)]
        s_mrow = sem("s_mrow")
        s_mev = sem("s_mev")
        s_mtr = sem("s_mtr")
        s_mod = sem("s_mod")
        s_gs = sem("s_gs")
        s_sq, s_ss = sem("s_sq"), sem("s_ss")
        s_rc, s_rt = sem("s_rc"), sem("s_rt")
        s_t1 = sem("s_t1")
        s_hhi, s_hlo = sem("s_hhi"), sem("s_hlo")
        raw_in = [sem(f"raw_in{i}") for i in range(2)]
        s_hi = sem("s_hi")
        s_lo = sem("s_lo")
        s_unit = sem("s_unit")
        s_ev = sem("s_ev")
        s_res = sem("s_res")
        s_pool = sem("s_pool")
        s_pm = sem("s_pm")
        s_dve, s_acts = sem("s_dve"), sem("s_acts")
        s_nkv = sem("s_nkv")
        s_sc, s_scc = sem("s_sc"), sem("s_scc")
        s_l1 = sem("s_l1")
        s_d, s_e = sem("s_d"), sem("s_e")
        s_pick = sem("s_pick")
        s_ptr, s_pte = sem("s_ptr"), sem("s_pte")
        s_pts = sem("s_pts")
        s_oh = sem("s_oh")
        s_gm = sem("s_gm")
        s_gev = sem("s_gev")
        s_gst = sem("s_gst")
        u_in = [sem(f"u_in{i}") for i in range(2)]
        g_in = [sem(f"g_in{i}") for i in range(2)]
        s_tr = sem("s_tr")
        s_uhi = sem("s_uhi")
        s_ulo = sem("s_ulo")
        s_S = sem("s_S")
        s_gel = sem("s_gel")
        s_w = sem("s_w")
        s_whi = sem("s_whi")
        s_wlo = sem("s_wlo")
        s_acc = sem("s_acc")
        s_at = sem("s_at")
        s_cm = sem("s_cm")
        s_yt, s_ytr, s_ye = sem("s_yt"), sem("s_ytr"), sem("s_ye")
        s_out = sem("s_out")
        s_free = sem("s_free")
        s_mpe, s_mact, s_mdve = sem("s_mpe"), sem("s_mact"), sem("s_mdve")

        BATCHES = [(qt, j) for qt in range(TT) for j in range(2)]
        NBT = len(BATCHES)
        pe_names = ["hm", "kv", "ktok", "rot", "s0"]
        for b in range(NBT):
            pe_names += ([f"s{b + 1}"] if b + 1 < NBT else []) + [f"t{b}", f"o{b}"]
        pe_names += [f"pw{g}" for g in range(4)]
        act_names = ["zsq", "root", "kpast", "vtok", "ktok"]
        for b in range(NBT):
            act_names += [f"e{b}", f"pt{b}", f"oh{b}"]
        act_names += [f"ph{g}" for g in range(4)]
        dve_names = ["rc", "qn", "rope"]
        for b in range(NBT):
            dve_names += [f"nb{b}", f"p{b}", f"ol{b}"]
        dve_names += [f"pl{g}" for g in range(4)]
        mpe, mact, mdve = Marks(s_mpe, pe_names), Marks(s_mact, act_names), Marks(s_mdve, dve_names)

        block = ctx.enter_context(nc.Block())

        def filled(stage, pair):
            return FILLED0[stage] + DMAS[stage] * (pair + 1)

        @block.sync
        def _(sp):
            def slot_free(sem_, value):
                sp.wait_ge(sem_, value)
                sp.sem_inc(s_free, 1)

            rows = [(R_N1, norm1_g.rearrange("l (k p) -> (l k) p", p=P)),
                    (R_N2, norm2_g.rearrange("l (k p) -> (l k) p", p=P)),
                    (R_FIN, final_g.rearrange("(k p) -> k p", p=P)),
                    (R_PS, pool_scale.rearrange("l (k p) -> (l k) p", p=P)),
                    (R_CW, c_conv_w.rearrange("l w (k p) -> (l w k) p", p=P)),
                    (R_CTX, c_ctx.rearrange("(k p) -> k p", p=P)),
                    (R_C, c.rearrange("b (k p) -> (b k) p", p=P))]
            for at, src in rows:
                sp.dma_start(VR[at:at + src.shape[0], :], src).then_inc(s_vec, 16)
            for at, src in ((R_QG, q_norm_g), (R_KG, k_norm_g)):
                for j in range(2):
                    sp.dma_start(VR[at:at + 1, 64 * j:64 * j + 64], src).then_inc(s_vec, 16)
            sp.dma_start(MBR[0:96, :], mod_b.rearrange("l (k p) -> (l k) p", p=P)).then_inc(s_vec, 16)
            sp.dma_start(IDENT[:, :], k_ident).then_inc(s_vec, 16)

            def load_mod(l, b, k):
                sp.dma_start(MODR[:, k, :, :], mod_w[l, :, bass.ds(b * MODB, MODB)]
                             .rearrange("(k p) m -> p k m", p=P)).then_inc(mod_in[k], 16)

            for k in range(2):
                load_mod(0, k, k)
            sp.dma_start(XS[:, 0, :], x_prompt[0, :, :]).then_inc(s_x, 16)
            sp.dma_start(XS[:, 1:3, :], x_sample[0, :, :].rearrange("(t p) d -> p t d", p=P)).then_inc(s_x, 16)
            sp.dma_start(HMEAN[:, :], k_headmean).then_inc(s_cst, 16)
            sp.dma_start(ROT[:, :], k_rot).then_inc(s_cst, 16)
            sp.dma_start(IOTA[:, :], k_iota).then_inc(s_cst, 16)
            sp.dma_start(SKR[:, :, :], peer_subkeys.rearrange("l s e k -> e (l s) k")).then_inc(s_cst, 16)
            with sp.Fori(1, MODPAIRS) as i:
                for k in range(2):
                    slot_free(s_mrow, 2 * i - 1 + k)
                    load_mod(0, 2 * i + k, k)

            def unit_free(n):
                slot_free(s_lo, n + 1)

            w_in = a_in_w[0, :, :]
            for u in range(COUNT["q"]):
                n = UNIT0["q"] + u
                unit_free(n)
                dst = RAW[:, n % 2, :].rearrange("p (k m) -> p k m", k=KC)
                for j in range(2):
                    h0 = 64 * (4 * j + u)
                    sp.dma_start(dst[:, :, 64 * j:64 * j + 64],
                                 w_in[:, h0:h0 + 64].rearrange("(k p) m -> p k m", p=P)).then_inc(raw_in[n % 2], 16)

            def load_units(stage, w, m0, first=0):
                with sp.Fori(first // 2, COUNT[stage] // 2) as i:
                    for k in range(2):
                        unit_free(UNIT0[stage] + 2 * i + k)
                        sp.dma_start(RAW[:, k, :].rearrange("p (k m) -> p k m", k=KC),
                                     w[:, bass.ds(m0 + (2 * i + k) * P, P)].rearrange("(k p) m -> p k m", p=P))\
                            .then_inc(raw_in[k], 16)

            load_units("kvp", w_in, 512)
            sp.wait_ge(s_gev, 3)
            sp.wait_ge(s_xe, KC)
            sp.dma_start(COS, k_cos).then_inc(s_att, 16)
            sp.dma_start(SIN, k_sin).then_inc(s_att, 16)
            sp.dma_start(RCNT, k_rcnt).then_inc(s_att, 16)
            sp.wait_ge(s_hlo, KC)
            sp.dma_start(VPAST, cache_v[0, 0, :, :, :].rearrange("s h d -> s (h d)")).then_inc(s_att, 16)
            sp.dma_start(KPAST, cache_k[0, 0, :, :, :].rearrange("s h d -> s (h d)")).then_inc(s_att, 16)
            sp.dma_start(PW, pool_w[0, :, :, :].rearrange("g c d -> c g d")).then_inc(s_att, 16)
            w_o = a_out_w[0, :, :]
            with sp.Fori(0, COUNT["a_out"] // 2) as i:
                for k in range(2):
                    unit_free(UNIT0["a_out"] + 2 * i + k)
                    dst = RAW[:, k, :].rearrange("p (k m) -> p k m", k=KC)
                    cols = w_o[:, bass.ds((2 * i + k) * P, P)]
                    for j in range(2):
                        sp.dma_start(dst[64 * j:64 * j + 64, 0:4, :],
                                     cols[256 * j:256 * j + 256, :].rearrange("(c d) m -> d c m", d=64))\
                            .then_inc(raw_in[k], 16)
                    sp.dma_start(dst[:, 4:8, :], cols[512:1024, :].rearrange("(k p) m -> p k m", p=P))\
                        .then_inc(raw_in[k], 16)

            def load_u(l, t, k):
                sp.dma_start(URAW[:, k, :], peer_u[l, bass.ds(t * P, P), :]).then_inc(u_in[k], 16)

            def load_v(l, t, k):
                unit_free(UNIT0[f"v{l}"] + t)
                sp.dma_start(RAW[:, k, :], peer_v[l, bass.ds(t * P, P), :]).then_inc(raw_in[k], 16)

            def load_g(l, t, k):
                sp.dma_start(GIN[:, k, :], GD[l, bass.ds(t, 1), :, :].rearrange("a p t -> p (a t)")).then_inc(g_in[k], 16)

            for l in range(LAYERS):
                if l:
                    wc = c_in_w[0, :, :]
                    with sp.Fori(0, 4) as i:
                        for q in range(6):
                            unit_free(UNIT0["c_in"] + 6 * i + q)
                            part = (1, 2, 0)[q % 3]
                            sp.dma_start(RAW[:, q % 2, :].rearrange("p (k m) -> p k m", k=KC),
                                         wc[:, bass.ds(part * D + (2 * i + q // 3) * P, P)]
                                         .rearrange("(k p) m -> p k m", p=P)).then_inc(raw_in[q % 2], 16)
                    load_units("c_out", c_out_w[0, :, :], 0)
                load_units(f"wq{l}", peer_wq[l, :, :], 0)
                for k in range(2):
                    if l:
                        sp.wait_ge(s_tr, 2 * P)
                    load_u(l, k, k)
                for k in range(2):
                    load_v(l, k, k)
                if l == 0:
                    with sp.Fori(0, MODPAIRS) as i:
                        for k in range(2):
                            slot_free(s_mrow, 2 * MODPAIRS + 2 * i - 1 + k)
                            load_mod(1, 2 * i + k, k)
                for tile in range(TT):
                    sp.wait_ge(s_gev, 4 + 32 * (TT * l + tile + 1))
                    sp.dma_start(GD[l, :, :, tile * P:(tile + 1) * P].rearrange("i p t -> p i t"), STAGE)\
                        .then_inc(s_gst, 16)
                sp.wait_ge(s_gst, 16 * TT * (l + 1))
                for k in range(2):
                    if l:
                        sp.wait_ge(s_w, P)
                    load_g(l, k, k)
                with sp.Fori(1, P // 2) as i:
                    for k in range(2):
                        t = 2 * i + k
                        slot_free(s_tr, 2 * (P * l + t - 1))
                        load_u(l, t, k)
                        load_v(l, t, k)
                        slot_free(s_w, P * l + t - 1)
                        load_g(l, t, k)
            sp.wait_ge(s_ye, 6)
            sp.dma_start(y_prompt[0, :, :], YTOK[:, 0, :]).then_inc(s_out, 16)
            sp.dma_start(y_sample[0, :, :].rearrange("(t p) d -> p t d", p=P), YTOK[:, 1:3, :]).then_inc(s_out, 16)
            sp.wait_ge(s_nkv, 32)
            sp.wait_ge(s_out, 32)

        @block.gpsimd
        def _(pool):
            own = Steps(pool, s_pool)
            pool.memset(MEAN1[:, :], 1.0 / D).then_inc(s_cst, 16)
            pool.wait_ge(s_ev, 2 + 10)
            pool.wait_ge(s_att, 16 * 6)
            pool.wait_ge(s_hlo, KC)
            own.do(pool.memset(XPAD, 0.0))
            pads = ((8, 0, NPROMPT), (8 + NPROMPT + 16, NPROMPT, NSAMPLE))
            for g, win in enumerate(WINDOWS):
                zg = Z[:, 6 + g, :]
                for at, t0, n in pads:
                    own.mark(pool.tensor_copy(XPAD[:, at:at + n], zg[:, t0:t0 + n]))
                own.wait()
                src, bufs, half = XPAD, [SUM0, SUM1], 1
                while half < win:
                    dst = bufs[0]
                    bufs.reverse()
                    n = PADW - 2 * half + 1
                    own.do(pool.tensor_tensor(dst[:, 0:n], src[:, 0:n], src[:, half:half + n], ALU.add))
                    src, half = dst, 2 * half
                out = bufs[0]
                for at, t0, n in pads:
                    a = at - win // 2
                    own.mark(pool.tensor_tensor(out[:, t0:t0 + n], src[:, a:a + n], RCNT[:, g, t0:t0 + n], ALU.mult))
                own.wait()
                pool.tensor_tensor(zg, out[:, 0:T], zg, ALU.subtract).then_inc(s_pm, 1)
                pool.wait_ge(s_pm, g + 1)

        @block.scalar
        def _(act):
            own = Steps(act, s_acts)
            nc.scalar.sem_inc(s_ev, 2)
            nc.scalar.sem_inc(s_gev, 4)
            nc.scalar.sem_inc(s_mod, 1)
            nc.scalar.sem_inc(s_gel, 1)
            act.wait_ge(s_vt, 1)
            nc.scalar.activation(COND[:, :, :].rearrange("p k c -> p c k"),
                                 VT[:, R_CTX:R_CTX + 16].rearrange("p (c k) -> p c k", c=2), ACT.Silu).then_inc(s_act0, 1)

            def mod(l, part, parts=1):
                n = MODPAIRS // parts
                with act.Fori(part * n, (part + 1) * n) as i:
                    for k in range(2):
                        act.wait_ge(s_mrow, 2 * MODPAIRS * l + 2 * i + k + 1)
                        nc.scalar.activation(MROW[:, k, :], PS[0:2, 5 + k, 0:MODB], ACT.Copy).then_inc(s_mev, 1)
                    act.wait_ge(s_mtr, MODPAIRS * l + i + 1)
                    nc.scalar.activation(MODT[:, l, bass.ds(4 * i, 4), :],
                                         PS[:, 7, 0:8].rearrange("p (a b) -> p a b", b=2), ACT.Copy).then_inc(s_mod, 1)

            mod(0, 0)
            act.wait_ge(s_init, 2)
            nc.scalar.activation(SKT[:, :, :].rearrange("p a b -> p (a b)"), PS[:, 4, :], ACT.Copy).then_inc(s_act0, 1)

            def norm(n):
                l, which = divmod(n, 2)
                for k in range(KC):
                    q = KC * n + k
                    if n or k >= 2:
                        act.wait_ge(s_ss, q - 1)
                    if k == 0:
                        if n == 0:
                            act.wait_ge(s_xe, KC)
                        else:
                            act.wait_ge(s_res, KC * n)
                    nc.scalar.activation(SQ[:, k % 2, :], xT[:, k, :], ACT.Square).then_inc(s_sq, 1)
                act.wait_ge(s_rc, n + 1)
                nc.scalar.activation(RT, RC, ACT.Sqrt).then_inc(s_rt, 1)
                if n == 4:
                    return
                for k in range(KC):
                    act.wait_ge(s_t1, q0 := KC * n + k + 1)
                    for t0, m, cnd in SEGS:
                        ins = nc.scalar.activation(HH[:, k, t0:t0 + m], T1[:, k % 2, t0:t0 + m], ACT.Identity,
                                                   bias=MODT[:, l, 24 * which + k, cnd:cnd + 1])
                    ins.then_inc(s_hhi, 1)

            def hi(stage, pair, k):
                act.wait_ge(raw_in[k], filled(stage, pair))
                act.wait_ge(s_unit, UNIT0[stage] + 2 * pair + k + 1)
                nc.scalar.activation(WHI[k][:, :], RAW[:, k, :], ACT.Copy).then_inc(s_hi, 1)

            def his(stage, evacuate=None):
                with act.Fori(0, COUNT[stage] // 2 - 1) as i:
                    hi(stage, i, 1)
                    if evacuate:
                        evacuate(2 * i, 0)
                    hi(stage, i + 1, 0)
                    if evacuate:
                        evacuate(2 * i + 1, 1)
                i = COUNT[stage] // 2 - 1
                hi(stage, i, 1)
                if evacuate:
                    evacuate(2 * i, 0)
                hi(NEXT[stage], 0, 0)
                if evacuate:
                    evacuate(2 * i + 1, 1)

            def to_view(view, stage, first):
                def evacuate(u, k):
                    act.wait_ge(s_unit, UNIT0[stage] + u + 3)
                    nc.scalar.activation(view[:, bass.ds(first + u, 1), :].rearrange("p a t -> p (a t)"),
                                         PS[:, k, 0:T], ACT.Copy).then_inc(s_ev, 1)
                return evacuate

            hi("q", 0, 0)
            norm(0)
            his("q", to_view(Z, "q", 0))
            his("kvp", to_view(Z, "kvp", 4))

            act.wait_ge(s_ev, 2 + 10)
            mact.mark("zsq", nc.scalar.activation(ZS[:, :, :], Z[:, 0:5, :], ACT.Square))
            mdve.wait(act, "rc")
            mact.mark("root", nc.scalar.activation(ZS[:, :, :], QN[:, :, :], ACT.Sqrt))
            mpe.wait(act, "kv")
            mact.mark("kpast", nc.scalar.activation(KALL[:, NSAMPLE:T], PS[:, 7, 0:P], ACT.Copy))
            mact.mark("vtok", nc.scalar.activation(VTOK[:, :, :], PS[:, 7, P:512].rearrange("p (a b) -> p a b", a=3), ACT.Copy))
            mpe.wait(act, "ktok")
            mact.mark("ktok", nc.scalar.activation(KTOK, PS[:, 0, 0:P], ACT.Copy))
            mact.wait(act, "ktok")
            act.dma_start(new_k[0, 0, :, :, :].rearrange("s h d -> s (h d)"), KTOK).then_inc(s_nkv, 16)
            act.dma_start(new_v[0, 0, :, :, :].rearrange("s h d -> s (h d)"), VTOK[:, 0, :]).then_inc(s_nkv, 16)
            for b, (qt, j) in enumerate(BATCHES):
                n = P if qt == 0 else T
                mdve.wait(act, f"nb{b}")
                for q in range(4):
                    ins = nc.scalar.activation(PROB[b % 2][:, q, 0:n], PS[:, q, 0:n], ACT.Exp, bias=NB[:, q:q + 1],
                                               scale=0.125, accum_out=SM[:, q:q + 1])
                mact.mark(f"e{b}", ins)
                mpe.wait(act, f"t{b}")
                mact.mark(f"pt{b}", nc.scalar.activation(PROBT[:, :, 0:n], PS[:, 4:8, 0:n], ACT.Copy))
                mpe.wait(act, f"o{b}")
                rows = slice(64 * j, 64 * j + 64)
                mact.mark(f"oh{b}", nc.scalar.activation(HH[rows, 0:4, qt * P:qt * P + P],
                                                         PS[rows, 4, :].rearrange("p (a b) -> p a b", a=4), ACT.Copy))
            for g in range(4):
                mpe.wait(act, f"pw{g}")
                mact.mark(f"ph{g}", nc.scalar.activation(HH[:, 4 + g, :], PS[:, g, 0:T], ACT.Copy,
                                                         scale=VT[:, R_PS + g:R_PS + g + 1]))
            his("a_out")

            for l in range(LAYERS):
                if l:
                    norm(2)
                    his("c_in")
                    for k in range(0, KC, 2):
                        act.wait_ge(s_cm, KC)
                        nc.scalar.activation(HH[:, k:k + 2, :], CM[:, k:k + 2, :], ACT.Copy).then_inc(s_hhi, 1)
                    his("c_out")
                else:
                    act.wait_ge(s_nkv, 32)
                norm(2 * l + 1)
                his(f"wq{l}", to_view(QT, f"wq{l}", 0))
                for tile in range(TT):
                    g = TT * l + tile
                    act.wait_ge(s_sc, g + 1)
                    if tile:
                        act.wait_ge(s_l1, g)
                    nc.scalar.activation(SC[:, :, :].rearrange("p (a b) c -> p a (b c)", a=4), PS[:, 1:5, :], ACT.Copy)\
                        .then_inc(s_scc, 1)
                    if l == 0:
                        if tile >= 1:
                            mod(1, tile - 1, 3)
                    if tile:
                        _tail(act, nc, g - 1, tile - 1, EX, s_d, s_e, s_ptr, s_pte, PS, IT1, IT2)
                if l == 0:
                    mod(1, 2, 3)
                _tail(act, nc, TT * l + 2, 2, EX, s_d, s_e, s_ptr, s_pte, PS, IT1, IT2)
                for tile in range(TT):
                    g0 = 32 * (TT * l + tile)
                    if tile:
                        act.wait_ge(s_gst, 16 * (TT * l + tile))
                    with act.Fori(0, 8) as i:
                        for k in range(4):
                            act.wait_ge(s_gm, 2 + g0 + 4 * i + k + 1)
                            nc.scalar.activation(STAGE[:, :, bass.ds(16 * i + 4 * k, 4)].rearrange("p i t -> p t i"),
                                                 PS[:, 2 + k, :].rearrange("p (t i) -> p t i", t=4), ACT.Copy).then_inc(s_gev, 1)

                def u_hi(t, k, half):
                    g = P * l + t
                    act.wait_ge(s_tr, 2 * g + half + 1)
                    if half == 0 and not (isinstance(t, int) and g < 2):
                        act.wait_ge(s_S, g - 1)
                    nc.scalar.activation(UHI[k][:, 512 * half:512 * half + 512], PS[:, 1, :], ACT.Copy).then_inc(s_uhi, 1)

                def gelu(t, k):
                    g = P * l + t
                    act.wait_ge(s_S, g + 1)
                    if not (isinstance(t, int) and g < 2):
                        act.wait_ge(s_wlo, g - 1)
                    nc.scalar.activation(GEL[:, k, :], PS[:, 0, 0:T], ACT.Gelu).then_inc(s_gel, 1)

                def w_hi(t, k):
                    g = P * l + t
                    act.wait_ge(s_w, g + 1)
                    act.wait_ge(s_unit, UNIT0[f"v{l}"] + t + 1)
                    nc.scalar.activation(EHI[k][:, :], GEL[:, k, :], ACT.Copy).then_inc(s_whi, 1)

                def body(t, k, last=False):
                    if not last:
                        u_hi(t + 1, 1 - k, 0)
                    gelu(t, k)
                    if not last:
                        u_hi(t + 1, 1 - k, 1)
                    w_hi(t, k)

                v = f"v{l}"
                u_hi(0, 0, 0)
                u_hi(0, 0, 1)
                body(0, 0)
                hi(v, 0, 1)
                with act.Fori(0, P // 2 - 1) as i:
                    body(2 * i + 1, 1)
                    hi(v, i + 1, 0)
                    body(2 * i + 2, 0)
                    hi(v, i + 1, 1)
                body(P - 1, 1, last=True)
                if l == 0:
                    hi("c_in", 0, 0)
                act.wait_ge(s_unit, UNIT0[v] + P + 2)
                for tile in range(TT):
                    nc.scalar.activation(XS[:, tile, :].rearrange("p (a b) -> p a b", a=2),
                                         PS[:, 2 + 2 * tile:4 + 2 * tile, :], ACT.Copy).then_inc(s_acc, 1)
            norm(4)
            for q in range(6):
                act.wait_ge(s_ytr, q + 1)
                nc.scalar.activation(YTOK[:, q // 2, 512 * (q % 2):512 * (q % 2) + 512], PS[:, 3 + q % 2, :], ACT.Copy)\
                    .then_inc(s_ye, 1)

        @block.tensor
        def _(pe):
            nc.tensor.sem_inc(s_unit, 2)
            nc.tensor.sem_inc(s_gm, 2)
            pe.wait_ge(s_vec, 16 * 13)
            nc.tensor.transpose(PS[:, 3, 0:VROWS], VR[0:VROWS, :], IDENT[0:VROWS, 0:VROWS])
            nc.tensor.transpose(PS[:, 3, P:P + 96], MBR[0:96, :], IDENT[0:96, 0:96]).then_inc(s_init, 1)
            pe.wait_ge(s_cst, 16 * 5)
            for q in range(4):
                ins = nc.tensor.transpose(PS[:, 4, q * P:q * P + P], SKR[:, q, :], IDENT[:, :])
            ins.then_inc(s_init, 1)
            pe.wait_ge(s_x, 32)
            for k in range(KC):
                if k >= 2:
                    pe.wait_ge(s_xe, k - 1)
                for tile in range(TT):
                    ins = nc.tensor.transpose(PS[:, k % 2, tile * P:tile * P + P], XS[:, tile, k * P:k * P + P], IDENT[:, :])
                ins.then_inc(s_xt, 1)
            pe.wait_ge(s_act0, 1)

            def mod(l, part, parts=1):
                n = MODPAIRS // parts
                with pe.Fori(part * n, (part + 1) * n) as i:
                    pair = MODPAIRS * l + i
                    for k in range(2):
                        pe.wait_ge(mod_in[k], 16 * (pair + 1))
                        for kc in range(KC):
                            ins = nc.tensor.matmul(PS[0:2, 5 + k, 0:MODB], COND[:, kc, :], MODR[:, k, kc, :],
                                                   start=kc == 0, stop=kc == KC - 1)
                        ins.then_inc(s_mrow, 1)
                    pe.wait_ge(s_mod, pair + 1)
                    for k in range(2):
                        pe.wait_ge(s_mev, 2 * pair + k + 1)
                        for m in range(2):
                            ins = nc.tensor.matmul(PS[:, 7, 4 * k + 2 * m:4 * k + 2 * m + 2],
                                                   MROW[:, k, m * P:m * P + P], IDENT[0:2, 0:2], start=True, stop=True)
                    ins.then_inc(s_mtr, 1)

            mod(0, 0)

            def norm(n):
                for k in range(KC):
                    pe.wait_ge(s_sq, KC * n + k + 1)
                    nc.tensor.matmul(PS[:, 2, 0:T], MEAN1[:, :], SQ[:, k % 2, :], start=k == 0, stop=k == KC - 1)\
                        .then_inc(s_ss, 1)

            def project(stage):
                with pe.Fori(0, COUNT[stage] // 2) as i:
                    for s in range(2):
                        u = 2 * i + s
                        pe.wait_ge(s_lo, UNIT0[stage] + u + 3)
                        pe.wait_ge(s_ev, PROJ0[stage] + u + 1)
                        for k in range(KC):
                            cols = slice(k * P, k * P + P)
                            nc.tensor.matmul(PS[:, s, 0:T], WHI[s][:, cols], HH[:, k, :], start=k == 0, stop=False)
                            nc.tensor.matmul(PS[:, s, 0:T], WHI[s][:, cols], HL[:, k, :], start=False, stop=False)
                            ins = nc.tensor.matmul(PS[:, s, 0:T], WLO[s][:, cols], HH[:, k, :], start=False, stop=k == KC - 1)
                        ins.then_inc(s_unit, 1)

            norm(0)
            pe.wait_ge(s_hhi, KC)
            pe.wait_ge(s_hlo, KC)
            project("q")
            project("kvp")

            mact.wait(pe, "zsq")
            for q in range(5):
                ins = nc.tensor.matmul(PS[:, 2 + q, 0:T], HMEAN[:, :], ZS[:, q, :], start=True, stop=True)
            mpe.mark("hm", ins)
            pe.wait_ge(s_att, 16 * 6)
            nc.tensor.transpose(PS[:, 7, 0:P], KPAST, IDENT[:, :])
            for tile in range(TT):
                ins = nc.tensor.transpose(PS[:, 7, (tile + 1) * P:(tile + 2) * P], Z[:, 5, tile * P:tile * P + P], IDENT[:, :])
            mpe.mark("kv", ins)
            mdve.wait(pe, "qn")
            mpe.mark("ktok", nc.tensor.transpose(PS[:, 0, 0:P], QN[:, 4, 0:P], IDENT[:, :]))
            for q in range(5):
                ins = nc.tensor.matmul(PS[:, 2 + q, 0:NSAMPLE], ROT[:, :], QN[:, q, NPROMPT:T], start=True, stop=True)
            mpe.mark("rot", ins)

            def scores(b):
                qt, j = BATCHES[b]
                rows = slice(64 * j, 64 * j + 64)
                if b:
                    mact.wait(pe, f"e{b - 1}")
                else:
                    mact.wait(pe, "ktok")
                if b == 2:
                    mdve.wait(pe, "rope")
                    mact.wait(pe, "kpast")
                for q in range(4):
                    if qt == 0:
                        ins = nc.tensor.matmul(PS[:, q, 0:P], QN[rows, q, 0:P], QN[rows, 4, 0:P], start=True, stop=True)
                    else:
                        ins = nc.tensor.matmul(PS[:, q, 0:T], RQ[rows, q, (qt - 1) * P:qt * P], KALL[rows, :], start=True, stop=True)
                mpe.mark(f"s{b}", ins)

            mdve.wait(pe, "rope")
            scores(0)
            for b, (qt, j) in enumerate(BATCHES):
                rows = slice(64 * j, 64 * j + 64)
                nkt = 1 if qt == 0 else 3
                if b + 1 < NBT:
                    scores(b + 1)
                mdve.wait(pe, f"p{b}")
                if b:
                    mdve.wait(pe, f"ol{b - 1}")
                else:
                    mact.wait(pe, "vtok")
                for q in range(4):
                    for kt in range(nkt):
                        ins = nc.tensor.transpose(PS[:, 4 + q, kt * P:kt * P + P], PROB[b % 2][:, q, kt * P:kt * P + P], IDENT[:, :])
                mpe.mark(f"t{b}", ins)
                mact.wait(pe, f"pt{b}")
                for kt in range(nkt):
                    if qt == 0:
                        val = VTOK[:, 0, rows]
                    else:
                        val = VTOK[:, 1 + kt, rows] if kt < 2 else VPAST[:, rows]
                    ins = nc.tensor.matmul(PS[rows, 4, :], val, PROBT[:, :, kt * P:kt * P + P], start=kt == 0, stop=kt == nkt - 1)
                mpe.mark(f"o{b}", ins)
            mact.wait(pe, f"e{NBT - 1}")
            for g in range(4):
                pe.wait_ge(s_pm, g + 1)
                mpe.mark(f"pw{g}", nc.tensor.matmul(PS[:, g, 0:T], PW[:, g, :], Z[:, 6 + g, :], start=True, stop=True))
            mdve.wait(pe, "pl3")
            project("a_out")

            for l in range(LAYERS):
                if l:
                    norm(2)
                    pe.wait_ge(s_hlo, 3 * KC)
                    project("c_in")
                    pe.wait_ge(s_hlo, 3 * KC + 4)
                    project("c_out")
                norm(2 * l + 1)
                pe.wait_ge(s_hlo, (4 * KC + 4) if l else 2 * KC)
                project(f"wq{l}")

                def tile_scores(tile):
                    if tile:
                        pe.wait_ge(s_scc, TT * l + tile)
                    else:
                        pe.wait_ge(s_ev, 2 + PROJ0[f"wq{l}"] + 16)
                    for u in range(16):
                        ins = nc.tensor.matmul(PS[:, 1 + u // 4, (u % 4) * P:(u % 4) * P + P],
                                               QT[:, u, tile * P:tile * P + P], SKT[:, 2 * l + u % 2, :], start=True, stop=True)
                    ins.then_inc(s_sc, 1)

                def turn_picks(tile):
                    g = TT * l + tile
                    pe.wait_ge(s_pick, g + 1)
                    if g:
                        pe.wait_ge(s_pte, g)
                        pe.wait_ge(s_pts, g)
                    for q, src in enumerate((ID1, ID2, GT.rearrange("p a b -> p (a b)"))):
                        ins = nc.tensor.transpose(PS[:, 0, q * P:q * P + P], src, IDENT[:, :])
                    ins.then_inc(s_ptr, 1)

                pe.wait_ge(s_act0, 2)
                for tile in range(TT):
                    tile_scores(tile)
                    if l == 0 and tile:
                        mod(1, tile - 1, 3)
                    if tile:
                        turn_picks(tile - 1)
                if l == 0:
                    mod(1, 2, 3)
                turn_picks(2)

                for tile in range(TT):
                    g0 = 32 * (TT * l + tile)
                    with pe.Fori(0, 8) as i:
                        for k in range(4):
                            g = g0 + 4 * i + k
                            pe.wait_ge(s_oh, g + 1)
                            pe.wait_ge(s_gev, g + 1)
                            for q in range(4):
                                for part in range(3):
                                    ins = nc.tensor.matmul(PS[:, 2 + k, q * P:q * P + P], OH2[:, 4 * (k % 2) + q, :],
                                                           OH1[:, 4 * (k % 2) + q, part, :], start=part == 0, stop=part == 2)
                            ins.then_inc(s_gm, 1)

                def turn_half(g, pair, k, half):
                    if half == 0:
                        pe.wait_ge(u_in[k], 16 * (64 * l + pair + 1))
                    pe.wait_ge(s_ulo, 2 * g + half + 1)
                    for q in range(4):
                        c0 = (4 * half + q) * P
                        ins = nc.tensor.transpose(PS[:, 1, q * P:q * P + P], URAW[:, k, c0:c0 + P], IDENT[:, :])
                    ins.then_inc(s_tr, 1)

                def s_tile(g, k):
                    pe.wait_ge(s_ulo, 2 * g + 3)
                    pe.wait_ge(s_gel, g + 1)
                    for c_ in range(KC):
                        cols = slice(c_ * P, c_ * P + P)
                        nc.tensor.matmul(PS[:, 0, 0:T], UHI[k][:, cols], HH[:, c_, :], start=c_ == 0, stop=False)
                        nc.tensor.matmul(PS[:, 0, 0:T], UHI[k][:, cols], HL[:, c_, :], start=False, stop=False)
                        ins = nc.tensor.matmul(PS[:, 0, 0:T], ULO[k][:, cols], HH[:, c_, :], start=False, stop=c_ == KC - 1)
                    ins.then_inc(s_S, 1)

                def v_tile(t, k, first=False, last=False):
                    pe.wait_ge(s_wlo, P * l + t + 1)
                    pe.wait_ge(s_lo, UNIT0[f"v{l}"] + t + 3)
                    for tile in range(TT):
                        tok = slice(tile * P, tile * P + P)
                        for q, (e, w) in enumerate(((EHI, WHI), (EHI, WLO), (ELO, WHI))):
                            for half in range(2):
                                ins = nc.tensor.matmul(PS[:, 2 + 2 * tile + half, :], e[k][:, tok],
                                                       w[k][:, 512 * half:512 * half + 512],
                                                       start=first and q == 0, stop=last and q == 2)
                    ins.then_inc(s_unit, 1)

                G = P * l
                turn_half(G, 0, 0, 0)
                turn_half(G, 0, 0, 1)
                turn_half(G + 1, 0, 1, 0)
                s_tile(G, 0)
                turn_half(G + 1, 0, 1, 1)
                turn_half(G + 2, 1, 0, 0)
                s_tile(G + 1, 1)
                turn_half(G + 2, 1, 0, 1)
                pe.wait_ge(s_gev, 4 + 32 * TT * (l + 1))
                v_tile(0, 0, first=True)
                with pe.Fori(1, P // 2 - 1) as i:
                    turn_half(G + 2 * i + 1, i, 1, 0)
                    s_tile(G + 2 * i, 0)
                    turn_half(G + 2 * i + 1, i, 1, 1)
                    v_tile(2 * i - 1, 1)
                    turn_half(G + 2 * i + 2, i + 1, 0, 0)
                    s_tile(G + 2 * i + 1, 1)
                    turn_half(G + 2 * i + 2, i + 1, 0, 1)
                    v_tile(2 * i, 0)
                t = P - 2
                turn_half(G + t + 1, P // 2 - 1, 1, 0)
                s_tile(G + t, 0)
                turn_half(G + t + 1, P // 2 - 1, 1, 1)
                v_tile(t - 1, 1)
                s_tile(G + t + 1, 1)
                v_tile(t, 0)
                v_tile(t + 1, 1, last=True)
                pe.wait_ge(s_acc, TT * (l + 1))
                for k in range(KC):
                    if k >= 2:
                        pe.wait_ge(s_res, KC * (2 * l + 1) + k - 1)
                    if l == 0 and k == 0:
                        pe.wait_ge(s_gel, P + 1)
                    for tile in range(TT):
                        ins = nc.tensor.transpose(PS[:, k % 2, tile * P:tile * P + P], XS[:, tile, k * P:k * P + P], IDENT[:, :])
                    ins.then_inc(s_at, 1)
            norm(4)
            for q in range(6):
                tile, half = divmod(q, 2)
                pe.wait_ge(s_yt, KC)
                if q >= 2:
                    pe.wait_ge(s_ye, q - 1)
                for m in range(4):
                    ins = nc.tensor.transpose(PS[:, 3 + half, m * P:m * P + P], YT[:, 4 * half + m, tile * P:tile * P + P], IDENT[:, :])
                ins.then_inc(s_ytr, 1)

        @block.vector
        def _(dve):
            V = nc.vector
            own = Steps(dve, s_dve)
            V.sem_inc(s_lo, 2)
            V.sem_inc(s_ulo, 1)
            dve.wait_ge(s_init, 1)
            V.tensor_copy(MBT[:, :], PS[:, 3, P:P + 96])
            V.tensor_copy(VT[:, :], PS[:, 3, 0:VROWS]).then_inc(s_vt, 1)
            for k in range(KC):
                dve.wait_ge(s_xt, k + 1)
                V.tensor_copy(xT[:, k, :], PS[:, k % 2, 0:T]).then_inc(s_xe, 1)
            dve.wait_ge(s_cst, 16 * 5)
            own.mark(V.tensor_copy(IOTAB[:, :], IOTA[:, :]))

            def modulation(l):
                dve.wait_ge(s_mod, 1 + MODPAIRS * (l + 1))
                dve.wait_ge(s_vt, 1)
                own.do(V.tensor_tensor(MODT[:, l, :, :], MODT[:, l, :, :],
                                       MBT[:, 48 * l:48 * l + 48].unsqueeze(2).to_broadcast([P, 48, 2]), ALU.add))
                for which, r in ((0, R_N1), (1, R_N2)):
                    ins = V.scalar_tensor_tensor(out=GS[:, l, which, :, :], in0=MODT[:, l, 24 * which + 8:24 * which + 16, :],
                                                 scalar=1.0, in1=VT[:, r + 8 * l:r + 8 * l + 8].unsqueeze(2).to_broadcast([P, KC, 2]),
                                                 op0=ALU.add, op1=ALU.mult)
                ins.then_inc(s_gs, 1)
                dve.wait_ge(s_gs, l + 1)

            def rsqrt_step(y, v, t):
                own.do(V.tensor_tensor(t, y, y, ALU.mult))
                own.do(V.tensor_tensor(t, t, v, ALU.mult))
                own.do(V.tensor_scalar(t, t, -0.5, 1.5, ALU.mult, ALU.add))
                own.do(V.tensor_tensor(y, y, t, ALU.mult))

            def norm(n):
                l, which = divmod(n, 2)
                dve.wait_ge(s_ss, KC * (n + 1))
                own.do(V.tensor_scalar(MV, PS[:, 2, 0:T], EPS, None, ALU.add))
                V.reciprocal(RC, MV).then_inc(s_rc, 1)
                dve.wait_ge(s_rt, n + 1)
                rsqrt_step(RT, MV, NT)
                if n == 4:
                    for k in range(KC):
                        V.scalar_tensor_tensor(out=YT[:, k, :], in0=xT[:, k, :], scalar=VT[:, R_FIN + k:R_FIN + k + 1],
                                               in1=RT, op0=ALU.mult, op1=ALU.mult).then_inc(s_yt, 1)
                    return

                def scaled(k):
                    for t0, m, cnd in SEGS:
                        ins = V.scalar_tensor_tensor(out=T1[:, k % 2, t0:t0 + m], in0=xT[:, k, t0:t0 + m],
                                                     scalar=GS[:, l, which, k, cnd:cnd + 1], in1=RT[:, t0:t0 + m],
                                                     op0=ALU.mult, op1=ALU.mult)
                    ins.then_inc(s_t1, 1)

                def low(k):
                    dve.wait_ge(s_hhi, (KC * n + k + 1) + (4 if n == 3 else 0))
                    for t0, m, cnd in SEGS:
                        ins = V.scalar_tensor_tensor(out=HL[:, k, t0:t0 + m], in0=T1[:, k % 2, t0:t0 + m],
                                                     scalar=MODT[:, l, 24 * which + k, cnd:cnd + 1],
                                                     in1=HH[:, k, t0:t0 + m].bitcast(F32), op0=ALU.add, op1=ALU.subtract)
                    ins.then_inc(s_hlo, 1)

                hlo0 = KC * n + (4 if n == 3 else 0)
                scaled(0)
                for k in range(KC):
                    if k + 1 < KC:
                        if k >= 1:
                            dve.wait_ge(s_hlo, hlo0 + k)
                        scaled(k + 1)
                    if k == 0:
                        dve.wait_ge(s_t1, KC * n + 1)
                    low(k)

            def lo(stage, pair, k):
                dve.wait_ge(s_hi, UNIT0[stage] + 2 * pair + k + 1)
                V.tensor_tensor(WLO[k][:, :], RAW[:, k, :], WHI[k][:, :].bitcast(F32), ALU.subtract).then_inc(s_lo, 1)

            def los(stage, evacuate=None):
                with dve.Fori(0, COUNT[stage] // 2 - 1) as i:
                    lo(stage, i, 1)
                    if evacuate:
                        evacuate(2 * i, 0)
                    lo(stage, i + 1, 0)
                    if evacuate:
                        evacuate(2 * i + 1, 1)
                i = COUNT[stage] // 2 - 1
                lo(stage, i, 1)
                if evacuate:
                    evacuate(2 * i, 0)
                lo(NEXT[stage], 0, 0)
                if evacuate:
                    evacuate(2 * i + 1, 1)

            def add_gated(k, bank, l, gate, sem_, also=None):
                xk = xT[:, bass.ds(k, 1), :].rearrange("p a t -> p (a t)")
                for t0, m, cnd in SEGS:
                    g = MODT[:, l, bass.ds(gate + k, 1), cnd:cnd + 1].rearrange("p a b -> p (a b)")
                    ins = V.scalar_tensor_tensor(out=xk[:, t0:t0 + m], in0=PS[:, bank, t0:t0 + m], scalar=g,
                                                 in1=xk[:, t0:t0 + m], op0=ALU.mult, op1=ALU.add)
                ins.then_inc(sem_, 1)

            def to_residual(stage, l):
                def evacuate(u, k):
                    dve.wait_ge(s_unit, UNIT0[stage] + u + 3)
                    add_gated(u, k, l, 16, s_ev)
                return evacuate

            modulation(0)
            lo("q", 0, 0)
            norm(0)
            los("q")
            los("kvp")

            mpe.wait(dve, "hm")
            own.do(V.tensor_scalar(VAR[:, :, :], PS[:, 2:7, 0:T], EPS, None, ALU.add))
            mdve.mark("rc", V.reciprocal(QN[:, :, :], VAR[:, :, :]))
            mact.wait(dve, "root")
            rsqrt_step(ZS[:, :, :], VAR[:, :, :], QN[:, :, :])
            V.scalar_tensor_tensor(out=QN[:, 0:4, :], in0=Z[:, 0:4, :], scalar=VT[:, R_QG:R_QG + 1],
                                   in1=ZS[:, 0:4, :], op0=ALU.mult, op1=ALU.mult)
            mdve.mark("qn", V.scalar_tensor_tensor(out=QN[:, 4, :], in0=Z[:, 4, :], scalar=VT[:, R_KG:R_KG + 1],
                                                   in1=ZS[:, 4, :], op0=ALU.mult, op1=ALU.mult))
            mdve.wait(dve, "qn")
            mpe.wait(dve, "rot")
            dve.wait_ge(s_att, 16 * 6)
            own.mark(V.tensor_tensor(RQ[:, :, :], QN[:, 0:4, NPROMPT:T], COS.unsqueeze(1).to_broadcast([P, 4, NSAMPLE]), ALU.mult))
            own.mark(V.tensor_tensor(KALL[:, 0:NSAMPLE], QN[:, 4, NPROMPT:T], COS, ALU.mult))
            own.mark(V.tensor_tensor(VAR[:, :, 0:NSAMPLE], PS[:, 2:7, 0:NSAMPLE],
                                     SIN.unsqueeze(1).to_broadcast([P, 5, NSAMPLE]), ALU.mult))
            own.wait()
            own.mark(V.tensor_tensor(RQ[:, :, :], RQ[:, :, :], VAR[:, 0:4, 0:NSAMPLE], ALU.add))
            mdve.mark("rope", V.tensor_tensor(KALL[:, 0:NSAMPLE], KALL[:, 0:NSAMPLE], VAR[:, 4, 0:NSAMPLE], ALU.add))
            mdve.wait(dve, "rope")
            for b, (qt, j) in enumerate(BATCHES):
                n = P if qt == 0 else T
                rows = slice(64 * j, 64 * j + 64)
                mpe.wait(dve, f"s{b}")
                own.do(V.tensor_reduce(MX, PS[:, 0:4, 0:n], AX.X, ALU.max))
                mdve.mark(f"nb{b}", V.tensor_scalar(NB, MX, -0.125, None, ALU.mult))
                mact.wait(dve, f"e{b}")
                own.do(V.reciprocal(RV, SM))
                mdve.mark(f"p{b}", V.tensor_tensor(PROB[b % 2][:, :, 0:n], PROB[b % 2][:, :, 0:n],
                                                   RV.unsqueeze(2).to_broadcast([P, 4, n]), ALU.mult))
                mact.wait(dve, f"oh{b}")
                mdve.mark(f"ol{b}", V.tensor_tensor(HL[rows, 0:4, qt * P:qt * P + P],
                                                    PS[rows, 4, :].rearrange("p (a b) -> p a b", a=4),
                                                    HH[rows, 0:4, qt * P:qt * P + P].bitcast(F32), ALU.subtract))
            for g in range(4):
                mact.wait(dve, f"ph{g}")
                mdve.mark(f"pl{g}", V.scalar_tensor_tensor(out=HL[:, 4 + g, :], in0=PS[:, g, 0:T],
                                                           scalar=VT[:, R_PS + g:R_PS + g + 1],
                                                           in1=HH[:, 4 + g, :].bitcast(F32), op0=ALU.mult, op1=ALU.subtract))
            los("a_out", to_residual("a_out", 0))
            dve.wait_ge(s_ev, 2 + 18)
            V.sem_inc(s_res, KC)

            for l in range(LAYERS):
                if l:
                    modulation(1)
                    norm(2)
                    own.mark(V.memset(UP, 0.0))

                    def evac(i, jj, what, k):
                        u = 6 * i + 3 * jj + what
                        j = 2 * i + jj
                        dve.wait_ge(s_unit, UNIT0["c_in"] + u + 3)
                        own.wait()
                        if what == 0:
                            own.mark(V.tensor_copy(GC, PS[:, k, 0:T]))
                            own.wait()
                            V.sem_inc(s_ev, 1)
                        elif what == 1:
                            own.mark(V.tensor_tensor(UP[:, 1:1 + NPROMPT], PS[:, k, 0:NPROMPT], GC[:, 0:NPROMPT], ALU.mult))
                            V.tensor_tensor(UP[:, 2 + NPROMPT:2 + T], PS[:, k, NPROMPT:T], GC[:, NPROMPT:T], ALU.mult).then_inc(s_ev, 1)
                            own.wait()
                            dve.wait_ge(s_ev, 2 + PROJ0["c_in"] + u + 1)
                            tap = [VT[:, bass.ds(R_CW + 8 * w + j, 1)] for w in range(3)]
                            own.do(V.tensor_scalar(YA[:, 0:T + 1], UP[:, 0:T + 1], tap[0], None, ALU.mult))
                            for w in (1, 2):
                                own.do(V.scalar_tensor_tensor(out=YA[:, 0:T + 1], in0=UP[:, w:w + T + 1], scalar=tap[w],
                                                              in1=YA[:, 0:T + 1], op0=ALU.mult, op1=ALU.add))
                        else:
                            cm = CM[:, bass.ds(j, 1), :].rearrange("p a t -> p (a t)")
                            own.mark(V.tensor_tensor(cm[:, 0:NPROMPT], PS[:, k, 0:NPROMPT], YA[:, 0:NPROMPT], ALU.mult))
                            V.tensor_tensor(cm[:, NPROMPT:T], PS[:, k, NPROMPT:T], YA[:, NPROMPT + 1:T + 1], ALU.mult).then_inc(s_ev, 1)

                    def conv_pair(i, last=False):
                        for q in range(6):
                            if q < 5:
                                k = (q + 1) % 2
                                lo("c_in", 3 * i + (q + 1) // 2, k)
                            elif not last:
                                lo("c_in", 3 * i + 3, 0)
                            else:
                                lo("c_out", 0, 0)
                            evac(i, q // 3, q % 3, q % 2)

                    with own.loop(3, 12) as i:
                        conv_pair(i)
                    conv_pair(3, last=True)
                    dve.wait_ge(s_ev, 2 + PROJ0["c_in"] + 24)
                    own.wait()
                    V.sem_inc(s_cm, KC)
                    for k in range(0, KC, 2):
                        dve.wait_ge(s_hhi, 3 * KC + k // 2 + 1)
                        V.tensor_tensor(HL[:, k:k + 2, :], CM[:, k:k + 2, :], HH[:, k:k + 2, :].bitcast(F32), ALU.subtract)\
                            .then_inc(s_hlo, 1)
                    los("c_out", to_residual("c_out", 1))
                    dve.wait_ge(s_ev, 2 + PROJ0["c_out"] + 8)
                    V.sem_inc(s_res, KC)
                norm(2 * l + 1)
                los(f"wq{l}")

                def top16(vals, idx, src, rest, rows):
                    for u in range(rows):
                        ins = V.max(vals[:, u, 0:8], src[:, u, :])
                    own.do(ins)
                    for u in range(rows):
                        V.max_index(idx[:, u, 0:8], vals[:, u, 0:8], src[:, u, :])
                        ins = V.match_replace(rest[:, u, :], vals[:, u, 0:8], src[:, u, :], NEG)
                    own.do(ins)
                    for u in range(rows):
                        ins = V.max(vals[:, u, 8:16], rest[:, u, :])
                    own.do(ins)
                    for u in range(rows):
                        ins = V.max_index(idx[:, u, 8:16], vals[:, u, 8:16], rest[:, u, :])
                    return ins

                def pick_tail(g, cols):
                    dve.wait_ge(s_pte, g + 1)
                    bank = PS[:, 0, 2 * P:3 * P]
                    own.do(V.tensor_copy(GB[:, :], bank))
                    own.do(V.tensor_copy(GP[:, 0, cols], GB[:, :]))
                    own.do(V.tensor_tensor(GRES, bank, GP[:, 0, cols], ALU.subtract))
                    own.do(V.tensor_copy(GB[:, :], GRES))
                    own.do(V.tensor_copy(GP[:, 1, cols], GB[:, :]))
                    V.tensor_tensor(GP[:, 2, cols], GRES, GP[:, 1, cols], ALU.subtract).then_inc(s_pts, 1)
                    dve.wait_ge(s_pts, g + 1)

                for tile in range(TT):
                    g = TT * l + tile
                    dve.wait_ge(s_scc, g + 1)
                    top16(V16, I16U, SC, SC2, 16).then_inc(s_l1, 1)
                    dve.wait_ge(s_l1, g + 1)
                    if tile:
                        pick_tail(g - 1, slice((tile - 1) * P, tile * P))
                    own.mark(V.tensor_copy(I16F[:, :, :], I16U[:, :, :]))
                    side = V16.rearrange("p (h s) k -> p h s k", s=2)
                    for a in range(TOPK):
                        ins = V.tensor_tensor(CA[:, :, a * TOPK:(a + 1) * TOPK],
                                              side[:, :, 1, :], side[:, :, 0, a:a + 1].to_broadcast([P, HEADS, TOPK]), ALU.add)
                    own.do(ins)
                    own.do(top16(V2, FIU, CA, CA2, HEADS))
                    fi = FIU[:, :, :].rearrange("p a b -> p (a b)")
                    own.mark(V.tensor_scalar(FAU[:, :], fi, 4, None, ALU.logical_shift_right))
                    own.mark(V.tensor_scalar(FBU[:, :], fi, TOPK - 1, None, ALU.bitwise_and))
                    V.tensor_tensor(EX[:, :, :], V2[:, :, :], V2[:, :, 0:1].to_broadcast([P, HEADS, TOPK]), ALU.subtract)\
                        .then_inc(s_d, 1)
                    own.wait()
                    own.mark(V.tensor_copy(FA, FAU[:, :]))
                    own.do(V.tensor_copy(FB, FBU[:, :]))
                    iota16 = IOTA[:, 0:TOPK].unsqueeze(1).to_broadcast([P, PICKS, TOPK])
                    own.mark(V.tensor_tensor(EQ[:, :, :], FA.unsqueeze(2).to_broadcast([P, PICKS, TOPK]), iota16, ALU.is_equal))
                    own.do(V.tensor_tensor(EQ2[:, :, :], FB.unsqueeze(2).to_broadcast([P, PICKS, TOPK]), iota16, ALU.is_equal))
                    keys = I16F.rearrange("p (h s) k -> p h s k", s=2)
                    for eq, s in ((EQ, 0), (EQ2, 1)):
                        for h in range(HEADS):
                            e = eq[:, h * TOPK:(h + 1) * TOPK, :]
                            ins = V.tensor_tensor(e, e, keys[:, h, s:s + 1, :].to_broadcast([P, TOPK, TOPK]), ALU.mult)
                    own.do(ins)
                    own.mark(V.tensor_reduce(ID1, EQ[:, :, :], AX.X, ALU.add))
                    own.mark(V.tensor_reduce(ID2, EQ2[:, :, :], AX.X, ALU.add))
                    dve.wait_ge(s_e, g + 1)
                    own.do(V.tensor_reduce(ZSUM, EX[:, :, :], AX.X, ALU.add))
                    own.do(V.reciprocal(ZINV, ZSUM))
                    V.tensor_tensor(GT[:, :, :], EX[:, :, :], ZINV.unsqueeze(2).to_broadcast([P, HEADS, TOPK]), ALU.mult)\
                        .then_inc(s_pick, 1)
                pick_tail(TT * l + 2, slice(2 * P, 3 * P))

                for tile in range(TT):
                    g0 = 32 * (TT * l + tile)
                    with dve.Fori(0, 8) as i:
                        for k in range(4):
                            dve.wait_ge(s_gm, g0 + 4 * i + k + 1)
                            for q in range(4):
                                tok = bass.ds(tile * P + 16 * i + 4 * k + q, 1)
                                slot = 4 * (k % 2) + q
                                V.tensor_scalar(OH2[:, slot, :], IOTAB[:, :], IT2[:, tok], None, ALU.is_equal)
                                for part in range(3):
                                    ins = V.tensor_scalar(OH1[:, slot, part, :], IOTAB[:, :], IT1[:, tok],
                                                          GP[:, part, tok], ALU.is_equal, ALU.mult)
                            ins.then_inc(s_oh, 1)

                def u_lo(t, k, half):
                    g = P * l + t
                    dve.wait_ge(s_uhi, 2 * g + half + 1)
                    c0 = slice(512 * half, 512 * half + 512)
                    V.tensor_tensor(ULO[k][:, c0], PS[:, 1, :], UHI[k][:, c0].bitcast(F32), ALU.subtract).then_inc(s_ulo, 1)

                def weigh(t, k, pair):
                    g = P * l + t
                    dve.wait_ge(s_gel, g + 2)
                    dve.wait_ge(g_in[k], 16 * (64 * l + pair + 1))
                    V.tensor_tensor(GEL[:, k, :], GEL[:, k, :], GIN[:, k, :], ALU.mult).then_inc(s_w, 1)

                def w_lo(t, k):
                    dve.wait_ge(s_whi, P * l + t + 1)
                    V.tensor_tensor(ELO[k][:, :], GEL[:, k, :], EHI[k][:, :].bitcast(F32), ALU.subtract).then_inc(s_wlo, 1)

                def body(t, k, pair, last=False):
                    if not last:
                        u_lo(t + 1, 1 - k, 0)
                    weigh(t, k, pair)
                    if not last:
                        u_lo(t + 1, 1 - k, 1)
                    w_lo(t, k)

                v = f"v{l}"
                u_lo(0, 0, 0)
                u_lo(0, 0, 1)
                body(0, 0, 0)
                lo(v, 0, 1)
                with dve.Fori(0, P // 2 - 1) as i:
                    body(2 * i + 1, 1, i)
                    lo(v, i + 1, 0)
                    body(2 * i + 2, 0, i + 1)
                    lo(v, i + 1, 1)
                body(P - 1, 1, P // 2 - 1, last=True)
                if l == 0:
                    lo("c_in", 0, 0)
                for k in range(KC):
                    dve.wait_ge(s_at, KC * l + k + 1)
                    add_gated(k, k % 2, l, 40, s_res)
            norm(4)


def _tail(act, nc, g, tile, EX, s_d, s_e, s_ptr, s_pte, PS, IT1, IT2):
    act.wait_ge(s_d, g + 1)
    nc.scalar.activation(EX[:, :, :], EX[:, :, :], ACT.Exp).then_inc(s_e, 1)
    act.wait_ge(s_ptr, g + 1)
    cols = slice(tile * P, tile * P + P)
    nc.scalar.activation(IT1[:, cols], PS[:, 0, 0:P], ACT.Copy)
    nc.scalar.activation(IT2[:, cols], PS[:, 0, P:2 * P], ACT.Copy).then_inc(s_pte, 1)


_INS = ["x_prompt", "x_sample", "cache_k", "cache_v", "c", "c_ctx", "mod_w", "mod_b", "norm1_g", "norm2_g",
        "a_in_w", "a_out_w", "q_norm_g", "k_norm_g", "pool_w", "pool_scale", "c_in_w", "c_conv_w", "c_out_w",
        "peer_wq", "peer_subkeys", "peer_u", "peer_v", "final_g"]
_OUTS = [(1, 128, 1024), (1, 256, 1024), (1, 1, 128, 2, 64), (1, 1, 128, 2, 64)]


def _tables():
    import numpy as np

    f = np.float32
    ident = np.eye(128, dtype=f)
    headmean = np.kron(np.eye(2), np.ones((64, 64)) / 64).astype(f)
    rot = np.zeros((128, 128), f)
    for m in range(128):
        if m % 32 < 16:
            rot[m + 16, m] = -1
        else:
            rot[m - 16, m] = 1
    inv = f(10000.0) ** (-np.arange(16, dtype=f) / f(16))
    tok = np.arange(256)
    d = np.arange(128) % 64
    pos = np.where((d < 32)[:, None], (tok // 64)[None, :], (tok % 64)[None, :]).astype(f)
    ang = pos * inv[d % 16][:, None]
    rcnt = np.zeros((4, 384), f)
    for g, win in enumerate((2, 4, 8, 16)):
        for t0, n in ((0, 128), (128, 256)):
            t = np.arange(n)
            cnt = np.clip(t + win - win // 2, 0, n) - np.clip(t - win // 2, 0, n)
            rcnt[g, t0:t0 + n] = 1.0 / cnt
    rcnt = np.ascontiguousarray(np.broadcast_to(rcnt, (128, 4, 384)))
    iota = np.ascontiguousarray(np.broadcast_to(np.arange(128, dtype=f), (128, 128)))
    return {"k_ident": ident, "k_headmean": headmean, "k_rot": rot, "k_cos": np.cos(ang).astype(f),
            "k_sin": np.sin(ang).astype(f), "k_rcnt": rcnt, "k_iota": iota}


def kernel(**inputs):
    import numpy as _np
    import concourse.bacc as _bacc
    from concourse import mybir as _mybir
    from concourse.bass_utils import run_bass_kernel_spmd as _run

    nc = _bacc.Bacc("TRN2", target_bir_lowering=False, num_devices=1)
    arrays, args = {}, {}
    for name, a in [(n, inputs[n]) for n in _INS] + list(_tables().items()):
        a = _np.ascontiguousarray(a)
        arrays[f"in_{name}_dram"] = a
        args[name] = nc.dram_tensor(f"in_{name}_dram", a.shape, _mybir.dt.from_np(a.dtype), kind="ExternalInput").ap()
    for i, (name, shape) in enumerate(zip(("y_prompt", "y_sample", "new_k", "new_v"), _OUTS)):
        args[name] = nc.dram_tensor(f"out_{i}_dram", shape, F32, kind="ExternalOutput").ap()
    build_step(nc, **args)
    r = _run(nc, [arrays], core_ids=[0])
    return tuple(r.results[0][f"out_{i}_dram"] for i in range(len(_OUTS)))
```

```python
import concourse.bass as bass
from concourse import mybir
from contextlib import ExitStack, contextmanager

F32 = mybir.dt.float32
F32R = mybir.dt.float32r
BF16 = mybir.dt.bfloat16
U32 = mybir.dt.uint32
ALU = mybir.AluOpType
ACT = mybir.ActivationFunctionType
AX = mybir.AxisListType

P = 128
D = 1024
KC = D // P
NPROMPT, NSAMPLE = 128, 256
T = NPROMPT + NSAMPLE
TT = T // P
SEGS = ((0, NPROMPT, 0), (NPROMPT, NSAMPLE, 1))
LAYERS = 2
EPS = 1e-6
HEADS, TOPK, NK = 8, 16, 128
PICKS = HEADS * TOPK
NEG = -3.0e38
WINDOWS = (2, 4, 8, 16)

R_QG, R_KG, R_PS, R_CW = 0, 1, 2, 6
VROWS = 30
R_N1, R_N2, R_FIN, R_CTX, R_C = 30, 46, 62, 70, 78
VCOLS = 86

STAGES = (("q", 4, 2), ("kvp", 6, 1), ("a_out", 8, 2), ("wq0", 16, 1), ("v0", 128, 1),
          ("c_in", 24, 1), ("c_out", 8, 1), ("wq1", 16, 1), ("v1", 128, 1))
UNIT0, FILLED0, PROJ0, DMAS = {}, {}, {}, {}
_u = _f = _p = 0
for _name, _n, _d in STAGES:
    UNIT0[_name], FILLED0[_name], PROJ0[_name], DMAS[_name] = _u, _f, _p, 16 * _d
    _u += _n
    _f += 16 * _d * _n // 2
    _p += 0 if _name in ("v0", "v1", "a_out", "c_out") else _n
NEXT = {a[0]: b[0] for a, b in zip(STAGES, STAGES[1:])}
COUNT = {s[0]: s[1] for s in STAGES}

MODB = 256
SEGB = D // MODB
MODSEGS = 6

S_LEVEL1, S_LEVEL2 = 6, 12
BATCH = 8
TURNS = P // (2 * BATCH)
S_STORE = 8
S_REST = P - TT * (S_LEVEL1 + S_LEVEL2) - TT * 2 * TURNS - (TT - 1) * S_STORE


class Steps:

    def __init__(self, eng, sem):
        self.eng, self.sem, self.n, self.extra = eng, sem, 0, 0

    def mark(self, ins):
        ins.then_inc(self.sem, 1)
        self.n += 1

    def wait(self):
        self.eng.wait_ge(self.sem, self.extra + self.n)

    def do(self, ins):
        self.mark(ins)
        self.wait()

    @contextmanager
    def loop(self, turns, per):
        n0 = self.n
        with self.eng.Fori(0, turns) as i:
            self.extra = i * per
            yield i
            self.extra = 0
        assert self.n - n0 == per, (self.n - n0, per)
        self.n = n0 + turns * per


class Marks:

    def __init__(self, sem, names):
        self.sem, self.names, self.at = sem, names, 0

    def mark(self, name, ins):
        assert self.names[self.at] == name, (self.names[self.at], name)
        self.at += 1
        ins.then_inc(self.sem, 1)

    def wait(self, eng, name):
        eng.wait_ge(self.sem, self.names.index(name) + 1)


def build_step(nc, x_prompt, x_sample, cache_k, cache_v, c, c_ctx, mod_w, mod_b, norm1_g, norm2_g,
               a_in_w, a_out_w, q_norm_g, k_norm_g, pool_w, pool_scale, c_in_w, c_conv_w, c_out_w,
               peer_wq, peer_subkeys, peer_u, peer_v, final_g,
               k_ident, k_headmean, k_rot, k_cos, k_sin, k_rcnt, k_iota,
               y_prompt, y_sample, new_k, new_v):
    ctx = ExitStack()
    with ctx:
        def sb(name, shape, dt=F32):
            return ctx.enter_context(nc.sbuf_tensor(name, shape, dt))

        def sem(name):
            return ctx.enter_context(nc.semaphore(name))

        xT = sb("xT", [P, KC, T])
        HH = sb("HH", [P, KC, T], F32R)
        HL = sb("HL", [P, KC, T], F32R)
        RAW = sb("RAW", [P, 2, D])
        WHI = [sb(f"WHI{i}", [P, D], F32R) for i in range(2)]
        WLO = [sb(f"WLO{i}", [P, D], F32R) for i in range(2)]
        URAW = sb("URAW", [P, 2, 4, D // 4])
        UT = sb("UT", [P, 2, D])
        UHI = [sb(f"UHI{i}", [P, D], F32R) for i in range(2)]
        ULO = [sb(f"ULO{i}", [P, D], F32R) for i in range(2)]
        GIN = sb("GIN", [P, 2, T])
        GEL = sb("GEL", [P, 2, T])
        EHI = [sb(f"EHI{i}", [P, T], F32R) for i in range(2)]
        ELO = [sb(f"ELO{i}", [P, T], F32R) for i in range(2)]
        VR = sb("VR", [P, P])
        VT = sb("VT", [P, VCOLS])
        MBT = sb("MBT", [P, LAYERS * 48])
        COND = sb("COND", [P, KC, 2])
        MODR = sb("MODR", [P, 2, KC, MODB])
        MROW = sb("MROW", [2, D])
        MODT = sb("MODT", [P, LAYERS, 48, 2])
        GS = sb("GS", [P, LAYERS, 2, KC, 2])
        IDENT = sb("IDENT", [P, P])
        MEAN1 = sb("MEAN1", [P, P])
        HMEAN = sb("HMEAN", [P, P])
        ROT = sb("ROT", [P, P])
        IOTA = sb("IOTA", [P, P])
        IOTA8 = sb("IOTA8", [P, P, BATCH], BF16)
        EQ1 = sb("EQ1", [P, P, BATCH], BF16)
        SKR = sb("SKR", [P, 4, P])
        SKT = sb("SKT", [P, 4, P])
        I16U = sb("I16U", [P, 16, TOPK], U32)
        FIU = sb("FIU", [P, HEADS, TOPK], U32)
        FAU = sb("FAU", [P, PICKS], U32)
        FBU = sb("FBU", [P, PICKS], U32)
        IT1 = sb("IT1", [P, T], BF16)
        IT2 = sb("IT2", [P, T], BF16)
        GP = sb("GP", [P, 3, T], BF16)
        AR = sb("AR", [P, P * P])

        def ar(at, *dims):
            n = 1
            for d in dims:
                n *= d
            v = AR[:, at:at + n]
            if len(dims) == 2:
                v = v.rearrange("p (a b) -> p a b", a=dims[0])
            if len(dims) == 3:
                v = v.rearrange("p (a b c) -> p a b c", a=dims[0], b=dims[1])
            return v

        XS = ar(0, TT, D)
        Z = ar(0, 10, T)
        QN = ar(3840, 5, T)
        ZS = ar(5760, 5, T)
        VAR = ar(7680, 5, T)
        RQ = ar(9600, 4, NSAMPLE)
        COS, SIN = ar(10880, NSAMPLE), ar(11136, NSAMPLE)
        RCNT = ar(11392, 4, T)
        KALL = ar(12928, T)
        VTOK = ar(13312, 3, P)
        VPAST = ar(13696, P)
        KTOK = ar(13824, P)
        KPAST = ar(13952, P)
        PADW = 432
        XPAD, SUM0, SUM1 = ar(14080, PADW), ar(14512, PADW), ar(14944, PADW)
        MX, NB, SM, RV = ar(15376, 4), ar(15380, 4), ar(15384, 4), ar(15388, 4)
        PW = ar(15392, 4, P)
        PROB = [ar(5760, 4, T), ar(7680, 4, T)]
        PROBT = ar(0, 4, T)
        NB0 = 13312
        SQ = ar(NB0, 2, T)
        MV, RC, RT, NT = (ar(NB0 + (2 + i) * T, T) for i in range(4))
        T1 = ar(NB0 + 6 * T, 2, T)
        QT = ar(0, 16, T)
        SC = ar(6144, 16, NK)
        SC2 = ar(8192, 16, NK)
        V16 = ar(10240, 16, TOPK)
        I16F = ar(10496, 16, TOPK)
        CA = ar(10752, HEADS, 256)
        CA2 = ar(12800, HEADS, 256)
        V2 = ar(14848, HEADS, TOPK)
        FA, FB = ar(14976, PICKS), ar(15104, PICKS)
        ID1, ID2 = ar(15232, PICKS), ar(15360, PICKS)
        EX = ar(15488, HEADS, TOPK)
        GT = ar(15616, HEADS, TOPK)
        ZSUM, ZINV = ar(15744, HEADS), ar(15752, HEADS)
        GRES = ar(15760, P)
        EQ = ar(8192, PICKS, TOPK)
        EQ2 = ar(12800, PICKS, TOPK)
        STAGE = ar(0, P, P)
        CM = ar(0, KC, T)
        GC = ar(3072, T)
        UP = ar(3456, 388)
        YA = ar(3844, 386)
        YT = ar(3072, KC, T)
        YTOK = ar(6144, TT, D)

        PS = ctx.enter_context(nc.psum_tensor("PS", [P, 8, 512], F32))
        GD = nc.dram_tensor("gates_dram", [LAYERS, P, P, T], F32, kind="Internal").ap()

        SD = nc.dram_tensor("gelu_dram", [LAYERS, P, P, T], F32, kind="Internal").ap()

        OH = MODR[:, :, :, :].rearrange("p a b c -> p (a b c)").bitcast(BF16)
        n1 = P * BATCH
        OH2 = [OH[:, k * n1:(k + 1) * n1].rearrange("p (a b) -> p a b", b=BATCH) for k in range(2)]
        OH1 = [[OH[:, (2 + 3 * k + part) * n1:(3 + 3 * k + part) * n1].rearrange("p (a b) -> p a b", b=BATCH)
                for part in range(3)] for k in range(2)]

        s_vec, s_cst, s_x = sem("s_vec"), sem("s_cst"), sem("s_x")
        s_att = sem("s_att")
        s_init = sem("s_init")
        s_vt = sem("s_vt")
        s_act0 = sem("s_act0")
        s_xt, s_xe = sem("s_xt"), sem("s_xe")
        mod_in = [sem(f"mod_in{i}") for i in range(2)]
        s_mrow = sem("s_mrow")
        s_mev = sem("s_mev")
        s_mtr = sem("s_mtr")
        s_mod = sem("s_mod")
        s_gs = sem("s_gs")
        s_sq, s_ss = sem("s_sq"), sem("s_ss")
        s_rc, s_rt = sem("s_rc"), sem("s_rt")
        s_t1 = sem("s_t1")
        s_hhi, s_hlo = sem("s_hhi"), sem("s_hlo")
        raw_in = [sem(f"raw_in{i}") for i in range(2)]
        s_hi = sem("s_hi")
        s_lo = sem("s_lo")
        s_unit = sem("s_unit")
        s_ev = sem("s_ev")
        s_res = sem("s_res")
        s_pool = sem("s_pool")
        s_pm = sem("s_pm")
        s_dve, s_acts = sem("s_dve"), sem("s_acts")
        s_nkv = sem("s_nkv")
        s_sc, s_scc = sem("s_sc"), sem("s_scc")
        s_l1 = sem("s_l1")
        s_d, s_e = sem("s_d"), sem("s_e")
        s_pick = sem("s_pick")
        s_ptr, s_pte = sem("s_ptr"), sem("s_pte")
        s_pts = sem("s_pts")
        s_oh = sem("s_oh")
        s_gm = sem("s_gm")
        s_gev = sem("s_gev")
        s_gst = sem("s_gst")
        u_in = [sem(f"u_in{i}") for i in range(2)]
        s_tr = sem("s_tr")
        s_uhi = sem("s_uhi")
        s_ulo = sem("s_ulo")
        s_S = sem("s_S")
        s_gel = sem("s_gel")
        s_sst = [sem(f"s_sst{i}") for i in range(2)]
        g_in = [sem(f"g_in{i}") for i in range(2)]
        s_w = sem("s_w")
        s_whi = sem("s_whi")
        s_wlo = sem("s_wlo")
        s_acc = sem("s_acc")
        s_at = sem("s_at")
        s_cm = sem("s_cm")
        s_yt, s_ytr, s_ye = sem("s_yt"), sem("s_ytr"), sem("s_ye")
        s_out = sem("s_out")
        s_free = sem("s_free")
        s_mpe, s_mact, s_mdve = sem("s_mpe"), sem("s_mact"), sem("s_mdve")

        BATCHES = [(qt, j) for qt in range(TT) for j in range(2)]
        NBT = len(BATCHES)
        pe_names = ["hm", "kv", "ktok", "rot", "s0"]
        for b in range(NBT):
            pe_names += ([f"s{b + 1}"] if b + 1 < NBT else []) + [f"t{b}", f"o{b}"]
        pe_names += [f"pw{g}" for g in range(4)]
        act_names = ["zsq", "root", "kpast", "vtok", "ktok"]
        for b in range(NBT):
            act_names += [f"e{b}", f"pt{b}", f"oh{b}"]
        act_names += [f"ph{g}" for g in range(4)]
        dve_names = ["rc", "qn", "rope"]
        for b in range(NBT):
            dve_names += [f"nb{b}", f"p{b}", f"ol{b}"]
        dve_names += [f"pl{g}" for g in range(4)]
        mpe, mact, mdve = Marks(s_mpe, pe_names), Marks(s_mact, act_names), Marks(s_mdve, dve_names)

        def chunk_view(x):
            return x.rearrange("p (m c) -> p c m", c=KC)

        block = ctx.enter_context(nc.Block())

        def s_tiles(eng, first, count, step):
            with eng.Fori(first // 2, (first + count) // 2) as i:
                step(i, 0)
                step(i, 1)

        NORM_BANK = (2, 0, 2, 0, 2)

        def filled(stage, pair):
            return FILLED0[stage] + DMAS[stage] * (pair + 1)

        @block.sync
        def _(sp):
            def slot_free(sem_, value):
                sp.wait_ge(sem_, value)
                sp.sem_inc(s_free, 1)

            cols = [(R_N1, norm1_g.rearrange("l (p k) -> p l k", k=KC)),
                    (R_N2, norm2_g.rearrange("l (p k) -> p l k", k=KC)),
                    (R_FIN, final_g.rearrange("(a p k) -> p a k", a=1, k=KC)),
                    (R_CTX, c_ctx.rearrange("(a p k) -> p a k", a=1, k=KC)),
                    (R_C, c.rearrange("a (p k) -> p a k", k=KC))]
            for at, src in cols:
                n = KC * src.shape[1]
                sp.dma_start(VT[:, at:at + n].rearrange("p (l k) -> p l k", k=KC), src).then_inc(s_vec, 16)
            rows = [(R_PS, pool_scale.rearrange("l (k p) -> (l k) p", p=P)),
                    (R_CW, c_conv_w.rearrange("l w (k p) -> (l w k) p", p=P))]
            for at, src in rows:
                sp.dma_start(VR[at:at + src.shape[0], :], src).then_inc(s_vec, 16)
            for at, src in ((R_QG, q_norm_g), (R_KG, k_norm_g)):
                for j in range(2):
                    sp.dma_start(VR[at:at + 1, 64 * j:64 * j + 64], src).then_inc(s_vec, 16)
            sp.dma_start(MBT[:, :].rearrange("p (s k) -> p s k", k=KC), mod_b.rearrange("l (s p k) -> p (l s) k", s=6, k=KC))\
                .then_inc(s_vec, 16)
            sp.dma_start(IDENT[:, :], k_ident).then_inc(s_vec, 16)

            def load_mod(l, b, k):
                sp.dma_start(MODR[:, k, :, :], mod_w[l, :, bass.ds(b * MODB, MODB)]
                             .rearrange("(p k) m -> p k m", k=KC)).then_inc(mod_in[k], 16)

            for k in range(2):
                load_mod(0, k, k)
            sp.dma_start(XS[:, 0, :], x_prompt[0, :, :]).then_inc(s_x, 16)
            sp.dma_start(XS[:, 1:3, :], x_sample[0, :, :].rearrange("(t p) d -> p t d", p=P)).then_inc(s_x, 16)
            sp.dma_start(HMEAN[:, :], k_headmean).then_inc(s_cst, 16)
            sp.dma_start(ROT[:, :], k_rot).then_inc(s_cst, 16)
            sp.dma_start(IOTA[:, :], k_iota).then_inc(s_cst, 16)
            sp.dma_start(SKR[:, :, :], peer_subkeys.rearrange("l s e k -> e (l s) k")).then_inc(s_cst, 16)
            with sp.Fori(1, MODSEGS * SEGB // 2) as i:
                for k in range(2):
                    slot_free(s_mrow, 2 * i - 1 + k)
                    load_mod(0, 2 * i + k, k)

            def unit_free(n):
                slot_free(s_lo, n + 1)

            w_in = a_in_w[0, :, :]
            for u in range(COUNT["q"]):
                n = UNIT0["q"] + u
                unit_free(n)
                dst = RAW[:, n % 2, :].rearrange("p (k m) -> p k m", k=KC)
                for j in range(2):
                    h0 = 64 * (4 * j + u)
                    sp.dma_start(dst[:, :, 64 * j:64 * j + 64],
                                 w_in[:, h0:h0 + 64].rearrange("(p k) m -> p k m", k=KC)).then_inc(raw_in[n % 2], 16)

            def load_units(stage, w, m0, first=0):
                with sp.Fori(first // 2, COUNT[stage] // 2) as i:
                    for k in range(2):
                        unit_free(UNIT0[stage] + 2 * i + k)
                        sp.dma_start(RAW[:, k, :].rearrange("p (k m) -> p k m", k=KC),
                                     w[:, bass.ds(m0 + (2 * i + k) * P, P)].rearrange("(p k) m -> p k m", k=KC))\
                            .then_inc(raw_in[k], 16)

            load_units("kvp", w_in, 512)
            sp.wait_ge(s_gev, 3)
            sp.wait_ge(s_xe, KC)
            sp.dma_start(COS, k_cos).then_inc(s_att, 16)
            sp.dma_start(SIN, k_sin).then_inc(s_att, 16)
            sp.dma_start(RCNT, k_rcnt).then_inc(s_att, 16)
            sp.wait_ge(s_hlo, KC)
            sp.dma_start(VPAST, cache_v[0, 0, :, :, :].rearrange("s h d -> s (h d)")).then_inc(s_att, 16)
            sp.dma_start(KPAST, cache_k[0, 0, :, :, :].rearrange("s h d -> s (h d)")).then_inc(s_att, 16)
            sp.dma_start(PW, pool_w[0, :, :, :].rearrange("g c d -> c g d")).then_inc(s_att, 16)
            w_o = a_out_w[0, :, :]
            for u in range(KC):
                unit_free(UNIT0["a_out"] + u)
                for j in range(2):
                    r = 64 * u + 256 * j if u < 4 else 128 * u + 64 * j
                    sp.dma_start(RAW[64 * j:64 * j + 64, u % 2, :], w_o[r:r + 64, :]).then_inc(raw_in[u % 2], 16)

            def load_u(l, t, k):
                for a in range(4):
                    sp.dma_start(URAW[32 * a:32 * a + 32, k, :, :],
                                 peer_u[l, bass.ds(t * P, P), 256 * a:256 * a + 256].rearrange("(b e) m -> e b m", e=32))\
                        .then_inc(u_in[k], 16)

            def load_v(l, t, k):
                unit_free(UNIT0[f"v{l}"] + t)
                sp.dma_start(RAW[:, k, :], peer_v[l, bass.ds(t * P, P), :]).then_inc(raw_in[k], 16)

            def load_gs(l, t, k):
                for dst, src in ((GIN, GD), (GEL, SD)):
                    sp.dma_start(dst[:, k, :], src[l, bass.ds(t, 1), :, :].rearrange("a p t -> p (a t)")).then_inc(g_in[k], 16)

            def s_step(l, load=True):
                def step(i, k):
                    if load:
                        slot_free(s_tr, P * l + 2 * i + k + 1)
                        load_u(l, 2 * i + k + 2, k)
                    slot_free(s_gel, P * l + 2 * i + k + 1)
                    sp.dma_start(SD[l, bass.ds(2 * i + k - 2, 1), :, :].rearrange("a p t -> p (a t)"), GEL[:, k, :])\
                        .then_inc(s_sst[k], 16)
                return step

            sp.sem_inc(s_sst[0], 16)
            sp.sem_inc(s_sst[1], 16)
            for l in range(LAYERS):
                if l:
                    wc = c_in_w[0, :, :]
                    with sp.Fori(0, 4) as i:
                        for q in range(6):
                            unit_free(UNIT0["c_in"] + 6 * i + q)
                            part = (1, 2, 0)[q % 3]
                            sp.dma_start(RAW[:, q % 2, :].rearrange("p (k m) -> p k m", k=KC),
                                         wc[:, bass.ds(part * D + (2 * i + q // 3) * P, P)]
                                         .rearrange("(p k) m -> p k m", k=KC)).then_inc(raw_in[q % 2], 16)
                    with sp.Fori(0, KC // 2) as i:
                        for k in range(2):
                            unit_free(UNIT0["c_out"] + 2 * i + k)
                            sp.dma_start(RAW[:, k, :], c_out_w[0, bass.ds((2 * i + k) * P, P), :]).then_inc(raw_in[k], 16)
                load_units(f"wq{l}", peer_wq[l, :, :], 0)
                for k in range(2):
                    if l:
                        sp.wait_ge(s_tr, P)
                    load_u(l, k, k)
                for k in range(2):
                    load_v(l, k, k)
                if l == 0:
                    for k in range(2):
                        sp.wait_ge(s_mrow, MODSEGS * SEGB - 1 + k)
                        load_mod(1, k, k)
                for k in range(2):
                    sp.wait_ge(s_tr, P * l + k + 1)
                    load_u(l, k + 2, k)
                at = 0
                for tile in range(TT):
                    n = S_LEVEL1 + S_LEVEL2
                    skip = 0 if tile else 2
                    s_tiles(sp, at + skip, n - skip, s_step(l))
                    at += n
                    if l == 0:
                        pairs = MODSEGS * SEGB // 2
                        part = pairs // TT
                        with sp.Fori(tile * part + 1, min((tile + 1) * part + 1, pairs)) as i:
                            for k in range(2):
                                slot_free(s_mrow, 2 * pairs + 2 * i - 1 + k)
                                load_mod(1, 2 * i + k, k)
                for tile in range(TT):
                    s_tiles(sp, at, 2 * TURNS, s_step(l))
                    at += 2 * TURNS
                    sp.wait_ge(s_gev, 4 + 32 * (TT * l + tile + 1))
                    sp.dma_start(GD[l, :, :, tile * P:(tile + 1) * P].rearrange("i p t -> p i t"), STAGE)\
                        .then_inc(s_gst, 16)
                    if tile + 1 < TT:
                        s_tiles(sp, at, S_STORE, s_step(l))
                        at += S_STORE
                s_tiles(sp, at, S_REST - 2, s_step(l))
                for i in (P // 2 - 1, P // 2):
                    for k in range(2):
                        s_step(l, load=False)(i, k)
                sp.wait_ge(s_gst, 16 * TT * (l + 1))
                for k in range(2):
                    sp.wait_ge(s_sst[k], 16 * (P // 2 * (l + 1) + 1))
                for k in range(2):
                    load_gs(l, k, k)
                with sp.Fori(1, P // 2) as i:
                    for k in range(2):
                        t = 2 * i + k
                        slot_free(s_wlo, P * l + t - 1)
                        load_gs(l, t, k)
                        load_v(l, t, k)
            sp.wait_ge(s_ye, 6)
            sp.dma_start(y_prompt[0, :, :], YTOK[:, 0, :]).then_inc(s_out, 16)
            sp.dma_start(y_sample[0, :, :].rearrange("(t p) d -> p t d", p=P), YTOK[:, 1:3, :]).then_inc(s_out, 16)
            sp.wait_ge(s_nkv, 32)
            sp.wait_ge(s_out, 32)

        @block.gpsimd
        def _(pool):
            own = Steps(pool, s_pool)
            pool.memset(MEAN1[:, :], 1.0 / D).then_inc(s_cst, 16)
            pool.wait_ge(s_ev, 2 + 10)
            pool.wait_ge(s_att, 16 * 6)
            pool.wait_ge(s_hlo, KC)
            own.do(pool.memset(XPAD, 0.0))
            pads = ((8, 0, NPROMPT), (8 + NPROMPT + 16, NPROMPT, NSAMPLE))
            for g, win in enumerate(WINDOWS):
                zg = Z[:, 6 + g, :]
                for at, t0, n in pads:
                    own.mark(pool.tensor_copy(XPAD[:, at:at + n], zg[:, t0:t0 + n]))
                own.wait()
                src, bufs, half = XPAD, [SUM0, SUM1], 1
                while half < win:
                    dst = bufs[0]
                    bufs.reverse()
                    n = PADW - 2 * half + 1
                    own.do(pool.tensor_tensor(dst[:, 0:n], src[:, 0:n], src[:, half:half + n], ALU.add))
                    src, half = dst, 2 * half
                out = bufs[0]
                for at, t0, n in pads:
                    a = at - win // 2
                    own.mark(pool.tensor_tensor(out[:, t0:t0 + n], src[:, a:a + n], RCNT[:, g, t0:t0 + n], ALU.mult))
                own.wait()
                pool.tensor_tensor(zg, out[:, 0:T], zg, ALU.subtract).then_inc(s_pm, 1)
                pool.wait_ge(s_pm, g + 1)
            pool.sem_inc(s_ulo, 2)
            with pool.Fori(0, LAYERS * P // 2) as i:
                for k in range(2):
                    pool.wait_ge(s_uhi, 2 * i + k + 1)
                    pool.tensor_tensor(ULO[k][:, :], UT[:, k, :], UHI[k][:, :].bitcast(F32), ALU.subtract).then_inc(s_ulo, 1)

        @block.scalar
        def _(act):
            own = Steps(act, s_acts)
            nc.scalar.sem_inc(s_ev, 2)
            nc.scalar.sem_inc(s_gev, 4)
            nc.scalar.sem_inc(s_mod, 1)
            nc.scalar.sem_inc(s_gel, 2)
            act.wait_ge(s_vt, 1)
            nc.scalar.activation(COND[:, :, :].rearrange("p k c -> p c k"),
                                 VT[:, R_CTX:R_CTX + 16].rearrange("p (c k) -> p c k", c=2), ACT.Silu).then_inc(s_act0, 1)

            def mod(l, first, last):
                with act.Fori(first, last) as i:
                    for q in range(SEGB):
                        act.wait_ge(s_mrow, SEGB * (MODSEGS * l + i) + q + 1)
                        nc.scalar.activation(MROW[:, q * MODB:(q + 1) * MODB], PS[0:2, 5 + q % 2, 0:MODB], ACT.Copy)\
                            .then_inc(s_mev, 1)
                    act.wait_ge(s_mtr, MODSEGS * l + i + 1)
                    nc.scalar.activation(MODT[:, l, bass.ds(KC * i, KC), :],
                                         PS[:, 7, 0:2 * KC].rearrange("p (a b) -> p a b", b=2), ACT.Copy).then_inc(s_mod, 1)

            mod(0, 0, MODSEGS)
            act.wait_ge(s_init, 2)
            nc.scalar.activation(SKT[:, :, :].rearrange("p a b -> p (a b)"), PS[:, 4, :], ACT.Copy).then_inc(s_act0, 1)

            def norm(n):
                l, which = divmod(n, 2)
                for k in range(KC):
                    q = KC * n + k
                    if n or k >= 2:
                        act.wait_ge(s_ss, q - 1)
                    if n == 0:
                        act.wait_ge(s_xe, k + 1)
                    else:
                        act.wait_ge(s_res, KC * (n - 1) + k + 1)
                    nc.scalar.activation(SQ[:, k % 2, :], xT[:, k, :], ACT.Square).then_inc(s_sq, 1)
                act.wait_ge(s_rc, n + 1)
                nc.scalar.activation(RT, RC, ACT.Sqrt).then_inc(s_rt, 1)
                if n == 4:
                    return
                for k in range(KC):
                    act.wait_ge(s_t1, q0 := KC * n + k + 1)
                    for t0, m, cnd in SEGS:
                        ins = nc.scalar.activation(HH[:, k, t0:t0 + m], T1[:, k % 2, t0:t0 + m], ACT.Identity,
                                                   bias=MODT[:, l, 24 * which + k, cnd:cnd + 1])
                    ins.then_inc(s_hhi, 1)

            def hi(stage, pair, k):
                act.wait_ge(raw_in[k], filled(stage, pair))
                act.wait_ge(s_unit, UNIT0[stage] + 2 * pair + k + 1)
                if stage in ("a_out", "c_out"):
                    nc.scalar.activation(WHI[k][:, :].rearrange("p (c m) -> p c m", c=KC), chunk_view(RAW[:, k, :]), ACT.Copy)\
                        .then_inc(s_hi, 1)
                else:
                    nc.scalar.activation(WHI[k][:, :], RAW[:, k, :], ACT.Copy).then_inc(s_hi, 1)

            def his(stage, evacuate=None):
                with act.Fori(0, COUNT[stage] // 2 - 1) as i:
                    hi(stage, i, 1)
                    if evacuate:
                        evacuate(2 * i, 0)
                    hi(stage, i + 1, 0)
                    if evacuate:
                        evacuate(2 * i + 1, 1)
                i = COUNT[stage] // 2 - 1
                hi(stage, i, 1)
                if evacuate:
                    evacuate(2 * i, 0)
                hi(NEXT[stage], 0, 0)
                if evacuate:
                    evacuate(2 * i + 1, 1)

            def to_view(view, stage, first):
                def evacuate(u, k):
                    act.wait_ge(s_unit, UNIT0[stage] + u + 3)
                    nc.scalar.activation(view[:, bass.ds(first + u, 1), :].rearrange("p a t -> p (a t)"),
                                         PS[:, k, 0:T], ACT.Copy).then_inc(s_ev, 1)
                return evacuate

            hi("q", 0, 0)
            norm(0)
            his("q", to_view(Z, "q", 0))
            his("kvp", to_view(Z, "kvp", 4))

            act.wait_ge(s_ev, 2 + 10)
            mact.mark("zsq", nc.scalar.activation(ZS[:, :, :], Z[:, 0:5, :], ACT.Square))
            mdve.wait(act, "rc")
            mact.mark("root", nc.scalar.activation(ZS[:, :, :], QN[:, :, :], ACT.Sqrt))
            mpe.wait(act, "kv")
            mact.mark("kpast", nc.scalar.activation(KALL[:, NSAMPLE:T], PS[:, 7, 0:P], ACT.Copy))
            mact.mark("vtok", nc.scalar.activation(VTOK[:, :, :], PS[:, 7, P:512].rearrange("p (a b) -> p a b", a=3), ACT.Copy))
            mpe.wait(act, "ktok")
            mact.mark("ktok", nc.scalar.activation(KTOK, PS[:, 0, 0:P], ACT.Copy))
            mact.wait(act, "ktok")
            act.dma_start(new_k[0, 0, :, :, :].rearrange("s h d -> s (h d)"), KTOK).then_inc(s_nkv, 16)
            act.dma_start(new_v[0, 0, :, :, :].rearrange("s h d -> s (h d)"), VTOK[:, 0, :]).then_inc(s_nkv, 16)
            for b, (qt, j) in enumerate(BATCHES):
                n = P if qt == 0 else T
                mdve.wait(act, f"nb{b}")
                for q in range(4):
                    ins = nc.scalar.activation(PROB[b % 2][:, q, 0:n], PS[:, q, 0:n], ACT.Exp, bias=NB[:, q:q + 1],
                                               scale=0.125, accum_out=SM[:, q:q + 1])
                mact.mark(f"e{b}", ins)
                mpe.wait(act, f"t{b}")
                mact.mark(f"pt{b}", nc.scalar.activation(PROBT[:, :, 0:n], PS[:, 4:8, 0:n], ACT.Copy))
                mpe.wait(act, f"o{b}")
                rows = slice(64 * j, 64 * j + 64)
                mact.mark(f"oh{b}", nc.scalar.activation(HH[rows, 0:4, qt * P:qt * P + P],
                                                         PS[rows, 4, :].rearrange("p (a b) -> p a b", a=4), ACT.Copy))
            for g in range(4):
                mpe.wait(act, f"pw{g}")
                mact.mark(f"ph{g}", nc.scalar.activation(HH[:, 4 + g, :], PS[:, g, 0:T], ACT.Copy,
                                                         scale=VT[:, R_PS + g:R_PS + g + 1]))
            his("a_out")

            for l in range(LAYERS):
                if l:
                    norm(2)
                    his("c_in")
                    for k in range(0, KC, 2):
                        act.wait_ge(s_cm, KC)
                        nc.scalar.activation(HH[:, k:k + 2, :], CM[:, k:k + 2, :], ACT.Copy).then_inc(s_hhi, 1)
                    his("c_out")
                else:
                    act.wait_ge(s_nkv, 32)
                norm(2 * l + 1)
                his(f"wq{l}", to_view(QT, f"wq{l}", 0))
                def copy_scores(tile):
                    g = TT * l + tile
                    act.wait_ge(s_sc, g + 1)
                    if tile:
                        act.wait_ge(s_l1, g)
                    nc.scalar.activation(SC[:, :, :].rearrange("p (a b) c -> p a (b c)", a=4), PS[:, 3:7, :], ACT.Copy)\
                        .then_inc(s_scc, 1)

                def u_hi(i, k):
                    g = P * l + 2 * i + k
                    act.wait_ge(s_tr, g + 1)
                    act.wait_ge(s_S, g + 1)
                    nc.scalar.activation(UHI[k][:, :], UT[:, k, :], ACT.Copy).then_inc(s_uhi, 1)

                def gelu(i, k):
                    act.wait_ge(s_S, P * l + 2 * i + k + 3)
                    act.wait_ge(s_sst[k], 16 * (P // 2 * l + i + 1))
                    nc.scalar.activation(GEL[:, k, :], PS[:, k, 0:T], ACT.Gelu).then_inc(s_gel, 1)

                def s_step(i, k):
                    u_hi(i + 1, k)
                    gelu(i, k)

                def gates(tile, turn, group):
                    act.wait_ge(s_gm, 4 + 32 * (TT * l + tile) + 4 * turn + group + 1)
                    nc.scalar.activation(STAGE[:, :, bass.ds(16 * turn + 4 * group, 4)].rearrange("p i t -> p t i"),
                                         PS[:, 3 + group, :].rearrange("p (t i) -> p t i", t=4), ACT.Copy).then_inc(s_gev, 1)

                copy_scores(0)
                u_hi(0, 0)
                u_hi(0, 1)
                at = 0
                for tile in range(TT):
                    g = TT * l + tile
                    s_tiles(act, at, S_LEVEL1, s_step)
                    at += S_LEVEL1
                    if tile + 1 < TT:
                        copy_scores(tile + 1)
                    s_tiles(act, at, S_LEVEL2, s_step)
                    at += S_LEVEL2
                    act.wait_ge(s_d, g + 1)
                    nc.scalar.activation(EX[:, :, :], EX[:, :, :], ACT.Exp).then_inc(s_e, 1)
                    if l == 0:
                        mod(1, 2 * tile, 2 * tile + 2)
                    act.wait_ge(s_ptr, g + 1)
                    cols = slice(tile * P, tile * P + P)
                    nc.scalar.activation(IT1[:, cols], PS[:, 7, 0:P], ACT.Copy)
                    nc.scalar.activation(IT2[:, cols], PS[:, 7, P:2 * P], ACT.Copy).then_inc(s_pte, 1)
                for tile in range(TT):
                    if tile:
                        act.wait_ge(s_gst, 16 * (TT * l + tile))
                    with act.Fori(0, TURNS) as i:
                        for k in range(2):
                            s_step(at // 2 + i, k)
                            gates(tile, i, 2 * k)
                            gates(tile, i, 2 * k + 1)
                    at += 2 * TURNS
                    if tile + 1 < TT:
                        s_tiles(act, at, S_STORE, s_step)
                        at += S_STORE
                s_tiles(act, at, S_REST - 2, s_step)
                gelu(P // 2 - 1, 0)
                gelu(P // 2 - 1, 1)

                def w_hi(i, k):
                    t = 2 * i + k
                    act.wait_ge(s_w, P * l + t + 1)
                    act.wait_ge(s_unit, UNIT0[f"v{l}"] + t + 1)
                    nc.scalar.activation(EHI[k][:, :], GEL[:, k, :], ACT.Copy).then_inc(s_whi, 1)

                v = f"v{l}"
                w_hi(0, 0)
                with act.Fori(0, P // 2 - 1) as i:
                    w_hi(i, 1)
                    hi(v, i, 1)
                    w_hi(i + 1, 0)
                    hi(v, i + 1, 0)
                w_hi(P // 2 - 1, 1)
                hi(v, P // 2 - 1, 1)
                if l == 0:
                    hi("c_in", 0, 0)
                act.wait_ge(s_unit, UNIT0[v] + P + 2)
                for tile in range(TT):
                    nc.scalar.activation(XS[:, tile, :].rearrange("p (a b) -> p a b", a=2),
                                         PS[:, 2 + 2 * tile:4 + 2 * tile, :], ACT.Copy).then_inc(s_acc, 1)
            norm(4)
            for q in range(6):
                act.wait_ge(s_ytr, q + 1)
                nc.scalar.activation(chunk_view(YTOK[:, q // 2, :])[:, 4 * (q % 2):4 * (q % 2) + 4, :],
                                     PS[:, 3 + q % 2, :].rearrange("p (c m) -> p c m", c=4), ACT.Copy).then_inc(s_ye, 1)

        @block.tensor
        def _(pe):
            nc.tensor.sem_inc(s_unit, 2)
            nc.tensor.sem_inc(s_gm, 4)
            nc.tensor.sem_inc(s_S, 2)
            pe.wait_ge(s_vec, 16 * 13)
            nc.tensor.transpose(PS[:, 3, 0:VROWS], VR[0:VROWS, :], IDENT[0:VROWS, 0:VROWS]).then_inc(s_init, 1)
            pe.wait_ge(s_cst, 16 * 5)
            for q in range(4):
                ins = nc.tensor.transpose(PS[:, 4, q * P:q * P + P], SKR[:, q, :], IDENT[:, :])
            ins.then_inc(s_init, 1)
            pe.wait_ge(s_x, 32)
            for k in range(KC):
                if k >= 2:
                    pe.wait_ge(s_xe, k - 1)
                for tile in range(TT):
                    ins = nc.tensor.transpose(PS[:, k % 2, tile * P:tile * P + P], chunk_view(XS[:, tile, :])[:, k, :], IDENT[:, :])
                ins.then_inc(s_xt, 1)
            pe.wait_ge(s_act0, 1)

            def mod(l, first, last):
                with pe.Fori(first, last) as i:
                    row = MODSEGS * l + i
                    for q in range(SEGB):
                        pe.wait_ge(mod_in[q % 2], 8 * SEGB * row + 16 * (q // 2 + 1))
                        if q >= 2:
                            pe.wait_ge(s_mev, SEGB * row + q - 1)
                        for kc in range(KC):
                            ins = nc.tensor.matmul(PS[0:2, 5 + q % 2, 0:MODB], COND[:, kc, :], MODR[:, q % 2, kc, :],
                                                   start=kc == 0, stop=kc == KC - 1)
                        ins.then_inc(s_mrow, 1)
                    pe.wait_ge(s_mod, row + 1)
                    pe.wait_ge(s_mev, SEGB * (row + 1))
                    for m in range(KC):
                        ins = nc.tensor.matmul(PS[:, 7, 2 * m:2 * m + 2], chunk_view(MROW[:, :])[:, m, :], IDENT[0:2, 0:2],
                                               start=True, stop=True)
                    ins.then_inc(s_mtr, 1)

            mod(0, 0, MODSEGS)

            def norm(n):
                for k in range(KC):
                    pe.wait_ge(s_sq, KC * n + k + 1)
                    nc.tensor.matmul(PS[:, NORM_BANK[n], 0:T], MEAN1[:, :], SQ[:, k % 2, :], start=k == 0, stop=k == KC - 1)\
                        .then_inc(s_ss, 1)

            def project(stage):
                with pe.Fori(0, COUNT[stage] // 2) as i:
                    for s in range(2):
                        u = 2 * i + s
                        pe.wait_ge(s_lo, UNIT0[stage] + u + 3)
                        pe.wait_ge(s_ev, PROJ0[stage] + u + 1)
                        for k in range(KC):
                            cols = slice(k * P, k * P + P)
                            nc.tensor.matmul(PS[:, s, 0:T], WHI[s][:, cols], HH[:, k, :], start=k == 0, stop=False)
                            nc.tensor.matmul(PS[:, s, 0:T], WHI[s][:, cols], HL[:, k, :], start=False, stop=False)
                            ins = nc.tensor.matmul(PS[:, s, 0:T], WLO[s][:, cols], HH[:, k, :], start=False, stop=k == KC - 1)
                        ins.then_inc(s_unit, 1)

            def project_out(stage):
                for u in range(KC):
                    pe.wait_ge(s_lo, UNIT0[stage] + u + 3)
                    for k in range(KC):
                        cols = slice(k * P, k * P + P)
                        nc.tensor.matmul(PS[:, k, 0:T], WHI[u % 2][:, cols], HH[:, u, :], start=u == 0, stop=False)
                        nc.tensor.matmul(PS[:, k, 0:T], WHI[u % 2][:, cols], HL[:, u, :], start=False, stop=False)
                        ins = nc.tensor.matmul(PS[:, k, 0:T], WLO[u % 2][:, cols], HH[:, u, :], start=False, stop=u == KC - 1)
                    ins.then_inc(s_unit, 1)

            norm(0)
            pe.wait_ge(s_hhi, KC)
            pe.wait_ge(s_hlo, KC)
            project("q")
            project("kvp")

            mact.wait(pe, "zsq")
            for q in range(5):
                ins = nc.tensor.matmul(PS[:, 2 + q, 0:T], HMEAN[:, :], ZS[:, q, :], start=True, stop=True)
            mpe.mark("hm", ins)
            pe.wait_ge(s_att, 16 * 6)
            nc.tensor.transpose(PS[:, 7, 0:P], KPAST, IDENT[:, :])
            for tile in range(TT):
                ins = nc.tensor.transpose(PS[:, 7, (tile + 1) * P:(tile + 2) * P], Z[:, 5, tile * P:tile * P + P], IDENT[:, :])
            mpe.mark("kv", ins)
            mdve.wait(pe, "qn")
            mpe.mark("ktok", nc.tensor.transpose(PS[:, 0, 0:P], QN[:, 4, 0:P], IDENT[:, :]))
            for q in range(5):
                ins = nc.tensor.matmul(PS[:, 2 + q, 0:NSAMPLE], ROT[:, :], QN[:, q, NPROMPT:T], start=True, stop=True)
            mpe.mark("rot", ins)

            def scores(b):
                qt, j = BATCHES[b]
                rows = slice(64 * j, 64 * j + 64)
                if b:
                    mact.wait(pe, f"e{b - 1}")
                else:
                    mact.wait(pe, "ktok")
                if b == 2:
                    mdve.wait(pe, "rope")
                    mact.wait(pe, "kpast")
                for q in range(4):
                    if qt == 0:
                        ins = nc.tensor.matmul(PS[:, q, 0:P], QN[rows, q, 0:P], QN[rows, 4, 0:P], start=True, stop=True)
                    else:
                        ins = nc.tensor.matmul(PS[:, q, 0:T], RQ[rows, q, (qt - 1) * P:qt * P], KALL[rows, :], start=True, stop=True)
                mpe.mark(f"s{b}", ins)

            mdve.wait(pe, "rope")
            scores(0)
            for b, (qt, j) in enumerate(BATCHES):
                rows = slice(64 * j, 64 * j + 64)
                nkt = 1 if qt == 0 else 3
                if b + 1 < NBT:
                    scores(b + 1)
                mdve.wait(pe, f"p{b}")
                if b:
                    mdve.wait(pe, f"ol{b - 1}")
                else:
                    mact.wait(pe, "vtok")
                for q in range(4):
                    for kt in range(nkt):
                        ins = nc.tensor.transpose(PS[:, 4 + q, kt * P:kt * P + P], PROB[b % 2][:, q, kt * P:kt * P + P], IDENT[:, :])
                mpe.mark(f"t{b}", ins)
                mact.wait(pe, f"pt{b}")
                for kt in range(nkt):
                    if qt == 0:
                        val = VTOK[:, 0, rows]
                    else:
                        val = VTOK[:, 1 + kt, rows] if kt < 2 else VPAST[:, rows]
                    ins = nc.tensor.matmul(PS[rows, 4, :], val, PROBT[:, :, kt * P:kt * P + P], start=kt == 0, stop=kt == nkt - 1)
                mpe.mark(f"o{b}", ins)
            mact.wait(pe, f"e{NBT - 1}")
            for g in range(4):
                pe.wait_ge(s_pm, g + 1)
                mpe.mark(f"pw{g}", nc.tensor.matmul(PS[:, g, 0:T], PW[:, g, :], Z[:, 6 + g, :], start=True, stop=True))
            mdve.wait(pe, "pl3")
            project_out("a_out")

            for l in range(LAYERS):
                if l:
                    norm(2)
                    pe.wait_ge(s_hlo, 3 * KC)
                    project("c_in")
                    pe.wait_ge(s_hlo, 3 * KC + 4)
                    project_out("c_out")
                norm(2 * l + 1)
                pe.wait_ge(s_hlo, (4 * KC + 4) if l else 2 * KC)
                project(f"wq{l}")

                def tile_scores(tile):
                    if tile:
                        pe.wait_ge(s_scc, TT * l + tile)
                    else:
                        pe.wait_ge(s_ev, 2 + PROJ0[f"wq{l}"] + 16)
                    for u in range(16):
                        ins = nc.tensor.matmul(PS[:, 3 + u // 4, (u % 4) * P:(u % 4) * P + P],
                                               QT[:, u, tile * P:tile * P + P], SKT[:, 2 * l + u % 2, :], start=True, stop=True)
                    ins.then_inc(s_sc, 1)

                def turn_picks(tile):
                    g = TT * l + tile
                    pe.wait_ge(s_pick, g + 1)
                    if l == 0:
                        pe.wait_ge(s_mod, 1 + MODSEGS + (tile + 1) * MODSEGS // TT)
                    if g:
                        pe.wait_ge(s_pte, g)
                        pe.wait_ge(s_pts, g)
                    for q, src in enumerate((ID1, ID2, GT.rearrange("p a b -> p (a b)"))):
                        ins = nc.tensor.transpose(PS[:, 7, q * P:q * P + P], src, IDENT[:, :])
                    ins.then_inc(s_ptr, 1)

                def s_tile(i, k):
                    g = P * l + 2 * i + k
                    pe.wait_ge(s_ulo, g + 3)
                    pe.wait_ge(s_gel, g + 1)
                    for c_ in range(KC):
                        cols = slice(c_ * P, c_ * P + P)
                        nc.tensor.matmul(PS[:, k, 0:T], UHI[k][:, cols], HH[:, c_, :], start=c_ == 0, stop=False)
                        nc.tensor.matmul(PS[:, k, 0:T], UHI[k][:, cols], HL[:, c_, :], start=False, stop=False)
                        ins = nc.tensor.matmul(PS[:, k, 0:T], ULO[k][:, cols], HH[:, c_, :], start=False, stop=c_ == KC - 1)
                    ins.then_inc(s_S, 1)

                def gates(tile, turn, k):
                    b = 2 * TURNS * (TT * l + tile) + 2 * turn + k
                    pe.wait_ge(s_oh, b + 1)
                    for group in range(2):
                        pe.wait_ge(s_gev, 2 * b + group + 1)
                        for q in range(4):
                            for part in range(3):
                                tok = 4 * group + q
                                ins = nc.tensor.matmul(PS[:, 3 + 2 * k + group, q * P:q * P + P], OH2[k][:, :, tok],
                                                       OH1[k][part][:, :, tok], start=part == 0, stop=part == 2)
                        ins.then_inc(s_gm, 1)

                def v_tile(i, k, first=False, last=False):
                    t = 2 * i + k
                    pe.wait_ge(s_wlo, P * l + t + 1)
                    pe.wait_ge(s_lo, UNIT0[f"v{l}"] + t + 3)
                    for tile in range(TT):
                        tok = slice(tile * P, tile * P + P)
                        for q, (e, w) in enumerate(((EHI, WHI), (EHI, WLO), (ELO, WHI))):
                            for half in range(2):
                                ins = nc.tensor.matmul(PS[:, 2 + 2 * tile + half, :], e[k][:, tok],
                                                       w[k][:, 512 * half:512 * half + 512],
                                                       start=first and q == 0, stop=last and q == 2)
                    ins.then_inc(s_unit, 1)

                pe.wait_ge(s_act0, 2)
                tile_scores(0)
                at = 0
                for tile in range(TT):
                    s_tiles(pe, at, S_LEVEL1, s_tile)
                    at += S_LEVEL1
                    if tile + 1 < TT:
                        tile_scores(tile + 1)
                    s_tiles(pe, at, S_LEVEL2, s_tile)
                    at += S_LEVEL2
                    if l == 0:
                        pe.wait_ge(s_scc, min(tile + 2, TT))
                        if tile:
                            pe.wait_ge(s_pte, tile)
                            pe.wait_ge(s_pts, tile)
                        mod(1, 2 * tile, 2 * tile + 2)
                    turn_picks(tile)
                for tile in range(TT):
                    with pe.Fori(0, TURNS) as i:
                        for k in range(2):
                            s_tile(at // 2 + i, k)
                            gates(tile, i, k)
                    at += 2 * TURNS
                    if tile + 1 < TT:
                        s_tiles(pe, at, S_STORE, s_tile)
                        at += S_STORE
                s_tiles(pe, at, S_REST, s_tile)
                pe.wait_ge(s_gev, 4 + 32 * TT * (l + 1))
                v_tile(0, 0, first=True)
                v_tile(0, 1)
                with pe.Fori(1, P // 2 - 1) as i:
                    v_tile(i, 0)
                    v_tile(i, 1)
                v_tile(P // 2 - 1, 0)
                v_tile(P // 2 - 1, 1, last=True)
                pe.wait_ge(s_acc, TT * (l + 1))
                for k in range(KC):
                    if k >= 2:
                        pe.wait_ge(s_res, KC * (2 * l + 1) + k - 1)
                    if k == 0:
                        pe.wait_ge(s_gel, P * (l + 1) + 2)
                    for tile in range(TT):
                        ins = nc.tensor.transpose(PS[:, k % 2, tile * P:tile * P + P], chunk_view(XS[:, tile, :])[:, k, :], IDENT[:, :])
                    ins.then_inc(s_at, 1)
            norm(4)
            for q in range(6):
                tile, half = divmod(q, 2)
                pe.wait_ge(s_yt, KC)
                if q >= 2:
                    pe.wait_ge(s_ye, q - 1)
                for m in range(4):
                    ins = nc.tensor.transpose(PS[:, 3 + half, m * P:m * P + P], YT[:, 4 * half + m, tile * P:tile * P + P], IDENT[:, :])
                ins.then_inc(s_ytr, 1)

        @block.vector
        def _(dve):
            V = nc.vector
            own = Steps(dve, s_dve)
            V.sem_inc(s_lo, 2)
            dve.wait_ge(s_init, 1)
            V.tensor_copy(VT[:, 0:VROWS], PS[:, 3, 0:VROWS]).then_inc(s_vt, 1)
            for k in range(KC):
                dve.wait_ge(s_xt, k + 1)
                V.tensor_copy(xT[:, k, :], PS[:, k % 2, 0:T]).then_inc(s_xe, 1)
            dve.wait_ge(s_cst, 16 * 5)
            own.mark(V.tensor_copy(IOTA8[:, :, :], IOTA[:, :].unsqueeze(2).to_broadcast([P, P, BATCH])))

            def modulation(l):
                dve.wait_ge(s_mod, 1 + MODSEGS * (l + 1))
                dve.wait_ge(s_vt, 1)
                own.do(V.tensor_tensor(MODT[:, l, :, :], MODT[:, l, :, :],
                                       MBT[:, 48 * l:48 * l + 48].unsqueeze(2).to_broadcast([P, 48, 2]), ALU.add))
                for which, r in ((0, R_N1), (1, R_N2)):
                    ins = V.scalar_tensor_tensor(out=GS[:, l, which, :, :], in0=MODT[:, l, 24 * which + 8:24 * which + 16, :],
                                                 scalar=1.0, in1=VT[:, r + 8 * l:r + 8 * l + 8].unsqueeze(2).to_broadcast([P, KC, 2]),
                                                 op0=ALU.add, op1=ALU.mult)
                ins.then_inc(s_gs, 1)
                dve.wait_ge(s_gs, l + 1)

            def rsqrt_step(y, v, t):
                own.do(V.tensor_tensor(t, y, y, ALU.mult))
                own.do(V.tensor_tensor(t, t, v, ALU.mult))
                own.do(V.tensor_scalar(t, t, -0.5, 1.5, ALU.mult, ALU.add))
                own.do(V.tensor_tensor(y, y, t, ALU.mult))

            def norm(n):
                l, which = divmod(n, 2)
                dve.wait_ge(s_ss, KC * (n + 1))
                own.do(V.tensor_scalar(MV, PS[:, NORM_BANK[n], 0:T], EPS, None, ALU.add))
                V.reciprocal(RC, MV).then_inc(s_rc, 1)
                dve.wait_ge(s_rt, n + 1)
                rsqrt_step(RT, MV, NT)
                if n == 4:
                    for k in range(KC):
                        V.scalar_tensor_tensor(out=YT[:, k, :], in0=xT[:, k, :], scalar=VT[:, R_FIN + k:R_FIN + k + 1],
                                               in1=RT, op0=ALU.mult, op1=ALU.mult).then_inc(s_yt, 1)
                    return

                def scaled(k):
                    for t0, m, cnd in SEGS:
                        ins = V.scalar_tensor_tensor(out=T1[:, k % 2, t0:t0 + m], in0=xT[:, k, t0:t0 + m],
                                                     scalar=GS[:, l, which, k, cnd:cnd + 1], in1=RT[:, t0:t0 + m],
                                                     op0=ALU.mult, op1=ALU.mult)
                    ins.then_inc(s_t1, 1)

                def low(k):
                    dve.wait_ge(s_hhi, (KC * n + k + 1) + (4 if n == 3 else 0))
                    for t0, m, cnd in SEGS:
                        ins = V.scalar_tensor_tensor(out=HL[:, k, t0:t0 + m], in0=T1[:, k % 2, t0:t0 + m],
                                                     scalar=MODT[:, l, 24 * which + k, cnd:cnd + 1],
                                                     in1=HH[:, k, t0:t0 + m].bitcast(F32), op0=ALU.add, op1=ALU.subtract)
                    ins.then_inc(s_hlo, 1)

                hlo0 = KC * n + (4 if n == 3 else 0)
                scaled(0)
                for k in range(KC):
                    if k + 1 < KC:
                        if k >= 1:
                            dve.wait_ge(s_hlo, hlo0 + k)
                        scaled(k + 1)
                    if k == 0:
                        dve.wait_ge(s_t1, KC * n + 1)
                    low(k)

            def lo(stage, pair, k):
                dve.wait_ge(s_hi, UNIT0[stage] + 2 * pair + k + 1)
                if stage in ("a_out", "c_out"):
                    wlo, whi = (w[:, :].rearrange("p (c m) -> p c m", c=KC) for w in (WLO[k], WHI[k]))
                    V.tensor_tensor(wlo, chunk_view(RAW[:, k, :]), whi.bitcast(F32), ALU.subtract).then_inc(s_lo, 1)
                else:
                    V.tensor_tensor(WLO[k][:, :], RAW[:, k, :], WHI[k][:, :].bitcast(F32), ALU.subtract).then_inc(s_lo, 1)

            def los(stage, evacuate=None):
                with dve.Fori(0, COUNT[stage] // 2 - 1) as i:
                    lo(stage, i, 1)
                    if evacuate:
                        evacuate(2 * i, 0)
                    lo(stage, i + 1, 0)
                    if evacuate:
                        evacuate(2 * i + 1, 1)
                i = COUNT[stage] // 2 - 1
                lo(stage, i, 1)
                if evacuate:
                    evacuate(2 * i, 0)
                lo(NEXT[stage], 0, 0)
                if evacuate:
                    evacuate(2 * i + 1, 1)

            def add_gated(k, bank, l, gate, sem_, also=None):
                xk = xT[:, bass.ds(k, 1), :].rearrange("p a t -> p (a t)")
                for t0, m, cnd in SEGS:
                    g = MODT[:, l, bass.ds(gate + k, 1), cnd:cnd + 1].rearrange("p a b -> p (a b)")
                    ins = V.scalar_tensor_tensor(out=xk[:, t0:t0 + m], in0=PS[:, bank, t0:t0 + m], scalar=g,
                                                 in1=xk[:, t0:t0 + m], op0=ALU.mult, op1=ALU.add)
                ins.then_inc(sem_, 1)

            def to_residual(stage, l):
                dve.wait_ge(s_unit, UNIT0[stage] + KC + 2)
                for k in range(KC):
                    add_gated(k, k, l, 16, s_res)

            modulation(0)
            lo("q", 0, 0)
            norm(0)
            los("q")
            los("kvp")

            mpe.wait(dve, "hm")
            own.do(V.tensor_scalar(VAR[:, :, :], PS[:, 2:7, 0:T], EPS, None, ALU.add))
            mdve.mark("rc", V.reciprocal(QN[:, :, :], VAR[:, :, :]))
            mact.wait(dve, "root")
            rsqrt_step(ZS[:, :, :], VAR[:, :, :], QN[:, :, :])
            V.scalar_tensor_tensor(out=QN[:, 0:4, :], in0=Z[:, 0:4, :], scalar=VT[:, R_QG:R_QG + 1],
                                   in1=ZS[:, 0:4, :], op0=ALU.mult, op1=ALU.mult)
            mdve.mark("qn", V.scalar_tensor_tensor(out=QN[:, 4, :], in0=Z[:, 4, :], scalar=VT[:, R_KG:R_KG + 1],
                                                   in1=ZS[:, 4, :], op0=ALU.mult, op1=ALU.mult))
            mdve.wait(dve, "qn")
            mpe.wait(dve, "rot")
            dve.wait_ge(s_att, 16 * 6)
            own.mark(V.tensor_tensor(RQ[:, :, :], QN[:, 0:4, NPROMPT:T], COS.unsqueeze(1).to_broadcast([P, 4, NSAMPLE]), ALU.mult))
            own.mark(V.tensor_tensor(KALL[:, 0:NSAMPLE], QN[:, 4, NPROMPT:T], COS, ALU.mult))
            own.mark(V.tensor_tensor(VAR[:, :, 0:NSAMPLE], PS[:, 2:7, 0:NSAMPLE],
                                     SIN.unsqueeze(1).to_broadcast([P, 5, NSAMPLE]), ALU.mult))
            own.wait()
            own.mark(V.tensor_tensor(RQ[:, :, :], RQ[:, :, :], VAR[:, 0:4, 0:NSAMPLE], ALU.add))
            mdve.mark("rope", V.tensor_tensor(KALL[:, 0:NSAMPLE], KALL[:, 0:NSAMPLE], VAR[:, 4, 0:NSAMPLE], ALU.add))
            mdve.wait(dve, "rope")
            for b, (qt, j) in enumerate(BATCHES):
                n = P if qt == 0 else T
                rows = slice(64 * j, 64 * j + 64)
                mpe.wait(dve, f"s{b}")
                own.do(V.tensor_reduce(MX, PS[:, 0:4, 0:n], AX.X, ALU.max))
                mdve.mark(f"nb{b}", V.tensor_scalar(NB, MX, -0.125, None, ALU.mult))
                mact.wait(dve, f"e{b}")
                own.do(V.reciprocal(RV, SM))
                mdve.mark(f"p{b}", V.tensor_tensor(PROB[b % 2][:, :, 0:n], PROB[b % 2][:, :, 0:n],
                                                   RV.unsqueeze(2).to_broadcast([P, 4, n]), ALU.mult))
                mact.wait(dve, f"oh{b}")
                mdve.mark(f"ol{b}", V.tensor_tensor(HL[rows, 0:4, qt * P:qt * P + P],
                                                    PS[rows, 4, :].rearrange("p (a b) -> p a b", a=4),
                                                    HH[rows, 0:4, qt * P:qt * P + P].bitcast(F32), ALU.subtract))
            for g in range(4):
                mact.wait(dve, f"ph{g}")
                mdve.mark(f"pl{g}", V.scalar_tensor_tensor(out=HL[:, 4 + g, :], in0=PS[:, g, 0:T],
                                                           scalar=VT[:, R_PS + g:R_PS + g + 1],
                                                           in1=HH[:, 4 + g, :].bitcast(F32), op0=ALU.mult, op1=ALU.subtract))
            los("a_out")
            to_residual("a_out", 0)

            for l in range(LAYERS):
                if l:
                    modulation(1)
                    norm(2)
                    own.mark(V.memset(UP, 0.0))

                    def evac(i, jj, what, k):
                        u = 6 * i + 3 * jj + what
                        j = 2 * i + jj
                        dve.wait_ge(s_unit, UNIT0["c_in"] + u + 3)
                        own.wait()
                        if what == 0:
                            own.mark(V.tensor_copy(GC, PS[:, k, 0:T]))
                            own.wait()
                            V.sem_inc(s_ev, 1)
                        elif what == 1:
                            own.mark(V.tensor_tensor(UP[:, 1:1 + NPROMPT], PS[:, k, 0:NPROMPT], GC[:, 0:NPROMPT], ALU.mult))
                            V.tensor_tensor(UP[:, 2 + NPROMPT:2 + T], PS[:, k, NPROMPT:T], GC[:, NPROMPT:T], ALU.mult).then_inc(s_ev, 1)
                            own.wait()
                            dve.wait_ge(s_ev, 2 + PROJ0["c_in"] + u + 1)
                            tap = [VT[:, bass.ds(R_CW + 8 * w + j, 1)] for w in range(3)]
                            own.do(V.tensor_scalar(YA[:, 0:T + 1], UP[:, 0:T + 1], tap[0], None, ALU.mult))
                            for w in (1, 2):
                                own.do(V.scalar_tensor_tensor(out=YA[:, 0:T + 1], in0=UP[:, w:w + T + 1], scalar=tap[w],
                                                              in1=YA[:, 0:T + 1], op0=ALU.mult, op1=ALU.add))
                        else:
                            cm = CM[:, bass.ds(j, 1), :].rearrange("p a t -> p (a t)")
                            own.mark(V.tensor_tensor(cm[:, 0:NPROMPT], PS[:, k, 0:NPROMPT], YA[:, 0:NPROMPT], ALU.mult))
                            V.tensor_tensor(cm[:, NPROMPT:T], PS[:, k, NPROMPT:T], YA[:, NPROMPT + 1:T + 1], ALU.mult).then_inc(s_ev, 1)

                    def conv_pair(i, last=False):
                        for q in range(6):
                            if q < 5:
                                k = (q + 1) % 2
                                lo("c_in", 3 * i + (q + 1) // 2, k)
                            elif not last:
                                lo("c_in", 3 * i + 3, 0)
                            else:
                                lo("c_out", 0, 0)
                            evac(i, q // 3, q % 3, q % 2)

                    with own.loop(3, 12) as i:
                        conv_pair(i)
                    conv_pair(3, last=True)
                    dve.wait_ge(s_ev, 2 + PROJ0["c_in"] + 24)
                    own.wait()
                    V.sem_inc(s_cm, KC)
                    for k in range(0, KC, 2):
                        dve.wait_ge(s_hhi, 3 * KC + k // 2 + 1)
                        V.tensor_tensor(HL[:, k:k + 2, :], CM[:, k:k + 2, :], HH[:, k:k + 2, :].bitcast(F32), ALU.subtract)\
                            .then_inc(s_hlo, 1)
                    los("c_out")
                    to_residual("c_out", 1)
                norm(2 * l + 1)
                los(f"wq{l}")

                def turn_u(i, k):
                    dve.wait_ge(u_in[k], 64 * (P // 2 * l + i + 1))
                    dve.wait_ge(s_ulo, P * l + 2 * i + k + 1)
                    V.transpose(UT[:, k, :].rearrange("p (c b e) -> p c b e", c=KC, b=4),
                                URAW[:, k, :, :].rearrange("p b (j c) -> p c b j", c=KC)).then_inc(s_tr, 1)

                def s_step(i, k):
                    turn_u(i + 1, k)

                turned = [1]

                def next_u():
                    turned[0] += 1
                    turn_u(*divmod(turned[0], 2))

                def top16(vals, idx, src, rest, rows, beside):
                    def turn(step, u):
                        if (step, u) in beside:
                            next_u()

                    for u in range(rows):
                        turn(0, u)
                        ins = V.max(vals[:, u, 0:8], src[:, u, :])
                    own.do(ins)
                    for u in range(rows):
                        turn(1, u)
                        V.max_index(idx[:, u, 0:8], vals[:, u, 0:8], src[:, u, :])
                        ins = V.match_replace(rest[:, u, :], vals[:, u, 0:8], src[:, u, :], NEG)
                    own.do(ins)
                    for u in range(rows):
                        turn(2, u)
                        ins = V.max(vals[:, u, 8:16], rest[:, u, :])
                    own.do(ins)
                    for u in range(rows):
                        turn(3, u)
                        ins = V.max_index(idx[:, u, 8:16], vals[:, u, 8:16], rest[:, u, :])
                    return ins

                def pick_tail(tile):
                    cols = slice(tile * P, tile * P + P)
                    dve.wait_ge(s_pte, TT * l + tile + 1)
                    bank = PS[:, 7, 2 * P:3 * P]
                    own.do(V.tensor_copy(GP[:, 0, cols], bank))
                    own.do(V.tensor_tensor(GRES, bank, GP[:, 0, cols], ALU.subtract))
                    own.do(V.tensor_copy(GP[:, 1, cols], GRES))
                    V.tensor_tensor(GP[:, 2, cols], GRES, GP[:, 1, cols], ALU.subtract).then_inc(s_pts, 1)
                    dve.wait_ge(s_pts, TT * l + tile + 1)

                turn_u(0, 0)
                turn_u(0, 1)
                for tile in range(TT):
                    g = TT * l + tile
                    dve.wait_ge(s_scc, g + 1)
                    top16(V16, I16U, SC, SC2, 16, ((0, 8), (1, 0), (1, 6), (1, 12), (2, 4), (3, 0))).then_inc(s_l1, 1)
                    dve.wait_ge(s_l1, g + 1)
                    own.mark(V.tensor_copy(I16F[:, :, :], I16U[:, :, :]))
                    side = V16.rearrange("p (h s) k -> p h s k", s=2)
                    for a in range(TOPK):
                        if a == 8:
                            next_u()
                        ins = V.tensor_tensor(CA[:, :, a * TOPK:(a + 1) * TOPK],
                                              side[:, :, 1, :], side[:, :, 0, a:a + 1].to_broadcast([P, HEADS, TOPK]), ALU.add)
                    own.do(ins)
                    if tile:
                        pick_tail(tile - 1)
                    own.do(top16(V2, FIU, CA, CA2, HEADS, ((0, 0), (1, 0), (1, 3), (1, 6), (2, 2), (3, 2))))
                    fi = FIU[:, :, :].rearrange("p a b -> p (a b)")
                    own.mark(V.tensor_scalar(FAU[:, :], fi, 4, None, ALU.logical_shift_right))
                    own.mark(V.tensor_scalar(FBU[:, :], fi, TOPK - 1, None, ALU.bitwise_and))
                    V.tensor_tensor(EX[:, :, :], V2[:, :, :], V2[:, :, 0:1].to_broadcast([P, HEADS, TOPK]), ALU.subtract)\
                        .then_inc(s_d, 1)
                    own.wait()
                    own.mark(V.tensor_copy(FA, FAU[:, :]))
                    own.do(V.tensor_copy(FB, FBU[:, :]))
                    iota16 = IOTA[:, 0:TOPK].unsqueeze(1).to_broadcast([P, PICKS, TOPK])
                    own.mark(V.tensor_tensor(EQ[:, :, :], FA.unsqueeze(2).to_broadcast([P, PICKS, TOPK]), iota16, ALU.is_equal))
                    next_u()
                    own.do(V.tensor_tensor(EQ2[:, :, :], FB.unsqueeze(2).to_broadcast([P, PICKS, TOPK]), iota16, ALU.is_equal))
                    keys = I16F.rearrange("p (h s) k -> p h s k", s=2)
                    for eq, s in ((EQ, 0), (EQ2, 1)):
                        next_u()
                        for h in range(HEADS):
                            e = eq[:, h * TOPK:(h + 1) * TOPK, :]
                            ins = V.tensor_tensor(e, e, keys[:, h, s:s + 1, :].to_broadcast([P, TOPK, TOPK]), ALU.mult)
                    own.do(ins)
                    next_u()
                    own.mark(V.tensor_reduce(ID1, EQ[:, :, :], AX.X, ALU.add))
                    next_u()
                    own.mark(V.tensor_reduce(ID2, EQ2[:, :, :], AX.X, ALU.add))
                    dve.wait_ge(s_e, g + 1)
                    own.do(V.tensor_reduce(ZSUM, EX[:, :, :], AX.X, ALU.add))
                    own.do(V.reciprocal(ZINV, ZSUM))
                    V.tensor_tensor(GT[:, :, :], EX[:, :, :], ZINV.unsqueeze(2).to_broadcast([P, HEADS, TOPK]), ALU.mult)\
                        .then_inc(s_pick, 1)
                    assert turned[0] == 1 + (tile + 1) * (S_LEVEL1 + S_LEVEL2)
                pick_tail(2)

                def one_hots(tile, turn, k, at):
                    dve.wait_ge(s_gm, 2 * (2 * TURNS * (TT * l + tile) + 2 * turn + k) + 2)
                    tok = bass.ds(tile * P + 16 * turn + BATCH * k, BATCH)

                    def spread(x):
                        return x.unsqueeze(1).to_broadcast([P, P, BATCH])

                    own.do(V.tensor_tensor(EQ1[:, :, :], IOTA8[:, :, :], spread(IT1[:, tok]), ALU.is_equal))
                    V.tensor_tensor(OH2[k], IOTA8[:, :, :], spread(IT2[:, tok]), ALU.is_equal)
                    s_step(at, k)
                    for part in range(3):
                        ins = V.tensor_tensor(OH1[k][part], EQ1[:, :, :], spread(GP[:, part, tok]), ALU.mult)
                    ins.then_inc(s_oh, 1)
                    dve.wait_ge(s_oh, 2 * TURNS * (TT * l + tile) + 2 * turn + k + 1)

                at = TT * (S_LEVEL1 + S_LEVEL2)
                for tile in range(TT):
                    with own.loop(TURNS, 2) as i:
                        one_hots(tile, i, 0, at // 2 + i)
                        one_hots(tile, i, 1, at // 2 + i)
                    at += 2 * TURNS
                    if tile + 1 < TT:
                        s_tiles(dve, at, S_STORE, s_step)
                        at += S_STORE
                s_tiles(dve, at, S_REST - 2, s_step)

                def weigh(i, k):
                    dve.wait_ge(g_in[k], 32 * (P // 2 * l + i + 1))
                    V.tensor_tensor(GEL[:, k, :], GEL[:, k, :], GIN[:, k, :], ALU.mult).then_inc(s_w, 1)

                def w_lo(i, k):
                    g = P * l + 2 * i + k
                    dve.wait_ge(s_whi, g + 1)
                    V.tensor_tensor(ELO[k][:, :], GEL[:, k, :], EHI[k][:, :].bitcast(F32), ALU.subtract).then_inc(s_wlo, 1)

                v = f"v{l}"
                weigh(0, 0)
                w_lo(0, 0)
                weigh(0, 1)
                with dve.Fori(0, P // 2 - 1) as i:
                    w_lo(i, 1)
                    lo(v, i, 1)
                    weigh(i + 1, 0)
                    w_lo(i + 1, 0)
                    lo(v, i + 1, 0)
                    weigh(i + 1, 1)
                w_lo(P // 2 - 1, 1)
                lo(v, P // 2 - 1, 1)
                if l == 0:
                    lo("c_in", 0, 0)
                for k in range(KC):
                    dve.wait_ge(s_at, KC * l + k + 1)
                    add_gated(k, k % 2, l, 40, s_res)
            norm(4)


_INS = ["x_prompt", "x_sample", "cache_k", "cache_v", "c", "c_ctx", "mod_w", "mod_b", "norm1_g", "norm2_g",
        "a_in_w", "a_out_w", "q_norm_g", "k_norm_g", "pool_w", "pool_scale", "c_in_w", "c_conv_w", "c_out_w",
        "peer_wq", "peer_subkeys", "peer_u", "peer_v", "final_g"]
_OUTS = [(1, 128, 1024), (1, 256, 1024), (1, 1, 128, 2, 64), (1, 1, 128, 2, 64)]


def _tables():
    import numpy as np

    f = np.float32
    ident = np.eye(128, dtype=f)
    headmean = np.kron(np.eye(2), np.ones((64, 64)) / 64).astype(f)
    rot = np.zeros((128, 128), f)
    for m in range(128):
        if m % 32 < 16:
            rot[m + 16, m] = -1
        else:
            rot[m - 16, m] = 1
    inv = f(10000.0) ** (-np.arange(16, dtype=f) / f(16))
    tok = np.arange(256)
    d = np.arange(128) % 64
    pos = np.where((d < 32)[:, None], (tok // 64)[None, :], (tok % 64)[None, :]).astype(f)
    ang = pos * inv[d % 16][:, None]
    rcnt = np.zeros((4, 384), f)
    for g, win in enumerate((2, 4, 8, 16)):
        for t0, n in ((0, 128), (128, 256)):
            t = np.arange(n)
            cnt = np.clip(t + win - win // 2, 0, n) - np.clip(t - win // 2, 0, n)
            rcnt[g, t0:t0 + n] = 1.0 / cnt
    rcnt = np.ascontiguousarray(np.broadcast_to(rcnt, (128, 4, 384)))
    iota = np.ascontiguousarray(np.broadcast_to(np.arange(128, dtype=f), (128, 128)))
    return {"k_ident": ident, "k_headmean": headmean, "k_rot": rot, "k_cos": np.cos(ang).astype(f),
            "k_sin": np.sin(ang).astype(f), "k_rcnt": rcnt, "k_iota": iota}


def kernel(**inputs):
    import numpy as _np
    import concourse.bacc as _bacc
    from concourse import mybir as _mybir
    from concourse.bass_utils import run_bass_kernel_spmd as _run

    nc = _bacc.Bacc("TRN2", target_bir_lowering=False, num_devices=1)
    arrays, args = {}, {}
    for name, a in [(n, inputs[n]) for n in _INS] + list(_tables().items()):
        a = _np.ascontiguousarray(a)
        arrays[f"in_{name}_dram"] = a
        args[name] = nc.dram_tensor(f"in_{name}_dram", a.shape, _mybir.dt.from_np(a.dtype), kind="ExternalInput").ap()
    for i, (name, shape) in enumerate(zip(("y_prompt", "y_sample", "new_k", "new_v"), _OUTS)):
        args[name] = nc.dram_tensor(f"out_{i}_dram", shape, F32, kind="ExternalOutput").ap()
    build_step(nc, **args)
    r = _run(nc, [arrays], core_ids=[0])
    return tuple(r.results[0][f"out_{i}_dram"] for i in range(len(_OUTS)))
```

```python
import concourse.bass as bass
from concourse import mybir
from contextlib import ExitStack, contextmanager

F32 = mybir.dt.float32
F32R = mybir.dt.float32r
BF16 = mybir.dt.bfloat16
U32 = mybir.dt.uint32
ALU = mybir.AluOpType
ACT = mybir.ActivationFunctionType
AX = mybir.AxisListType

P = 128
D = 1024
KC = D // P
NPROMPT, NSAMPLE = 128, 256
T = NPROMPT + NSAMPLE
TT = T // P
SEGS = ((0, NPROMPT, 0), (NPROMPT, NSAMPLE, 1))
LAYERS = 2
EPS = 1e-6
HEADS, TOPK, NK = 8, 16, 128
PICKS = HEADS * TOPK
NEG = -3.0e38
WINDOWS = (2, 4, 8, 16)

R_QG, R_KG, R_PS, R_CW = 0, 1, 2, 6
VROWS = 30
R_N1, R_N2, R_FIN, R_CTX, R_C = 30, 46, 62, 70, 78
VCOLS = 86

STAGES = (("q", 4, 2), ("kvp", 6, 1), ("a_out", 8, 2), ("wq0", 16, 1), ("v0", 128, 1),
          ("c_in", 24, 1), ("c_out", 8, 1), ("wq1", 16, 1), ("v1", 128, 1))
UNIT0, FILLED0, PROJ0, DMAS = {}, {}, {}, {}
_u = _f = _p = 0
for _name, _n, _d in STAGES:
    UNIT0[_name], FILLED0[_name], PROJ0[_name], DMAS[_name] = _u, _f, _p, 16 * _d
    _u += _n
    _f += 16 * _d * _n // 2
    _p += 0 if _name in ("v0", "v1", "a_out", "c_out") else _n
NEXT = {a[0]: b[0] for a, b in zip(STAGES, STAGES[1:])}
COUNT = {s[0]: s[1] for s in STAGES}

MODB = 256
SEGB = D // MODB
MODSEGS = 6
EARLY = 2

S_LEVEL1, S_LEVEL2 = 6, 12
BATCH = 8
TURNS = P // (2 * BATCH)
S_STORE = 8
PIECES = 8
S_REST = P - TT * (S_LEVEL1 + S_LEVEL2) - TT * 2 * TURNS - (TT - 1) * S_STORE


class Steps:

    def __init__(self, eng, sem):
        self.eng, self.sem, self.n, self.extra = eng, sem, 0, 0

    def mark(self, ins):
        ins.then_inc(self.sem, 1)
        self.n += 1

    def wait(self):
        self.eng.wait_ge(self.sem, self.extra + self.n)

    def do(self, ins):
        self.mark(ins)
        self.wait()

    @contextmanager
    def loop(self, turns, per):
        n0 = self.n
        with self.eng.Fori(0, turns) as i:
            self.extra = i * per
            yield i
            self.extra = 0
        assert self.n - n0 == per, (self.n - n0, per)
        self.n = n0 + turns * per


class Marks:

    def __init__(self, sem, names):
        self.sem, self.names, self.at = sem, names, 0

    def mark(self, name, ins):
        assert self.names[self.at] == name, (self.names[self.at], name)
        self.at += 1
        ins.then_inc(self.sem, 1)

    def wait(self, eng, name):
        eng.wait_ge(self.sem, self.names.index(name) + 1)


def build_step(nc, x_prompt, x_sample, cache_k, cache_v, c, c_ctx, mod_w, mod_b, norm1_g, norm2_g,
               a_in_w, a_out_w, q_norm_g, k_norm_g, pool_w, pool_scale, c_in_w, c_conv_w, c_out_w,
               peer_wq, peer_subkeys, peer_u, peer_v, final_g,
               k_ident, k_headmean, k_rot, k_cos, k_sin, k_rcnt, k_iota,
               y_prompt, y_sample, new_k, new_v):
    ctx = ExitStack()
    with ctx:
        def sb(name, shape, dt=F32):
            return ctx.enter_context(nc.sbuf_tensor(name, shape, dt))

        def sem(name):
            return ctx.enter_context(nc.semaphore(name))

        xT = sb("xT", [P, KC, T])
        HH = sb("HH", [P, KC, T], F32R)
        HL = sb("HL", [P, KC, T], F32R)
        RAW = sb("RAW", [P, 2, D])
        WHI = [sb(f"WHI{i}", [P, D], F32R) for i in range(2)]
        WLO = [sb(f"WLO{i}", [P, D], F32R) for i in range(2)]
        URAW = sb("URAW", [P, 2, 4, D // 4])
        UT = sb("UT", [P, 2, D])
        UHI = [sb(f"UHI{i}", [P, D], F32R) for i in range(2)]
        ULO = [sb(f"ULO{i}", [P, D], F32R) for i in range(2)]
        GIN = sb("GIN", [P, 2, T])
        GEL = sb("GEL", [P, 2, T])
        EHI = [sb(f"EHI{i}", [P, T], F32R) for i in range(2)]
        ELO = [sb(f"ELO{i}", [P, T], F32R) for i in range(2)]
        VR = sb("VR", [P, P])
        VT = sb("VT", [P, VCOLS])
        MBT = sb("MBT", [P, LAYERS * 48])
        COND = sb("COND", [P, KC, 2])
        MODR = sb("MODR", [P, 2, KC, MODB])
        MROW = sb("MROW", [2, D])
        MODT = sb("MODT", [P, LAYERS, 48, 2])
        GS = sb("GS", [P, LAYERS, 2, KC, 2])
        IDENT = sb("IDENT", [P, P])
        TABLE = sb("TABLE", [P, 1])
        MEAN1 = sb("MEAN1", [P, P])
        HMEAN = sb("HMEAN", [P, P])
        ROT = sb("ROT", [P, P])
        IOTA = sb("IOTA", [P, P])
        IOTA8 = sb("IOTA8", [P, P, BATCH], BF16)
        EQ1 = sb("EQ1", [P, P, BATCH], BF16)
        SKR = sb("SKR", [P, 4, P])
        SKT = sb("SKT", [P, 4, P])
        I16U = sb("I16U", [P, 16, TOPK], U32)
        FIU = sb("FIU", [P, HEADS, TOPK], U32)
        FAU = sb("FAU", [P, PICKS], U32)
        FBU = sb("FBU", [P, PICKS], U32)
        IT1 = sb("IT1", [P, T], BF16)
        IT2 = sb("IT2", [P, T], BF16)
        GP = sb("GP", [P, 3, T], BF16)
        AR = sb("AR", [P, P * P])

        def ar(at, *dims):
            n = 1
            for d in dims:
                n *= d
            v = AR[:, at:at + n]
            if len(dims) == 2:
                v = v.rearrange("p (a b) -> p a b", a=dims[0])
            if len(dims) == 3:
                v = v.rearrange("p (a b c) -> p a b c", a=dims[0], b=dims[1])
            return v

        XS = ar(0, TT, D)
        Z = ar(0, 10, T)
        QN = ar(3840, 5, T)
        ZS = ar(5760, 5, T)
        VAR = ar(7680, 5, T)
        RQ = ar(9600, 4, NSAMPLE)
        COS, SIN = ar(10880, NSAMPLE), ar(11136, NSAMPLE)
        RCNT = ar(11392, 4, T)
        KALL = ar(12928, T)
        VTOK = ar(13312, 3, P)
        VPAST = ar(13696, P)
        KTOK = ar(13824, P)
        KPAST = ar(13952, P)
        PADW = 432
        XPAD, SUM0, SUM1 = ar(14080, PADW), ar(14512, PADW), ar(14944, PADW)
        MX, NB, SM, RV = ar(15376, 4), ar(15380, 4), ar(15384, 4), ar(15388, 4)
        PW = ar(15392, 4, P)
        PROB = [ar(5760, 4, T), ar(7680, 4, T)]
        PROBT = ar(0, 4, T)
        NB0 = 13312
        SQ = ar(NB0, 2, T)
        MV, RT, NT = (ar(NB0 + (2 + i) * T, T) for i in range(3))
        T1 = ar(NB0 + 6 * T, 2, T)
        QT = ar(0, 16, T)
        SC = ar(6144, 16, NK)
        SC2 = ar(8192, 16, NK)
        V16 = ar(10240, 16, TOPK)
        I16F = ar(10496, 16, TOPK)
        CA = ar(10752, HEADS, 256)
        CA2 = ar(12800, HEADS, 256)
        V2 = ar(14848, HEADS, TOPK)
        FA, FB = ar(14976, PICKS), ar(15104, PICKS)
        ID1, ID2 = ar(15232, PICKS), ar(15360, PICKS)
        EX = ar(15488, HEADS, TOPK)
        GT = ar(15616, HEADS, TOPK)
        ZSUM, ZINV = ar(15744, HEADS), ar(15752, HEADS)
        GRES = ar(15760, P)
        EQ = ar(8192, PICKS, TOPK)
        EQ2 = ar(12800, PICKS, TOPK)
        STAGE = ar(0, P, P)
        CM = ar(0, KC, T)
        GC = ar(3072, T)
        UP = ar(3456, 388)
        YA = ar(3844, 386)
        YT = ar(3072, KC, T)
        YTOK = ar(6144, TT, D)

        PS = ctx.enter_context(nc.psum_tensor("PS", [P, 8, 512], F32))
        GD = nc.dram_tensor("gates_dram", [LAYERS, P, P, T], F32, kind="Internal").ap()

        SD = nc.dram_tensor("gelu_dram", [LAYERS, P, P, T], F32, kind="Internal").ap()

        OH = MODR[:, :, :, :].rearrange("p a b c -> p (a b c)").bitcast(BF16)
        n1 = P * BATCH
        OH2 = [OH[:, k * n1:(k + 1) * n1].rearrange("p (a b) -> p a b", b=BATCH) for k in range(2)]
        OH1 = [[OH[:, (2 + 3 * k + part) * n1:(3 + 3 * k + part) * n1].rearrange("p (a b) -> p a b", b=BATCH)
                for part in range(3)] for k in range(2)]

        s_vec, s_cst, s_x = sem("s_vec"), sem("s_cst"), sem("s_x")
        s_att = sem("s_att")
        s_init = sem("s_init")
        s_vt = sem("s_vt")
        s_act0 = sem("s_act0")
        s_xt, s_xe = sem("s_xt"), sem("s_xe")
        mod_in = [sem(f"mod_in{i}") for i in range(2)]
        s_mrow = sem("s_mrow")
        s_mev = sem("s_mev")
        s_mtr = sem("s_mtr")
        s_mod = sem("s_mod")
        s_sq, s_ss = sem("s_sq"), sem("s_ss")
        s_var, s_rt = sem("s_var"), sem("s_rt")
        s_t1 = sem("s_t1")
        s_hhi, s_hlo = sem("s_hhi"), sem("s_hlo")
        raw_in = [sem(f"raw_in{i}") for i in range(2)]
        s_hi = sem("s_hi")
        s_lo = sem("s_lo")
        s_unit = sem("s_unit")
        s_ev = sem("s_ev")
        s_res = sem("s_res")
        s_pool = sem("s_pool")
        s_pm = sem("s_pm")
        s_dve, s_acts = sem("s_dve"), sem("s_acts")
        s_nkv = sem("s_nkv")
        s_sc, s_scc = sem("s_sc"), sem("s_scc")
        s_l1 = sem("s_l1")
        s_d, s_e = sem("s_d"), sem("s_e")
        s_pick = sem("s_pick")
        s_ptr, s_pte = sem("s_ptr"), sem("s_pte")
        s_pts = sem("s_pts")
        s_oh = sem("s_oh")
        s_gm = sem("s_gm")
        s_gev = sem("s_gev")
        s_gst = sem("s_gst")
        u_in = [sem(f"u_in{i}") for i in range(2)]
        s_tr = sem("s_tr")
        s_uhi = sem("s_uhi")
        s_ulo = sem("s_ulo")
        s_S = sem("s_S")
        s_gel = sem("s_gel")
        s_sst = [sem(f"s_sst{i}") for i in range(2)]
        g_in = [sem(f"g_in{i}") for i in range(2)]
        s_w = sem("s_w")
        s_whi = sem("s_whi")
        s_wlo = sem("s_wlo")
        s_acc = sem("s_acc")
        s_at = sem("s_at")
        s_cm = sem("s_cm")
        s_yt, s_ytr, s_ye = sem("s_yt"), sem("s_ytr"), sem("s_ye")
        s_out = sem("s_out")
        s_free = sem("s_free")
        s_mpe, s_mact, s_mdve = sem("s_mpe"), sem("s_mact"), sem("s_mdve")

        BATCHES = [(qt, j) for qt in range(TT) for j in range(2)]
        NBT = len(BATCHES)
        BESIDE = (1, 4, 6, 7)
        LATE00 = EARLY * SEGB
        LATE1 = 17
        LATE0 = range(LATE00 + len(BESIDE), LATE1)
        LATE2 = range(LATE1 + NBT, MODSEGS * SEGB)
        pe_names = ["hm", "kv", "ktok", "rot", "s0", "s1"]
        for b in range(NBT):
            pe_names += [f"t{b}", f"o{b}"] + ([f"s{b + 2}"] if b + 2 < NBT else [])
        pe_names += [f"pw{g}" for g in range(4)]
        act_names = ["zsq", "root", "kpast", "vtok", "ktok", "e0"]
        for b in range(NBT):
            act_names += ([f"e{b + 1}"] if b + 1 < NBT else []) + [f"pt{b}", f"oh{b}"]
        act_names += [f"ph{g}" for g in range(4)]
        dve_names = ["var", "qn", "rope", "nb0", "p0"]
        for b in range(NBT):
            dve_names += ([f"nb{b + 1}", f"p{b + 1}"] if b + 1 < NBT else []) + [f"ol{b}"]
        dve_names += [f"pl{g}" for g in range(4)]
        mpe, mact, mdve = Marks(s_mpe, pe_names), Marks(s_mact, act_names), Marks(s_mdve, dve_names)

        def chunk_view(x):
            return x.rearrange("p (m c) -> p c m", c=KC)

        block = ctx.enter_context(nc.Block())

        def s_tiles(eng, first, count, step):
            with eng.Fori(first // 2, (first + count) // 2) as i:
                step(i, 0)
                step(i, 1)

        NORM_BANK = (2, 0, 2, 0, 2)

        def filled(stage, pair):
            return FILLED0[stage] + DMAS[stage] * (pair + 1)

        @block.sync
        def _(sp):
            def slot_free(sem_, value):
                sp.wait_ge(sem_, value)
                sp.sem_inc(s_free, 1)

            cols = [(R_N1, norm1_g.rearrange("l (p k) -> p l k", k=KC)),
                    (R_N2, norm2_g.rearrange("l (p k) -> p l k", k=KC)),
                    (R_FIN, final_g.rearrange("(a p k) -> p a k", a=1, k=KC)),
                    (R_CTX, c_ctx.rearrange("(a p k) -> p a k", a=1, k=KC)),
                    (R_C, c.rearrange("a (p k) -> p a k", k=KC))]
            for at, src in cols:
                n = KC * src.shape[1]
                sp.dma_start(VT[:, at:at + n].rearrange("p (l k) -> p l k", k=KC), src).then_inc(s_vec, 16)
            rows = [(R_PS, pool_scale.rearrange("l (k p) -> (l k) p", p=P)),
                    (R_CW, c_conv_w.rearrange("l w (k p) -> (l w k) p", p=P))]
            for at, src in rows:
                sp.dma_start(VR[at:at + src.shape[0], :], src).then_inc(s_vec, 16)
            for at, src in ((R_QG, q_norm_g), (R_KG, k_norm_g)):
                for j in range(2):
                    sp.dma_start(VR[at:at + 1, 64 * j:64 * j + 64], src).then_inc(s_vec, 16)
            sp.dma_start(MBT[:, :].rearrange("p (s k) -> p s k", k=KC), mod_b.rearrange("l (s p k) -> p (l s) k", s=6, k=KC))\
                .then_inc(s_vec, 16)
            sp.dma_start(IDENT[:, :], k_ident).then_inc(s_vec, 16)

            def load_mod(l, b, k):
                sp.dma_start(MODR[:, k, :, :], mod_w[l, :, bass.ds(b * MODB, MODB)]
                             .rearrange("(p k) m -> p k m", k=KC)).then_inc(mod_in[k], 16)

            for k in range(2):
                load_mod(0, k, k)
            sp.dma_start(XS[:, 0, :], x_prompt[0, :, :]).then_inc(s_x, 16)
            sp.dma_start(XS[:, 1:3, :], x_sample[0, :, :].rearrange("(t p) d -> p t d", p=P)).then_inc(s_x, 16)
            sp.dma_start(HMEAN[:, :], k_headmean).then_inc(s_cst, 16)
            sp.dma_start(ROT[:, :], k_rot).then_inc(s_cst, 16)
            sp.dma_start(IOTA[:, :], k_iota).then_inc(s_cst, 16)
            sp.dma_start(SKR[:, :, :], peer_subkeys.rearrange("l s e k -> e (l s) k")).then_inc(s_cst, 16)
            def unit_free(n):
                slot_free(s_lo, n + 1)

            w_in = a_in_w[0, :, :]
            def load_late_mod(first, last):
                for b in range(first, last):
                    sp.wait_ge(s_mrow, b - 1)
                    load_mod(0, b, b % 2)

            def load_q(u):
                n = UNIT0["q"] + u
                unit_free(n)
                dst = RAW[:, n % 2, :].rearrange("p (k m) -> p k m", k=KC)
                for j in range(2):
                    h0 = 64 * (4 * j + u)
                    sp.dma_start(dst[:, :, 64 * j:64 * j + 64],
                                 w_in[:, h0:h0 + 64].rearrange("(p k) m -> p k m", k=KC)).then_inc(raw_in[n % 2], 16)

            for u in range(2):
                load_q(u)
            with sp.Fori(1, EARLY * SEGB // 2 + 1) as i:
                for k in range(2):
                    slot_free(s_mrow, 2 * i - 1 + k)
                    load_mod(0, 2 * i + k, k)
            load_late_mod(LATE00 + 2, LATE0[0] + 2)
            for u in range(2, COUNT["q"]):
                load_q(u)

            def load_units(stage, w, m0):
                with sp.Fori(0, COUNT[stage] // 2) as i:
                    for k in range(2):
                        unit_free(UNIT0[stage] + 2 * i + k)
                        sp.dma_start(RAW[:, k, :].rearrange("p (k m) -> p k m", k=KC),
                                     w[:, bass.ds(m0 + (2 * i + k) * P, P)].rearrange("(p k) m -> p k m", k=KC))\
                            .then_inc(raw_in[k], 16)

            load_units("kvp", w_in, 512)
            sp.wait_ge(s_xe, KC)
            sp.dma_start(COS, k_cos).then_inc(s_att, 16)
            sp.dma_start(SIN, k_sin).then_inc(s_att, 16)
            sp.dma_start(RCNT, k_rcnt).then_inc(s_att, 16)
            sp.wait_ge(s_hlo, KC)
            sp.dma_start(VPAST, cache_v[0, 0, :, :, :].rearrange("s h d -> s (h d)")).then_inc(s_att, 16)
            sp.dma_start(KPAST, cache_k[0, 0, :, :, :].rearrange("s h d -> s (h d)")).then_inc(s_att, 16)
            sp.dma_start(PW, pool_w[0, :, :, :].rearrange("g c d -> c g d")).then_inc(s_att, 16)
            w_o = a_out_w[0, :, :]
            def load_a_out(u):
                unit_free(UNIT0["a_out"] + u)
                for j in range(2):
                    r = 64 * u + 256 * j if u < 4 else 128 * u + 64 * j
                    sp.dma_start(RAW[64 * j:64 * j + 64, u % 2, :], w_o[r:r + 64, :]).then_inc(raw_in[u % 2], 16)

            for u in range(2):
                load_a_out(u)
            load_late_mod(LATE0[0] + 2, MODSEGS * SEGB)
            for u in range(2, KC):
                load_a_out(u)

            def load_u(l, t, k):
                for a in range(4):
                    sp.dma_start(URAW[32 * a:32 * a + 32, k, :, :],
                                 peer_u[l, bass.ds(t * P, P), 256 * a:256 * a + 256].rearrange("(b e) m -> e b m", e=32))\
                        .then_inc(u_in[k], 16)

            def load_v(l, t, k):
                unit_free(UNIT0[f"v{l}"] + t)
                sp.dma_start(RAW[:, k, :], peer_v[l, bass.ds(t * P, P), :]).then_inc(raw_in[k], 16)

            def load_gs(l, t, k):
                for dst, src in ((GIN, GD), (GEL, SD)):
                    sp.dma_start(dst[:, k, :], src[l, bass.ds(t, 1), :, :].rearrange("a p t -> p (a t)")).then_inc(g_in[k], 16)

            def s_step(l, load=True):
                def step(i, k):
                    if load:
                        slot_free(s_tr, P * l + 2 * i + k + 1)
                        load_u(l, 2 * i + k + 2, k)
                    slot_free(s_gel, P * l + 2 * i + k + 1)
                    sp.dma_start(SD[l, bass.ds(2 * i + k - 2, 1), :, :].rearrange("a p t -> p (a t)"), GEL[:, k, :])\
                        .then_inc(s_sst[k], 16)
                return step

            sp.sem_inc(s_sst[0], 16)
            sp.sem_inc(s_sst[1], 16)
            for l in range(LAYERS):
                if l:
                    wc = c_in_w[0, :, :]
                    with sp.Fori(0, 4) as i:
                        for q in range(6):
                            unit_free(UNIT0["c_in"] + 6 * i + q)
                            part = (1, 2, 0)[q % 3]
                            sp.dma_start(RAW[:, q % 2, :].rearrange("p (k m) -> p k m", k=KC),
                                         wc[:, bass.ds(part * D + (2 * i + q // 3) * P, P)]
                                         .rearrange("(p k) m -> p k m", k=KC)).then_inc(raw_in[q % 2], 16)
                    with sp.Fori(0, KC // 2) as i:
                        for k in range(2):
                            unit_free(UNIT0["c_out"] + 2 * i + k)
                            sp.dma_start(RAW[:, k, :], c_out_w[0, bass.ds((2 * i + k) * P, P), :]).then_inc(raw_in[k], 16)
                load_units(f"wq{l}", peer_wq[l, :, :], 0)
                for k in range(2):
                    if l:
                        sp.wait_ge(s_tr, P)
                    load_u(l, k, k)
                for k in range(2):
                    load_v(l, k, k)
                if l == 0:
                    for k in range(2):
                        sp.wait_ge(s_mrow, MODSEGS * SEGB - 1 + k)
                        load_mod(1, k, k)
                for k in range(2):
                    sp.wait_ge(s_tr, P * l + k + 1)
                    load_u(l, k + 2, k)
                at = 0
                for tile in range(TT):
                    n = S_LEVEL1 + S_LEVEL2
                    skip = 0 if tile else 2
                    s_tiles(sp, at + skip, n - skip, s_step(l))
                    at += n
                    if l == 0:
                        pairs = MODSEGS * SEGB // 2
                        part = pairs // TT
                        with sp.Fori(tile * part + 1, min((tile + 1) * part + 1, pairs)) as i:
                            for k in range(2):
                                slot_free(s_mrow, 2 * pairs + 2 * i - 1 + k)
                                load_mod(1, 2 * i + k, k)
                for tile in range(TT):
                    s_tiles(sp, at, 2 * TURNS, s_step(l))
                    at += 2 * TURNS
                    sp.wait_ge(s_gev, 4 + 32 * (TT * l + tile + 1))

                    def store_step(i, k):
                        n = P // PIECES
                        first = (2 * i + k - at) * n
                        sp.dma_start(GD[l, bass.ds(first, n), :, tile * P:(tile + 1) * P].rearrange("i p t -> p i t"),
                                     STAGE[:, bass.ds(first, n), :]).then_inc(s_gst, 16)
                        s_step(l)(i, k)

                    s_tiles(sp, at, PIECES, store_step)
                    at += PIECES
                    if tile + 1 < TT and S_STORE > PIECES:
                        s_tiles(sp, at, S_STORE - PIECES, s_step(l))
                        at += S_STORE - PIECES
                if at < P - 2:
                    s_tiles(sp, at, P - 2 - at, s_step(l))
                for i in (P // 2 - 1, P // 2):
                    for k in range(2):
                        s_step(l, load=False)(i, k)
                sp.wait_ge(s_gst, 16 * PIECES * TT * (l + 1))
                for k in range(2):
                    sp.wait_ge(s_sst[k], 16 * (P // 2 * (l + 1) + 1))
                for k in range(2):
                    load_gs(l, k, k)
                with sp.Fori(1, P // 2) as i:
                    for k in range(2):
                        t = 2 * i + k
                        slot_free(s_wlo, P * l + t - 1)
                        load_gs(l, t, k)
                        load_v(l, t, k)
            sp.wait_ge(s_ye, 6)
            sp.dma_start(y_prompt[0, :, :], YTOK[:, 0, :]).then_inc(s_out, 16)
            sp.dma_start(y_sample[0, :, :].rearrange("(t p) d -> p t d", p=P), YTOK[:, 1:3, :]).then_inc(s_out, 16)
            sp.wait_ge(s_nkv, 32)
            sp.wait_ge(s_out, 32)

        @block.gpsimd
        def _(pool):
            own = Steps(pool, s_pool)
            pool.memset(MEAN1[:, :], 1.0 / D).then_inc(s_cst, 16)
            pool.wait_ge(s_ev, 2 + 10)
            pool.wait_ge(s_att, 16 * 6)
            pool.wait_ge(s_hlo, KC)
            own.do(pool.memset(XPAD, 0.0))
            pads = ((8, 0, NPROMPT), (8 + NPROMPT + 16, NPROMPT, NSAMPLE))
            for g, win in enumerate(WINDOWS):
                zg = Z[:, 6 + g, :]
                for at, t0, n in pads:
                    own.mark(pool.tensor_copy(XPAD[:, at:at + n], zg[:, t0:t0 + n]))
                own.wait()
                src, bufs, half = XPAD, [SUM0, SUM1], 1
                while half < win:
                    dst = bufs[0]
                    bufs.reverse()
                    n = PADW - 2 * half + 1
                    own.do(pool.tensor_tensor(dst[:, 0:n], src[:, 0:n], src[:, half:half + n], ALU.add))
                    src, half = dst, 2 * half
                out = bufs[0]
                for at, t0, n in pads:
                    a = at - win // 2
                    own.mark(pool.tensor_tensor(out[:, t0:t0 + n], src[:, a:a + n], RCNT[:, g, t0:t0 + n], ALU.mult))
                own.wait()
                pool.tensor_tensor(zg, out[:, 0:T], zg, ALU.subtract).then_inc(s_pm, 1)
                pool.wait_ge(s_pm, g + 1)
            pool.sem_inc(s_ulo, 2)
            with pool.Fori(0, LAYERS * P // 2) as i:
                for k in range(2):
                    pool.wait_ge(s_uhi, 2 * i + k + 1)
                    pool.tensor_tensor(ULO[k][:, :], UT[:, k, :], UHI[k][:, :].bitcast(F32), ALU.subtract).then_inc(s_ulo, 1)

        @block.scalar
        def _(act):
            own = Steps(act, s_acts)
            nc.scalar.sem_inc(s_ev, 2)
            nc.scalar.sem_inc(s_gev, 4)
            nc.scalar.sem_inc(s_mod, 1)
            nc.scalar.sem_inc(s_gel, 2)
            act.wait_ge(s_vt, 1)
            nc.scalar.activation(COND[:, :, :].rearrange("p k c -> p c k"),
                                 VT[:, R_CTX:R_CTX + 16].rearrange("p (c k) -> p c k", c=2), ACT.Silu).then_inc(s_act0, 1)

            def mod(l, first, last):
                with act.Fori(first, last) as i:
                    for q in range(SEGB):
                        act.wait_ge(s_mrow, SEGB * (MODSEGS * l + i) + q + 1)
                        nc.scalar.activation(MROW[:, q * MODB:(q + 1) * MODB], PS[0:2, 5 + q % 2, 0:MODB], ACT.Copy)\
                            .then_inc(s_mev, 1)
                    act.wait_ge(s_mtr, MODSEGS * l + i + 1)
                    nc.scalar.activation(MODT[:, l, bass.ds(KC * i, KC), :],
                                         PS[:, 7, 0:2 * KC].rearrange("p (a b) -> p a b", b=2), ACT.Copy).then_inc(s_mod, 1)

            def late_mod(b, bank):
                act.wait_ge(s_mrow, b + 1)
                q = b % SEGB
                nc.scalar.activation(MROW[:, q * MODB:(q + 1) * MODB], PS[0:2, bank, 0:MODB], ACT.Copy).then_inc(s_mev, 1)
                if q == SEGB - 1:
                    i = b // SEGB
                    act.wait_ge(s_mtr, i + 1)
                    nc.scalar.activation(MODT[:, 0, KC * i:KC * (i + 1), :],
                                         PS[:, bank + 1, 0:2 * KC].rearrange("p (a b) -> p a b", b=2), ACT.Copy).then_inc(s_mod, 1)

            def norm_root(n):
                for k in range(KC):
                    q = KC * n + k
                    if n or k >= 2:
                        act.wait_ge(s_ss, q - 1)
                    if n == 0:
                        act.wait_ge(s_xe, k + 1)
                    else:
                        act.wait_ge(s_res, KC * (n - 1) + k + 1)
                    nc.scalar.activation(SQ[:, k % 2, :], xT[:, k, :], ACT.Square).then_inc(s_sq, 1)
                act.wait_ge(s_var, n + 1)
                nc.scalar.activation(RT, MV, ACT.Abs_reciprocal_sqrt).then_inc(s_rt, 1)

            def norm(n):
                l, which = divmod(n, 2)
                if n:
                    norm_root(n)
                for k in range(KC):
                    act.wait_ge(s_t1, q0 := KC * n + k + 1)
                    for t0, m, cnd in SEGS:
                        ins = nc.scalar.activation(HH[:, k, t0:t0 + m], T1[:, k % 2, t0:t0 + m], ACT.Identity,
                                                   bias=MODT[:, l, 24 * which + k, cnd:cnd + 1])
                    ins.then_inc(s_hhi, 1)
                    if n == 0 and k in BESIDE:
                        late_mod(LATE00 + BESIDE.index(k), 5)

            def hi(stage, pair, k):
                act.wait_ge(raw_in[k], filled(stage, pair))
                act.wait_ge(s_unit, UNIT0[stage] + 2 * pair + k + 1)
                if stage in ("a_out", "c_out"):
                    nc.scalar.activation(WHI[k][:, :].rearrange("p (c m) -> p c m", c=KC), chunk_view(RAW[:, k, :]), ACT.Copy)\
                        .then_inc(s_hi, 1)
                else:
                    nc.scalar.activation(WHI[k][:, :], RAW[:, k, :], ACT.Copy).then_inc(s_hi, 1)

            def his(stage, evacuate=None, fresh=False):
                def turn(i, second=True):
                    if second:
                        hi(stage, i, 1)
                    if evacuate:
                        evacuate(2 * i, 0)
                    hi(stage, i + 1, 0)
                    if evacuate:
                        evacuate(2 * i + 1, 1)

                if fresh:
                    turn(0, second=False)
                if COUNT[stage] // 2 - 1 > fresh:
                    with act.Fori(int(fresh), COUNT[stage] // 2 - 1) as i:
                        turn(i)
                i = COUNT[stage] // 2 - 1
                hi(stage, i, 1)
                if evacuate:
                    evacuate(2 * i, 0)
                hi(NEXT[stage], 0, 0)
                if evacuate:
                    evacuate(2 * i + 1, 1)

            def to_view(view, stage, first):
                def evacuate(u, k):
                    act.wait_ge(s_unit, UNIT0[stage] + u + 3)
                    nc.scalar.activation(view[:, bass.ds(first + u, 1), :].rearrange("p a t -> p (a t)"),
                                         PS[:, k, 0:T], ACT.Copy).then_inc(s_ev, 1)
                return evacuate

            mod(0, 0, 1)
            norm_root(0)
            hi("q", 0, 0)
            hi("q", 0, 1)
            mod(0, 1, EARLY)
            act.wait_ge(s_init, 2)
            nc.scalar.activation(SKT[:, :, :].rearrange("p a b -> p (a b)"), PS[:, 4, :], ACT.Copy).then_inc(s_act0, 1)
            norm(0)
            his("q", to_view(Z, "q", 0), fresh=True)
            his("kvp", to_view(Z, "kvp", 4))

            act.wait_ge(s_ev, 2 + 10)
            mact.mark("zsq", nc.scalar.activation(ZS[:, :, :], Z[:, 0:5, :], ACT.Square))
            mdve.wait(act, "var")
            mact.mark("root", nc.scalar.activation(ZS[:, :, :], VAR[:, :, :], ACT.Abs_reciprocal_sqrt))
            mpe.wait(act, "kv")
            mact.mark("kpast", nc.scalar.activation(KALL[:, NSAMPLE:T], PS[:, 7, 0:P], ACT.Copy))
            mact.mark("vtok", nc.scalar.activation(VTOK[:, :, :], PS[:, 7, P:512].rearrange("p (a b) -> p a b", a=3), ACT.Copy))
            for b in LATE0:
                late_mod(b, 0)
            mpe.wait(act, "ktok")
            mact.mark("ktok", nc.scalar.activation(KTOK, PS[:, 0, 0:P], ACT.Copy))
            mact.wait(act, "ktok")
            act.dma_start(new_k[0, 0, :, :, :].rearrange("s h d -> s (h d)"), KTOK).then_inc(s_nkv, 16)
            act.dma_start(new_v[0, 0, :, :, :].rearrange("s h d -> s (h d)"), VTOK[:, 0, :]).then_inc(s_nkv, 16)
            def exponents(b):
                n = P if BATCHES[b][0] == 0 else T
                mdve.wait(act, f"nb{b}")
                for q in range(4):
                    ins = nc.scalar.activation(PROB[b % 2][:, q, 0:n], PS[:, q, 0:n], ACT.Exp, bias=NB[:, q:q + 1],
                                               scale=0.125, accum_out=SM[:, q:q + 1])
                mact.mark(f"e{b}", ins)

            exponents(0)
            for b, (qt, j) in enumerate(BATCHES):
                n = P if qt == 0 else T
                if b + 1 < NBT:
                    exponents(b + 1)
                mpe.wait(act, f"t{b}")
                mact.mark(f"pt{b}", nc.scalar.activation(PROBT[:, :, 0:n], PS[:, 4:8, 0:n], ACT.Copy))
                mpe.wait(act, f"o{b}")
                rows = slice(64 * j, 64 * j + 64)
                mact.mark(f"oh{b}", nc.scalar.activation(HH[rows, 0:4, qt * P:qt * P + P],
                                                         PS[rows, 4, :].rearrange("p (a b) -> p a b", a=4), ACT.Copy))
                late_mod(LATE1 + b, 5)
            for b in LATE2:
                late_mod(b, 5)
            for g in range(4):
                mpe.wait(act, f"pw{g}")
                mact.mark(f"ph{g}", nc.scalar.activation(HH[:, 4 + g, :], PS[:, g, 0:T], ACT.Copy,
                                                         scale=VT[:, R_PS + g:R_PS + g + 1]))
            his("a_out")

            for l in range(LAYERS):
                if l:
                    hi("c_in", 0, 1)
                    norm(2)
                    his("c_in", fresh=True)
                    for k in range(0, KC, 2):
                        act.wait_ge(s_cm, KC)
                        nc.scalar.activation(HH[:, k:k + 2, :], CM[:, k:k + 2, :], ACT.Copy).then_inc(s_hhi, 1)
                    his("c_out")
                else:
                    act.wait_ge(s_nkv, 32)
                hi(f"wq{l}", 0, 1)
                norm(2 * l + 1)
                his(f"wq{l}", to_view(QT, f"wq{l}", 0), fresh=True)
                def copy_scores(tile):
                    g = TT * l + tile
                    act.wait_ge(s_sc, g + 1)
                    if tile:
                        act.wait_ge(s_l1, g)
                    nc.scalar.activation(SC[:, :, :].rearrange("p (a b) c -> p a (b c)", a=4), PS[:, 3:7, :], ACT.Copy)\
                        .then_inc(s_scc, 1)

                def u_hi(i, k):
                    g = P * l + 2 * i + k
                    act.wait_ge(s_tr, g + 1)
                    act.wait_ge(s_S, g + 1)
                    nc.scalar.activation(UHI[k][:, :], UT[:, k, :], ACT.Copy).then_inc(s_uhi, 1)

                def gelu(i, k):
                    act.wait_ge(s_S, P * l + 2 * i + k + 3)
                    act.wait_ge(s_sst[k], 16 * (P // 2 * l + i + 1))
                    nc.scalar.activation(GEL[:, k, :], PS[:, k, 0:T], ACT.Gelu).then_inc(s_gel, 1)

                def s_step(i, k):
                    u_hi(i + 1, k)
                    gelu(i, k)

                def gates(tile, turn, group):
                    act.wait_ge(s_gm, 4 + 32 * (TT * l + tile) + 4 * turn + group + 1)
                    nc.scalar.activation(STAGE[:, :, bass.ds(16 * turn + 4 * group, 4)].rearrange("p i t -> p t i"),
                                         PS[:, 3 + group, :].rearrange("p (t i) -> p t i", t=4), ACT.Copy).then_inc(s_gev, 1)

                def gelu_table():
                    nc.scalar.activation(TABLE[:, :], IDENT[:, 0:1], ACT.Gelu)

                gelu_table()
                copy_scores(0)
                u_hi(0, 0)
                u_hi(0, 1)
                at = 0
                for tile in range(TT):
                    g = TT * l + tile
                    s_tiles(act, at, S_LEVEL1, s_step)
                    at += S_LEVEL1
                    if tile + 1 < TT:
                        copy_scores(tile + 1)
                    s_tiles(act, at, S_LEVEL2, s_step)
                    at += S_LEVEL2
                    act.wait_ge(s_d, g + 1)
                    nc.scalar.activation(EX[:, :, :], EX[:, :, :], ACT.Exp).then_inc(s_e, 1)
                    gelu_table()
                    if l == 0:
                        mod(1, 2 * tile, 2 * tile + 2)
                    act.wait_ge(s_ptr, g + 1)
                    cols = slice(tile * P, tile * P + P)
                    nc.scalar.activation(IT1[:, cols], PS[:, 7, 0:P], ACT.Copy)
                    nc.scalar.activation(IT2[:, cols], PS[:, 7, P:2 * P], ACT.Copy).then_inc(s_pte, 1)
                for tile in range(TT):
                    if tile:
                        act.wait_ge(s_gst, 16 * PIECES * (TT * l + tile))
                    with act.Fori(0, TURNS) as i:
                        for k in range(2):
                            s_step(at // 2 + i, k)
                            gates(tile, i, 2 * k)
                            gates(tile, i, 2 * k + 1)
                    at += 2 * TURNS
                    if tile + 1 < TT:
                        s_tiles(act, at, S_STORE, s_step)
                        at += S_STORE
                s_tiles(act, at, S_REST - 2, s_step)
                gelu(P // 2 - 1, 0)
                gelu(P // 2 - 1, 1)

                def w_hi(i, k):
                    t = 2 * i + k
                    act.wait_ge(s_w, P * l + t + 1)
                    act.wait_ge(s_unit, UNIT0[f"v{l}"] + t + 1)
                    nc.scalar.activation(EHI[k][:, :], GEL[:, k, :], ACT.Copy).then_inc(s_whi, 1)

                v = f"v{l}"
                w_hi(0, 0)
                with act.Fori(0, P // 2 - 1) as i:
                    w_hi(i, 1)
                    hi(v, i, 1)
                    w_hi(i + 1, 0)
                    hi(v, i + 1, 0)
                w_hi(P // 2 - 1, 1)
                hi(v, P // 2 - 1, 1)
                if l == 0:
                    hi("c_in", 0, 0)
                act.wait_ge(s_unit, UNIT0[v] + P + 2)
                for tile in range(TT):
                    nc.scalar.activation(XS[:, tile, :].rearrange("p (a b) -> p a b", a=2),
                                         PS[:, 2 + 2 * tile:4 + 2 * tile, :], ACT.Copy).then_inc(s_acc, 1)
            norm_root(4)
            for q in range(6):
                act.wait_ge(s_ytr, q + 1)
                nc.scalar.activation(chunk_view(YTOK[:, q // 2, :])[:, 4 * (q % 2):4 * (q % 2) + 4, :],
                                     PS[:, 3 + q % 2, :].rearrange("p (c m) -> p c m", c=4), ACT.Copy).then_inc(s_ye, 1)

        @block.tensor
        def _(pe):
            nc.tensor.sem_inc(s_unit, 2)
            nc.tensor.sem_inc(s_gm, 4)
            nc.tensor.sem_inc(s_S, 2)
            pe.wait_ge(s_vec, 16 * 13)
            nc.tensor.transpose(PS[:, 3, 0:VROWS], VR[0:VROWS, :], IDENT[0:VROWS, 0:VROWS]).then_inc(s_init, 1)
            pe.wait_ge(s_act0, 1)

            def mod(l, first, last):
                with pe.Fori(first, last) as i:
                    row = MODSEGS * l + i
                    for q in range(SEGB):
                        pe.wait_ge(mod_in[q % 2], 8 * SEGB * row + 16 * (q // 2 + 1))
                        if q >= 2:
                            pe.wait_ge(s_mev, SEGB * row + q - 1)
                        for kc in range(KC):
                            ins = nc.tensor.matmul(PS[0:2, 5 + q % 2, 0:MODB], COND[:, kc, :], MODR[:, q % 2, kc, :],
                                                   start=kc == 0, stop=kc == KC - 1)
                        ins.then_inc(s_mrow, 1)
                    pe.wait_ge(s_mod, row + 1)
                    pe.wait_ge(s_mev, SEGB * (row + 1))
                    for m in range(KC):
                        ins = nc.tensor.matmul(PS[:, 7, 2 * m:2 * m + 2], chunk_view(MROW[:, :])[:, m, :], IDENT[0:2, 0:2],
                                               start=True, stop=True)
                    ins.then_inc(s_mtr, 1)

            def late_mod(b, bank):
                q = b % SEGB
                pe.wait_ge(mod_in[b % 2], 16 * (b // 2 + 1))
                pe.wait_ge(s_mev, b)
                for kc in range(KC):
                    ins = nc.tensor.matmul(PS[0:2, bank, 0:MODB], COND[:, kc, :], MODR[:, b % 2, kc, :],
                                           start=kc == 0, stop=kc == KC - 1)
                ins.then_inc(s_mrow, 1)
                if q == SEGB - 1:
                    row = b // SEGB
                    pe.wait_ge(s_mod, row + 1)
                    pe.wait_ge(s_mev, b + 1)
                    for m in range(KC):
                        ins = nc.tensor.matmul(PS[:, bank + 1, 2 * m:2 * m + 2], chunk_view(MROW[:, :])[:, m, :], IDENT[0:2, 0:2],
                                               start=True, stop=True)
                    ins.then_inc(s_mtr, 1)

            def late_mod_left(b):
                pe.wait_ge(s_mev, b + 1)
                pe.wait_ge(s_mod, 1 + (b + 1) // SEGB)

            def norm(n):
                for k in range(KC):
                    pe.wait_ge(s_sq, KC * n + k + 1)
                    nc.tensor.matmul(PS[:, NORM_BANK[n], 0:T], MEAN1[:, :], SQ[:, k % 2, :], start=k == 0, stop=k == KC - 1)\
                        .then_inc(s_ss, 1)

            def project(stage, chunks=None):
                if chunks is not None:
                    pe.wait_ge(s_lo, UNIT0[stage] + 4)
                    pe.wait_ge(s_ev, PROJ0[stage] + 2)
                    for k in range(KC):
                        pe.wait_ge(s_hlo, chunks + k + 1)
                        cols = slice(k * P, k * P + P)
                        for s in range(2):
                            nc.tensor.matmul(PS[:, s, 0:T], WHI[s][:, cols], HH[:, k, :], start=k == 0, stop=False)
                            nc.tensor.matmul(PS[:, s, 0:T], WHI[s][:, cols], HL[:, k, :], start=False, stop=False)
                            ins = nc.tensor.matmul(PS[:, s, 0:T], WLO[s][:, cols], HH[:, k, :], start=False, stop=k == KC - 1)
                            if k == KC - 1:
                                ins.then_inc(s_unit, 1)
                with pe.Fori(0 if chunks is None else 1, COUNT[stage] // 2) as i:
                    for s in range(2):
                        u = 2 * i + s
                        pe.wait_ge(s_lo, UNIT0[stage] + u + 3)
                        pe.wait_ge(s_ev, PROJ0[stage] + u + 1)
                        for k in range(KC):
                            cols = slice(k * P, k * P + P)
                            nc.tensor.matmul(PS[:, s, 0:T], WHI[s][:, cols], HH[:, k, :], start=k == 0, stop=False)
                            nc.tensor.matmul(PS[:, s, 0:T], WHI[s][:, cols], HL[:, k, :], start=False, stop=False)
                            ins = nc.tensor.matmul(PS[:, s, 0:T], WLO[s][:, cols], HH[:, k, :], start=False, stop=k == KC - 1)
                        ins.then_inc(s_unit, 1)

            def project_out(stage):
                for u in range(KC):
                    pe.wait_ge(s_lo, UNIT0[stage] + u + 3)
                    for k in range(KC):
                        cols = slice(k * P, k * P + P)
                        nc.tensor.matmul(PS[:, k, 0:T], WHI[u % 2][:, cols], HH[:, u, :], start=u == 0, stop=False)
                        nc.tensor.matmul(PS[:, k, 0:T], WHI[u % 2][:, cols], HL[:, u, :], start=False, stop=False)
                        ins = nc.tensor.matmul(PS[:, k, 0:T], WLO[u % 2][:, cols], HH[:, u, :], start=False, stop=u == KC - 1)
                    ins.then_inc(s_unit, 1)

            mod(0, 0, 1)
            pe.wait_ge(s_cst, 16 * 5)
            for q in range(4):
                ins = nc.tensor.transpose(PS[:, 4, q * P:q * P + P], SKR[:, q, :], IDENT[:, :])
            ins.then_inc(s_init, 1)
            pe.wait_ge(s_x, 32)
            for k in range(KC):
                if k >= 2:
                    pe.wait_ge(s_xe, k - 1)
                for tile in range(TT):
                    ins = nc.tensor.transpose(PS[:, k % 2, tile * P:tile * P + P], chunk_view(XS[:, tile, :])[:, k, :], IDENT[:, :])
                ins.then_inc(s_xt, 1)
            norm(0)
            mod(0, 1, EARLY)
            for b in range(LATE00, LATE0[0]):
                late_mod(b, 5)
            project("q", 0)
            project("kvp")

            mact.wait(pe, "zsq")
            late_mod_left(LATE0[0] - 1)
            for q in range(5):
                ins = nc.tensor.matmul(PS[:, 2 + q, 0:T], HMEAN[:, :], ZS[:, q, :], start=True, stop=True)
            mpe.mark("hm", ins)
            pe.wait_ge(s_att, 16 * 6)
            nc.tensor.transpose(PS[:, 7, 0:P], KPAST, IDENT[:, :])
            for tile in range(TT):
                ins = nc.tensor.transpose(PS[:, 7, (tile + 1) * P:(tile + 2) * P], Z[:, 5, tile * P:tile * P + P], IDENT[:, :])
            mpe.mark("kv", ins)
            for b in LATE0:
                late_mod(b, 0)
            late_mod_left(LATE1 - 1)
            mdve.wait(pe, "qn")
            mpe.mark("ktok", nc.tensor.transpose(PS[:, 0, 0:P], QN[:, 4, 0:P], IDENT[:, :]))
            for q in range(5):
                ins = nc.tensor.matmul(PS[:, 2 + q, 0:NSAMPLE], ROT[:, :], QN[:, q, NPROMPT:T], start=True, stop=True)
            mpe.mark("rot", ins)

            def scores(b):
                qt, j = BATCHES[b]
                rows = slice(64 * j, 64 * j + 64)
                if b:
                    mact.wait(pe, f"e{b - 1}")
                else:
                    mact.wait(pe, "ktok")
                if b == 2:
                    mdve.wait(pe, "rope")
                    mact.wait(pe, "kpast")
                for q in range(4):
                    if qt == 0:
                        ins = nc.tensor.matmul(PS[:, q, 0:P], QN[rows, q, 0:P], QN[rows, 4, 0:P], start=True, stop=True)
                    else:
                        ins = nc.tensor.matmul(PS[:, q, 0:T], RQ[rows, q, (qt - 1) * P:qt * P], KALL[rows, :], start=True, stop=True)
                mpe.mark(f"s{b}", ins)

            mdve.wait(pe, "rope")
            scores(0)
            scores(1)
            for b, (qt, j) in enumerate(BATCHES):
                rows = slice(64 * j, 64 * j + 64)
                nkt = 1 if qt == 0 else 3
                if b:
                    mdve.wait(pe, f"ol{b - 1}")
                    late_mod_left(LATE1 + b - 1)
                else:
                    mact.wait(pe, "vtok")
                mdve.wait(pe, f"p{b}")
                for q in range(4):
                    for kt in range(nkt):
                        ins = nc.tensor.transpose(PS[:, 4 + q, kt * P:kt * P + P], PROB[b % 2][:, q, kt * P:kt * P + P], IDENT[:, :])
                mpe.mark(f"t{b}", ins)
                mact.wait(pe, f"pt{b}")
                for kt in range(nkt):
                    if qt == 0:
                        val = VTOK[:, 0, rows]
                    else:
                        val = VTOK[:, 1 + kt, rows] if kt < 2 else VPAST[:, rows]
                    ins = nc.tensor.matmul(PS[rows, 4, :], val, PROBT[:, :, kt * P:kt * P + P], start=kt == 0, stop=kt == nkt - 1)
                mpe.mark(f"o{b}", ins)
                if b + 2 < NBT:
                    scores(b + 2)
                late_mod(LATE1 + b, 5)
            for b in LATE2:
                late_mod(b, 5)
            mact.wait(pe, f"e{NBT - 1}")
            for g in range(4):
                pe.wait_ge(s_pm, g + 1)
                mpe.mark(f"pw{g}", nc.tensor.matmul(PS[:, g, 0:T], PW[:, g, :], Z[:, 6 + g, :], start=True, stop=True))
            mdve.wait(pe, "pl3")
            late_mod_left(MODSEGS * SEGB - 1)
            project_out("a_out")

            for l in range(LAYERS):
                if l:
                    norm(2)
                    project("c_in", 2 * KC)
                    pe.wait_ge(s_hlo, 3 * KC + 4)
                    project_out("c_out")
                norm(2 * l + 1)
                project(f"wq{l}", 3 * KC + 4 if l else KC)

                def tile_scores(tile):
                    if tile:
                        pe.wait_ge(s_scc, TT * l + tile)
                    else:
                        pe.wait_ge(s_ev, 2 + PROJ0[f"wq{l}"] + 16)
                    for u in range(16):
                        ins = nc.tensor.matmul(PS[:, 3 + u // 4, (u % 4) * P:(u % 4) * P + P],
                                               QT[:, u, tile * P:tile * P + P], SKT[:, 2 * l + u % 2, :], start=True, stop=True)
                    ins.then_inc(s_sc, 1)

                def turn_picks(tile):
                    g = TT * l + tile
                    pe.wait_ge(s_pick, g + 1)
                    if l == 0:
                        pe.wait_ge(s_mod, 1 + MODSEGS + (tile + 1) * MODSEGS // TT)
                    if g:
                        pe.wait_ge(s_pte, g)
                        pe.wait_ge(s_pts, g)
                    for q, src in enumerate((ID1, ID2, GT.rearrange("p a b -> p (a b)"))):
                        ins = nc.tensor.transpose(PS[:, 7, q * P:q * P + P], src, IDENT[:, :])
                    ins.then_inc(s_ptr, 1)

                def s_tile(i, k):
                    g = P * l + 2 * i + k
                    pe.wait_ge(s_ulo, g + 3)
                    pe.wait_ge(s_gel, g + 1)
                    for c_ in range(KC):
                        cols = slice(c_ * P, c_ * P + P)
                        nc.tensor.matmul(PS[:, k, 0:T], UHI[k][:, cols], HH[:, c_, :], start=c_ == 0, stop=False)
                        nc.tensor.matmul(PS[:, k, 0:T], UHI[k][:, cols], HL[:, c_, :], start=False, stop=False)
                        ins = nc.tensor.matmul(PS[:, k, 0:T], ULO[k][:, cols], HH[:, c_, :], start=False, stop=c_ == KC - 1)
                    ins.then_inc(s_S, 1)

                def gates(tile, turn, k):
                    b = 2 * TURNS * (TT * l + tile) + 2 * turn + k
                    pe.wait_ge(s_oh, b + 1)
                    for group in range(2):
                        pe.wait_ge(s_gev, 2 * b + group + 1)
                        for q in range(4):
                            for part in range(3):
                                tok = 4 * group + q
                                ins = nc.tensor.matmul(PS[:, 3 + 2 * k + group, q * P:q * P + P], OH2[k][:, :, tok],
                                                       OH1[k][part][:, :, tok], start=part == 0, stop=part == 2)
                        ins.then_inc(s_gm, 1)

                def v_tile(i, k, first=False, last=False):
                    t = 2 * i + k
                    pe.wait_ge(s_wlo, P * l + t + 1)
                    pe.wait_ge(s_lo, UNIT0[f"v{l}"] + t + 3)
                    for tile in range(TT):
                        tok = slice(tile * P, tile * P + P)
                        for q, (e, w) in enumerate(((EHI, WHI), (EHI, WLO), (ELO, WHI))):
                            for half in range(2):
                                ins = nc.tensor.matmul(PS[:, 2 + 2 * tile + half, :], e[k][:, tok],
                                                       w[k][:, 512 * half:512 * half + 512],
                                                       start=first and q == 0, stop=last and q == 2)
                    ins.then_inc(s_unit, 1)

                pe.wait_ge(s_act0, 2)
                tile_scores(0)
                at = 0
                for tile in range(TT):
                    s_tiles(pe, at, S_LEVEL1, s_tile)
                    at += S_LEVEL1
                    if tile + 1 < TT:
                        tile_scores(tile + 1)
                    s_tiles(pe, at, S_LEVEL2, s_tile)
                    at += S_LEVEL2
                    if l == 0:
                        pe.wait_ge(s_scc, min(tile + 2, TT))
                        if tile:
                            pe.wait_ge(s_pte, tile)
                            pe.wait_ge(s_pts, tile)
                        mod(1, 2 * tile, 2 * tile + 2)
                    turn_picks(tile)
                for tile in range(TT):
                    with pe.Fori(0, TURNS) as i:
                        for k in range(2):
                            s_tile(at // 2 + i, k)
                            gates(tile, i, k)
                    at += 2 * TURNS
                    if tile + 1 < TT:
                        s_tiles(pe, at, S_STORE, s_tile)
                        at += S_STORE
                s_tiles(pe, at, S_REST, s_tile)
                pe.wait_ge(s_gev, 4 + 32 * TT * (l + 1))
                v_tile(0, 0, first=True)
                v_tile(0, 1)
                with pe.Fori(1, P // 2 - 1) as i:
                    v_tile(i, 0)
                    v_tile(i, 1)
                v_tile(P // 2 - 1, 0)
                v_tile(P // 2 - 1, 1, last=True)
                pe.wait_ge(s_acc, TT * (l + 1))
                for k in range(KC):
                    if k >= 2:
                        pe.wait_ge(s_res, KC * (2 * l + 1) + k - 1)
                    if k == 0:
                        pe.wait_ge(s_gel, P * (l + 1) + 2)
                    for tile in range(TT):
                        ins = nc.tensor.transpose(PS[:, k % 2, tile * P:tile * P + P], chunk_view(XS[:, tile, :])[:, k, :], IDENT[:, :])
                    ins.then_inc(s_at, 1)
            norm(4)
            for q in range(6):
                tile, half = divmod(q, 2)
                pe.wait_ge(s_yt, KC)
                if q >= 2:
                    pe.wait_ge(s_ye, q - 1)
                for m in range(4):
                    ins = nc.tensor.transpose(PS[:, 3 + half, m * P:m * P + P], YT[:, 4 * half + m, tile * P:tile * P + P], IDENT[:, :])
                ins.then_inc(s_ytr, 1)

        @block.vector
        def _(dve):
            V = nc.vector
            own = Steps(dve, s_dve)
            V.sem_inc(s_lo, 2)
            dve.wait_ge(s_init, 1)
            V.tensor_copy(VT[:, 0:VROWS], PS[:, 3, 0:VROWS]).then_inc(s_vt, 1)
            for k in range(KC):
                dve.wait_ge(s_xt, k + 1)
                V.tensor_copy(xT[:, k, :], PS[:, k % 2, 0:T]).then_inc(s_xe, 1)
            dve.wait_ge(s_cst, 16 * 5)
            own.mark(V.tensor_copy(IOTA8[:, :, :], IOTA[:, :].unsqueeze(2).to_broadcast([P, P, BATCH])))

            def modulation(l, first, last):
                cols = slice(KC * first, KC * last)
                dve.wait_ge(s_mod, 1 + MODSEGS * l + last)
                dve.wait_ge(s_vt, 1)
                own.do(V.tensor_tensor(MODT[:, l, cols, :], MODT[:, l, cols, :],
                                       MBT[:, 48 * l + cols.start:48 * l + cols.stop].unsqueeze(2)
                                       .to_broadcast([P, KC * (last - first), 2]), ALU.add))
                for which, r in ((0, R_N1), (1, R_N2)):
                    scale = 3 * which + 1
                    if first <= scale < last:
                        own.do(V.scalar_tensor_tensor(out=GS[:, l, which, :, :], in0=MODT[:, l, KC * scale:KC * scale + KC, :],
                                                      scalar=1.0, in1=VT[:, r + 8 * l:r + 8 * l + 8].unsqueeze(2).to_broadcast([P, KC, 2]),
                                                      op0=ALU.add, op1=ALU.mult))

            def rsqrt_step(y, v, t):
                own.do(V.tensor_tensor(t, y, y, ALU.mult))
                own.do(V.tensor_tensor(t, t, v, ALU.mult))
                own.do(V.tensor_scalar(t, t, -0.5, 1.5, ALU.mult, ALU.add))
                own.do(V.tensor_tensor(y, y, t, ALU.mult))

            def norm_root(n):
                dve.wait_ge(s_ss, KC * (n + 1))
                V.tensor_scalar(MV, PS[:, NORM_BANK[n], 0:T], EPS, None, ALU.add).then_inc(s_var, 1)
                dve.wait_ge(s_rt, n + 1)
                rsqrt_step(RT, MV, NT)

            def norm(n):
                l, which = divmod(n, 2)
                if n:
                    norm_root(n)

                def scaled(k):
                    for t0, m, cnd in SEGS:
                        ins = V.scalar_tensor_tensor(out=T1[:, k % 2, t0:t0 + m], in0=xT[:, k, t0:t0 + m],
                                                     scalar=GS[:, l, which, k, cnd:cnd + 1], in1=RT[:, t0:t0 + m],
                                                     op0=ALU.mult, op1=ALU.mult)
                    ins.then_inc(s_t1, 1)

                def low(k):
                    dve.wait_ge(s_hhi, (KC * n + k + 1) + (4 if n == 3 else 0))
                    for t0, m, cnd in SEGS:
                        ins = V.scalar_tensor_tensor(out=HL[:, k, t0:t0 + m], in0=T1[:, k % 2, t0:t0 + m],
                                                     scalar=MODT[:, l, 24 * which + k, cnd:cnd + 1],
                                                     in1=HH[:, k, t0:t0 + m].bitcast(F32), op0=ALU.add, op1=ALU.subtract)
                    ins.then_inc(s_hlo, 1)

                hlo0 = KC * n + (4 if n == 3 else 0)
                scaled(0)
                for k in range(KC):
                    if k + 1 < KC:
                        if k >= 1:
                            dve.wait_ge(s_hlo, hlo0 + k)
                        scaled(k + 1)
                    if k == 0:
                        dve.wait_ge(s_t1, KC * n + 1)
                    low(k)

            def lo(stage, pair, k):
                dve.wait_ge(s_hi, UNIT0[stage] + 2 * pair + k + 1)
                if stage in ("a_out", "c_out"):
                    wlo, whi = (w[:, :].rearrange("p (c m) -> p c m", c=KC) for w in (WLO[k], WHI[k]))
                    V.tensor_tensor(wlo, chunk_view(RAW[:, k, :]), whi.bitcast(F32), ALU.subtract).then_inc(s_lo, 1)
                else:
                    V.tensor_tensor(WLO[k][:, :], RAW[:, k, :], WHI[k][:, :].bitcast(F32), ALU.subtract).then_inc(s_lo, 1)

            def los(stage, evacuate=None, fresh=False):
                def turn(i, second=True):
                    if second:
                        lo(stage, i, 1)
                    if evacuate:
                        evacuate(2 * i, 0)
                    lo(stage, i + 1, 0)
                    if evacuate:
                        evacuate(2 * i + 1, 1)

                if fresh:
                    turn(0, second=False)
                if COUNT[stage] // 2 - 1 > fresh:
                    with dve.Fori(int(fresh), COUNT[stage] // 2 - 1) as i:
                        turn(i)
                i = COUNT[stage] // 2 - 1
                lo(stage, i, 1)
                if evacuate:
                    evacuate(2 * i, 0)
                lo(NEXT[stage], 0, 0)
                if evacuate:
                    evacuate(2 * i + 1, 1)

            def add_gated(k, bank, l, gate, sem_):
                xk = xT[:, bass.ds(k, 1), :].rearrange("p a t -> p (a t)")
                for t0, m, cnd in SEGS:
                    g = MODT[:, l, bass.ds(gate + k, 1), cnd:cnd + 1].rearrange("p a b -> p (a b)")
                    ins = V.scalar_tensor_tensor(out=xk[:, t0:t0 + m], in0=PS[:, bank, t0:t0 + m], scalar=g,
                                                 in1=xk[:, t0:t0 + m], op0=ALU.mult, op1=ALU.add)
                ins.then_inc(sem_, 1)

            def to_residual(stage, l):
                dve.wait_ge(s_unit, UNIT0[stage] + KC + 2)
                for k in range(KC):
                    add_gated(k, k, l, 16, s_res)

            norm_root(0)
            lo("q", 0, 0)
            lo("q", 0, 1)
            modulation(0, 0, EARLY)
            norm(0)
            los("q", fresh=True)
            los("kvp")

            mpe.wait(dve, "hm")
            mdve.mark("var", V.tensor_scalar(VAR[:, :, :], PS[:, 2:7, 0:T], EPS, None, ALU.add))
            mact.wait(dve, "root")
            rsqrt_step(ZS[:, :, :], VAR[:, :, :], QN[:, :, :])
            V.scalar_tensor_tensor(out=QN[:, 0:4, :], in0=Z[:, 0:4, :], scalar=VT[:, R_QG:R_QG + 1],
                                   in1=ZS[:, 0:4, :], op0=ALU.mult, op1=ALU.mult)
            mdve.mark("qn", V.scalar_tensor_tensor(out=QN[:, 4, :], in0=Z[:, 4, :], scalar=VT[:, R_KG:R_KG + 1],
                                                   in1=ZS[:, 4, :], op0=ALU.mult, op1=ALU.mult))
            mdve.wait(dve, "qn")
            mpe.wait(dve, "rot")
            dve.wait_ge(s_att, 16 * 6)
            own.mark(V.tensor_tensor(RQ[:, :, :], QN[:, 0:4, NPROMPT:T], COS.unsqueeze(1).to_broadcast([P, 4, NSAMPLE]), ALU.mult))
            own.mark(V.tensor_tensor(KALL[:, 0:NSAMPLE], QN[:, 4, NPROMPT:T], COS, ALU.mult))
            own.mark(V.tensor_tensor(VAR[:, :, 0:NSAMPLE], PS[:, 2:7, 0:NSAMPLE],
                                     SIN.unsqueeze(1).to_broadcast([P, 5, NSAMPLE]), ALU.mult))
            own.wait()
            own.mark(V.tensor_tensor(RQ[:, :, :], RQ[:, :, :], VAR[:, 0:4, 0:NSAMPLE], ALU.add))
            mdve.mark("rope", V.tensor_tensor(KALL[:, 0:NSAMPLE], KALL[:, 0:NSAMPLE], VAR[:, 4, 0:NSAMPLE], ALU.add))
            mdve.wait(dve, "rope")
            def softmax(b):
                n = P if BATCHES[b][0] == 0 else T
                mpe.wait(dve, f"s{b}")
                own.do(V.tensor_reduce(MX, PS[:, 0:4, 0:n], AX.X, ALU.max))
                mdve.mark(f"nb{b}", V.tensor_scalar(NB, MX, -0.125, None, ALU.mult))
                mact.wait(dve, f"e{b}")
                own.do(V.reciprocal(RV, SM))
                mdve.mark(f"p{b}", V.tensor_tensor(PROB[b % 2][:, :, 0:n], PROB[b % 2][:, :, 0:n],
                                                   RV.unsqueeze(2).to_broadcast([P, 4, n]), ALU.mult))

            softmax(0)
            for b, (qt, j) in enumerate(BATCHES):
                if b + 1 < NBT:
                    softmax(b + 1)
                rows = slice(64 * j, 64 * j + 64)
                mact.wait(dve, f"oh{b}")
                mdve.mark(f"ol{b}", V.tensor_tensor(HL[rows, 0:4, qt * P:qt * P + P],
                                                    PS[rows, 4, :].rearrange("p (a b) -> p a b", a=4),
                                                    HH[rows, 0:4, qt * P:qt * P + P].bitcast(F32), ALU.subtract))
            for g in range(4):
                mact.wait(dve, f"ph{g}")
                mdve.mark(f"pl{g}", V.scalar_tensor_tensor(out=HL[:, 4 + g, :], in0=PS[:, g, 0:T],
                                                           scalar=VT[:, R_PS + g:R_PS + g + 1],
                                                           in1=HH[:, 4 + g, :].bitcast(F32), op0=ALU.mult, op1=ALU.subtract))
            modulation(0, EARLY, MODSEGS)
            los("a_out")
            to_residual("a_out", 0)

            for l in range(LAYERS):
                if l:
                    modulation(1, 0, MODSEGS)
                    lo("c_in", 0, 1)
                    norm(2)
                    own.mark(V.memset(UP, 0.0))

                    def evac(i, jj, what, k):
                        u = 6 * i + 3 * jj + what
                        j = 2 * i + jj
                        dve.wait_ge(s_unit, UNIT0["c_in"] + u + 3)
                        own.wait()
                        if what == 0:
                            own.mark(V.tensor_copy(GC, PS[:, k, 0:T]))
                            own.wait()
                            V.sem_inc(s_ev, 1)
                        elif what == 1:
                            own.mark(V.tensor_tensor(UP[:, 1:1 + NPROMPT], PS[:, k, 0:NPROMPT], GC[:, 0:NPROMPT], ALU.mult))
                            V.tensor_tensor(UP[:, 2 + NPROMPT:2 + T], PS[:, k, NPROMPT:T], GC[:, NPROMPT:T], ALU.mult).then_inc(s_ev, 1)
                            own.wait()
                            dve.wait_ge(s_ev, 2 + PROJ0["c_in"] + u + 1)
                            tap = [VT[:, bass.ds(R_CW + 8 * w + j, 1)] for w in range(3)]
                            own.do(V.tensor_scalar(YA[:, 0:T + 1], UP[:, 0:T + 1], tap[0], None, ALU.mult))
                            for w in (1, 2):
                                own.do(V.scalar_tensor_tensor(out=YA[:, 0:T + 1], in0=UP[:, w:w + T + 1], scalar=tap[w],
                                                              in1=YA[:, 0:T + 1], op0=ALU.mult, op1=ALU.add))
                        else:
                            cm = CM[:, bass.ds(j, 1), :].rearrange("p a t -> p (a t)")
                            own.mark(V.tensor_tensor(cm[:, 0:NPROMPT], PS[:, k, 0:NPROMPT], YA[:, 0:NPROMPT], ALU.mult))
                            V.tensor_tensor(cm[:, NPROMPT:T], PS[:, k, NPROMPT:T], YA[:, NPROMPT + 1:T + 1], ALU.mult).then_inc(s_ev, 1)

                    def conv_pair(i, first=False, last=False):
                        for q in range(6):
                            if first and q == 0:
                                pass
                            elif q < 5:
                                k = (q + 1) % 2
                                lo("c_in", 3 * i + (q + 1) // 2, k)
                            elif not last:
                                lo("c_in", 3 * i + 3, 0)
                            else:
                                lo("c_out", 0, 0)
                            evac(i, q // 3, q % 3, q % 2)

                    conv_pair(0, first=True)
                    with own.loop(2, 12) as i:
                        conv_pair(i + 1)
                    conv_pair(3, last=True)
                    dve.wait_ge(s_ev, 2 + PROJ0["c_in"] + 24)
                    own.wait()
                    V.sem_inc(s_cm, KC)
                    for k in range(0, KC, 2):
                        dve.wait_ge(s_hhi, 3 * KC + k // 2 + 1)
                        V.tensor_tensor(HL[:, k:k + 2, :], CM[:, k:k + 2, :], HH[:, k:k + 2, :].bitcast(F32), ALU.subtract)\
                            .then_inc(s_hlo, 1)
                    los("c_out")
                    to_residual("c_out", 1)
                lo(f"wq{l}", 0, 1)
                norm(2 * l + 1)
                los(f"wq{l}", fresh=True)

                def turn_u(i, k):
                    dve.wait_ge(u_in[k], 64 * (P // 2 * l + i + 1))
                    dve.wait_ge(s_ulo, P * l + 2 * i + k + 1)
                    V.transpose(UT[:, k, :].rearrange("p (c b e) -> p c b e", c=KC, b=4),
                                URAW[:, k, :, :].rearrange("p b (j c) -> p c b j", c=KC)).then_inc(s_tr, 1)

                def s_step(i, k):
                    turn_u(i + 1, k)

                turned = [1]

                def next_u():
                    turned[0] += 1
                    turn_u(*divmod(turned[0], 2))

                def top16(vals, idx, src, rest, rows, beside):
                    def turn(step, u):
                        if (step, u) in beside:
                            next_u()

                    for u in range(rows):
                        turn(0, u)
                        ins = V.max(vals[:, u, 0:8], src[:, u, :])
                    own.do(ins)
                    for u in range(rows):
                        turn(1, u)
                        V.max_index(idx[:, u, 0:8], vals[:, u, 0:8], src[:, u, :])
                        ins = V.match_replace(rest[:, u, :], vals[:, u, 0:8], src[:, u, :], NEG)
                    own.do(ins)
                    for u in range(rows):
                        turn(2, u)
                        ins = V.max(vals[:, u, 8:16], rest[:, u, :])
                    own.do(ins)
                    for u in range(rows):
                        turn(3, u)
                        ins = V.max_index(idx[:, u, 8:16], vals[:, u, 8:16], rest[:, u, :])
                    return ins

                def pick_tail(tile):
                    cols = slice(tile * P, tile * P + P)
                    dve.wait_ge(s_pte, TT * l + tile + 1)
                    bank = PS[:, 7, 2 * P:3 * P]
                    own.do(V.tensor_copy(GP[:, 0, cols], bank))
                    own.do(V.tensor_tensor(GRES, bank, GP[:, 0, cols], ALU.subtract))
                    own.do(V.tensor_copy(GP[:, 1, cols], GRES))
                    V.tensor_tensor(GP[:, 2, cols], GRES, GP[:, 1, cols], ALU.subtract).then_inc(s_pts, 1)
                    dve.wait_ge(s_pts, TT * l + tile + 1)

                turn_u(0, 0)
                turn_u(0, 1)
                for tile in range(TT):
                    g = TT * l + tile
                    dve.wait_ge(s_scc, g + 1)
                    top16(V16, I16U, SC, SC2, 16, ((0, 8), (1, 0), (1, 6), (1, 12), (2, 4), (3, 0))).then_inc(s_l1, 1)
                    dve.wait_ge(s_l1, g + 1)
                    own.mark(V.tensor_copy(I16F[:, :, :], I16U[:, :, :]))
                    side = V16.rearrange("p (h s) k -> p h s k", s=2)
                    for a in range(TOPK):
                        if a == 8:
                            next_u()
                        ins = V.tensor_tensor(CA[:, :, a * TOPK:(a + 1) * TOPK],
                                              side[:, :, 1, :], side[:, :, 0, a:a + 1].to_broadcast([P, HEADS, TOPK]), ALU.add)
                    own.do(ins)
                    if tile:
                        pick_tail(tile - 1)
                    own.do(top16(V2, FIU, CA, CA2, HEADS, ((0, 0), (1, 0), (1, 3), (1, 6), (2, 2), (3, 2))))
                    fi = FIU[:, :, :].rearrange("p a b -> p (a b)")
                    own.mark(V.tensor_scalar(FAU[:, :], fi, 4, None, ALU.logical_shift_right))
                    own.mark(V.tensor_scalar(FBU[:, :], fi, TOPK - 1, None, ALU.bitwise_and))
                    V.tensor_tensor(EX[:, :, :], V2[:, :, :], V2[:, :, 0:1].to_broadcast([P, HEADS, TOPK]), ALU.subtract)\
                        .then_inc(s_d, 1)
                    own.wait()
                    own.mark(V.tensor_copy(FA, FAU[:, :]))
                    own.do(V.tensor_copy(FB, FBU[:, :]))
                    iota16 = IOTA[:, 0:TOPK].unsqueeze(1).to_broadcast([P, PICKS, TOPK])
                    own.mark(V.tensor_tensor(EQ[:, :, :], FA.unsqueeze(2).to_broadcast([P, PICKS, TOPK]), iota16, ALU.is_equal))
                    next_u()
                    own.do(V.tensor_tensor(EQ2[:, :, :], FB.unsqueeze(2).to_broadcast([P, PICKS, TOPK]), iota16, ALU.is_equal))
                    keys = I16F.rearrange("p (h s) k -> p h s k", s=2)
                    for eq, s in ((EQ, 0), (EQ2, 1)):
                        next_u()
                        for h in range(HEADS):
                            e = eq[:, h * TOPK:(h + 1) * TOPK, :]
                            ins = V.tensor_tensor(e, e, keys[:, h, s:s + 1, :].to_broadcast([P, TOPK, TOPK]), ALU.mult)
                    own.do(ins)
                    next_u()
                    own.mark(V.tensor_reduce(ID1, EQ[:, :, :], AX.X, ALU.add))
                    next_u()
                    own.mark(V.tensor_reduce(ID2, EQ2[:, :, :], AX.X, ALU.add))
                    dve.wait_ge(s_e, g + 1)
                    own.do(V.tensor_reduce(ZSUM, EX[:, :, :], AX.X, ALU.add))
                    own.do(V.reciprocal(ZINV, ZSUM))
                    V.tensor_tensor(GT[:, :, :], EX[:, :, :], ZINV.unsqueeze(2).to_broadcast([P, HEADS, TOPK]), ALU.mult)\
                        .then_inc(s_pick, 1)
                    assert turned[0] == 1 + (tile + 1) * (S_LEVEL1 + S_LEVEL2)
                pick_tail(2)

                def one_hots(tile, turn, k, at):
                    dve.wait_ge(s_gm, 2 * (2 * TURNS * (TT * l + tile) + 2 * turn + k) + 2)
                    tok = bass.ds(tile * P + 16 * turn + BATCH * k, BATCH)

                    def spread(x):
                        return x.unsqueeze(1).to_broadcast([P, P, BATCH])

                    own.do(V.tensor_tensor(EQ1[:, :, :], IOTA8[:, :, :], spread(IT1[:, tok]), ALU.is_equal))
                    V.tensor_tensor(OH2[k], IOTA8[:, :, :], spread(IT2[:, tok]), ALU.is_equal)
                    s_step(at, k)
                    for part in range(3):
                        ins = V.tensor_tensor(OH1[k][part], EQ1[:, :, :], spread(GP[:, part, tok]), ALU.mult)
                    ins.then_inc(s_oh, 1)
                    dve.wait_ge(s_oh, 2 * TURNS * (TT * l + tile) + 2 * turn + k + 1)

                at = TT * (S_LEVEL1 + S_LEVEL2)
                for tile in range(TT):
                    with own.loop(TURNS, 2) as i:
                        one_hots(tile, i, 0, at // 2 + i)
                        one_hots(tile, i, 1, at // 2 + i)
                    at += 2 * TURNS
                    if tile + 1 < TT:
                        s_tiles(dve, at, S_STORE, s_step)
                        at += S_STORE
                s_tiles(dve, at, S_REST - 2, s_step)

                def weigh(i, k):
                    dve.wait_ge(g_in[k], 32 * (P // 2 * l + i + 1))
                    V.tensor_tensor(GEL[:, k, :], GEL[:, k, :], GIN[:, k, :], ALU.mult).then_inc(s_w, 1)

                def w_lo(i, k):
                    g = P * l + 2 * i + k
                    dve.wait_ge(s_whi, g + 1)
                    V.tensor_tensor(ELO[k][:, :], GEL[:, k, :], EHI[k][:, :].bitcast(F32), ALU.subtract).then_inc(s_wlo, 1)

                v = f"v{l}"
                weigh(0, 0)
                w_lo(0, 0)
                weigh(0, 1)
                with dve.Fori(0, P // 2 - 1) as i:
                    w_lo(i, 1)
                    lo(v, i, 1)
                    weigh(i + 1, 0)
                    w_lo(i + 1, 0)
                    lo(v, i + 1, 0)
                    weigh(i + 1, 1)
                w_lo(P // 2 - 1, 1)
                lo(v, P // 2 - 1, 1)
                if l == 0:
                    lo("c_in", 0, 0)
                for k in range(KC):
                    dve.wait_ge(s_at, KC * l + k + 1)
                    add_gated(k, k % 2, l, 40, s_res)
            norm_root(4)
            for k in range(KC):
                V.scalar_tensor_tensor(out=YT[:, k, :], in0=xT[:, k, :], scalar=VT[:, R_FIN + k:R_FIN + k + 1],
                                       in1=RT, op0=ALU.mult, op1=ALU.mult).then_inc(s_yt, 1)


_INS = ["x_prompt", "x_sample", "cache_k", "cache_v", "c", "c_ctx", "mod_w", "mod_b", "norm1_g", "norm2_g",
        "a_in_w", "a_out_w", "q_norm_g", "k_norm_g", "pool_w", "pool_scale", "c_in_w", "c_conv_w", "c_out_w",
        "peer_wq", "peer_subkeys", "peer_u", "peer_v", "final_g"]
_OUTS = [(1, 128, 1024), (1, 256, 1024), (1, 1, 128, 2, 64), (1, 1, 128, 2, 64)]


def _tables():
    import numpy as np

    f = np.float32
    ident = np.eye(128, dtype=f)
    headmean = np.kron(np.eye(2), np.ones((64, 64)) / 64).astype(f)
    rot = np.zeros((128, 128), f)
    for m in range(128):
        if m % 32 < 16:
            rot[m + 16, m] = -1
        else:
            rot[m - 16, m] = 1
    inv = f(10000.0) ** (-np.arange(16, dtype=f) / f(16))
    tok = np.arange(256)
    d = np.arange(128) % 64
    pos = np.where((d < 32)[:, None], (tok // 64)[None, :], (tok % 64)[None, :]).astype(f)
    ang = pos * inv[d % 16][:, None]
    rcnt = np.zeros((4, 384), f)
    for g, win in enumerate((2, 4, 8, 16)):
        for t0, n in ((0, 128), (128, 256)):
            t = np.arange(n)
            cnt = np.clip(t + win - win // 2, 0, n) - np.clip(t - win // 2, 0, n)
            rcnt[g, t0:t0 + n] = 1.0 / cnt
    rcnt = np.ascontiguousarray(np.broadcast_to(rcnt, (128, 4, 384)))
    iota = np.ascontiguousarray(np.broadcast_to(np.arange(128, dtype=f), (128, 128)))
    return {"k_ident": ident, "k_headmean": headmean, "k_rot": rot, "k_cos": np.cos(ang).astype(f),
            "k_sin": np.sin(ang).astype(f), "k_rcnt": rcnt, "k_iota": iota}


def kernel(**inputs):
    import numpy as _np
    import concourse.bacc as _bacc
    from concourse import mybir as _mybir
    from concourse.bass_utils import run_bass_kernel_spmd as _run

    nc = _bacc.Bacc("TRN2", target_bir_lowering=False, num_devices=1)
    arrays, args = {}, {}
    for name, a in [(n, inputs[n]) for n in _INS] + list(_tables().items()):
        a = _np.ascontiguousarray(a)
        arrays[f"in_{name}_dram"] = a
        args[name] = nc.dram_tensor(f"in_{name}_dram", a.shape, _mybir.dt.from_np(a.dtype), kind="ExternalInput").ap()
    for i, (name, shape) in enumerate(zip(("y_prompt", "y_sample", "new_k", "new_v"), _OUTS)):
        args[name] = nc.dram_tensor(f"out_{i}_dram", shape, F32, kind="ExternalOutput").ap()
    build_step(nc, **args)
    r = _run(nc, [arrays], core_ids=[0])
    return tuple(r.results[0][f"out_{i}_dram"] for i in range(len(_OUTS)))
```
